# Optimizing a Trainium2 kernel written in Bass

```python
import math
import jax, jax.numpy as jnp
from jax import lax
import numpy as np

D_MODEL = 1024
BATCH = 1
SEQ = 256
DEPTH = 2

N_A_LAYERS = DEPTH // 2
N_B_LAYERS = DEPTH - N_A_LAYERS
N_DENSE_LAYERS = (DEPTH + 1) // 2
N_MOE_LAYERS = DEPTH // 2
SB_HEADS = 16
SB_HEAD_DIM = D_MODEL // SB_HEADS
MLA_HEADS = 16
Q_LORA_RANK = 384
KV_LORA_RANK = 256
QK_NOPE_DIM = 64
QK_ROPE_DIM = 32
V_HEAD_DIM = 64
ROPE_THETA = 10000.0
D_FF_DENSE = 2816
N_EXPERTS = 8
TOP_K = 2
D_FF_EXPERT = 3584
Q_BLOCK = 128
EXPERT_BLOCK = 128
EPS = 1e-6

kernel_name = "yoco_stickbreak_mla_moe_trunk"

def rmsnorm(x, g):
    xf = x.astype(jnp.float32)
    y = xf * lax.rsqrt(jnp.mean(xf * xf, axis=-1, keepdims=True) + EPS)
    return (y * g.astype(jnp.float32)).astype(x.dtype)

def rope_tables(seq_len):
    pos = jnp.arange(seq_len, dtype=jnp.float32)
    inv_freq = ROPE_THETA ** (-jnp.arange(0, QK_ROPE_DIM, 2, dtype=jnp.float32) / QK_ROPE_DIM)
    ang = pos[:, None] * inv_freq[None, :]
    ang = jnp.concatenate([ang, ang], axis=-1)
    return jnp.cos(ang), jnp.sin(ang)

def apply_rope(x, cos, sin):
    half = x.shape[-1] // 2
    x1, x2 = x[..., :half], x[..., half:]
    rot = jnp.concatenate([-x2, x1], axis=-1)
    return x * cos.astype(x.dtype) + rot * sin.astype(x.dtype)

def to_query_blocks(t):
    b, s, h, d = t.shape
    return t.reshape(b, s // Q_BLOCK, Q_BLOCK, h, d).transpose(1, 0, 3, 2, 4)

def from_query_blocks(o):
    nb, b, h, qb, d = o.shape
    return o.transpose(1, 0, 3, 2, 4).reshape(b, nb * qb, h * d)

def stick_breaking_attention(xn, w_qkv, w_o):
    b, s, _ = xn.shape
    qkv = (xn @ w_qkv).reshape(b, s, 3, SB_HEADS, SB_HEAD_DIM)
    q, k, v = qkv[:, :, 0], qkv[:, :, 1], qkv[:, :, 2]
    k = k.transpose(0, 2, 1, 3)
    v = v.transpose(0, 2, 1, 3)
    scale = 1.0 / math.sqrt(SB_HEAD_DIM)
    kpos = jnp.arange(s)

    def one_block(args):
        qb, blk = args
        z = jnp.einsum('bhqd,bhkd->bhqk', qb, k, preferred_element_type=jnp.float32) * scale
        qpos = blk * Q_BLOCK + jnp.arange(Q_BLOCK)
        mask = kpos[None, :] < qpos[:, None]
        log_1m_beta = jnp.where(mask, jax.nn.log_sigmoid(-z), 0.0)
        later = lax.cumsum(log_1m_beta, axis=3, reverse=True) - log_1m_beta
        att = jnp.where(mask, jnp.exp(jax.nn.log_sigmoid(z) + later), 0.0)
        return jnp.einsum('bhqk,bhkd->bhqd', att.astype(v.dtype), v)

    o = lax.map(one_block, (to_query_blocks(q), jnp.arange(s // Q_BLOCK)))
    return from_query_blocks(o) @ w_o

def mla_shared_kv(h, g_src, w_kv_a, g_kv_a, w_kv_b, g_k_nope, g_k_pe, cos, sin):
    b, s, _ = h.shape
    hn = rmsnorm(h, g_src)
    kv_a = hn @ w_kv_a
    c_kv = rmsnorm(kv_a[..., :KV_LORA_RANK], g_kv_a)
    k_pe = apply_rope(rmsnorm(kv_a[..., KV_LORA_RANK:], g_k_pe), cos, sin)
    kv = (c_kv @ w_kv_b).reshape(b, s, MLA_HEADS, QK_NOPE_DIM + V_HEAD_DIM)
    k_nope = rmsnorm(kv[..., :QK_NOPE_DIM], g_k_nope).transpose(0, 2, 1, 3)
    v = kv[..., QK_NOPE_DIM:].transpose(0, 2, 1, 3)
    return k_nope, k_pe, v

def mla_attention(xn, w_q_a, g_q_a, w_q_b, g_q_nope, g_q_pe, w_o, k_nope, k_pe, v, cos, sin):
    b, s, _ = xn.shape
    q = (rmsnorm(xn @ w_q_a, g_q_a) @ w_q_b).reshape(b, s, MLA_HEADS, QK_NOPE_DIM + QK_ROPE_DIM)
    q_nope = rmsnorm(q[..., :QK_NOPE_DIM], g_q_nope)
    q_pe = apply_rope(rmsnorm(q[..., QK_NOPE_DIM:], g_q_pe), cos[:, None, :], sin[:, None, :])
    scale = 1.0 / math.sqrt(QK_NOPE_DIM + QK_ROPE_DIM)
    kpos = jnp.arange(s)

    def one_block(args):
        qn, qp, blk = args
        sc = (jnp.einsum('bhqd,bhkd->bhqk', qn, k_nope, preferred_element_type=jnp.float32)
              + jnp.einsum('bhqr,bkr->bhqk', qp, k_pe, preferred_element_type=jnp.float32)) * scale
        qpos = blk * Q_BLOCK + jnp.arange(Q_BLOCK)
        mask = kpos[None, :] <= qpos[:, None]
        p = jax.nn.softmax(jnp.where(mask, sc, -jnp.inf), axis=-1)
        return jnp.einsum('bhqk,bhkd->bhqd', p.astype(v.dtype), v)

    o = lax.map(one_block, (to_query_blocks(q_nope), to_query_blocks(q_pe), jnp.arange(s // Q_BLOCK)))
    return from_query_blocks(o) @ w_o

def swiglu(x, w_gate, w_up, w_down):
    return (jax.nn.silu(x @ w_gate) * (x @ w_up)) @ w_down

def moe_swiglu(x2d, w_router, b_router, w_gate, w_up, w_down):
    t, d = x2d.shape
    logits = (x2d @ w_router).astype(jnp.float32) + b_router.astype(jnp.float32)
    top_vals, top_idx = lax.top_k(logits, TOP_K)
    gates = jax.nn.softmax(top_vals, axis=-1).astype(x2d.dtype)
    n_assign = t * TOP_K
    flat_e = top_idx.reshape(-1)
    flat_tok = jnp.repeat(jnp.arange(t), TOP_K)
    flat_g = gates.reshape(-1)
    order = jnp.argsort(flat_e)
    sorted_e, sorted_tok, sorted_g = flat_e[order], flat_tok[order], flat_g[order]
    counts = jnp.zeros((N_EXPERTS,), jnp.int32).at[flat_e].add(1)
    starts = jnp.cumsum(counts) - counts
    padded = ((counts + EXPERT_BLOCK - 1) // EXPERT_BLOCK) * EXPERT_BLOCK
    pends = jnp.cumsum(padded)
    pstarts = pends - padded
    dest = pstarts[sorted_e] + (jnp.arange(n_assign) - starts[sorted_e])
    n_rows = n_assign + N_EXPERTS * EXPERT_BLOCK
    n_rows = ((n_rows + EXPERT_BLOCK - 1) // EXPERT_BLOCK) * EXPERT_BLOCK
    n_blocks = n_rows // EXPERT_BLOCK
    buf = jnp.zeros((n_rows, d), x2d.dtype).at[dest].set(x2d[sorted_tok])
    block_e = jnp.clip(jnp.searchsorted(pends, jnp.arange(n_blocks) * EXPERT_BLOCK, side='right'),
                       0, N_EXPERTS - 1)

    def expert_block(args):
        xb, e = args
        return (jax.nn.silu(xb @ w_gate[e]) * (xb @ w_up[e])) @ w_down[e]

    out = lax.map(expert_block, (buf.reshape(n_blocks, EXPERT_BLOCK, d), block_e)).reshape(n_rows, d)
    rows = out[dest] * sorted_g[:, None]
    return jax.ops.segment_sum(rows, sorted_tok, num_segments=t)

def setup_inputs(seed: int = 0) -> dict:
    key = jax.random.key(seed)
    ks = iter(jax.random.split(key, 32))

    def w(shape, fan_in):
        return jax.random.normal(next(ks), shape, jnp.float32) * (fan_in ** -0.5)

    def g(shape):
        return 1.0 + 0.02 * jax.random.normal(next(ks), shape, jnp.float32)

    sb_w = SB_HEADS * SB_HEAD_DIM
    return {
        "x": jax.random.normal(next(ks), (BATCH, SEQ, D_MODEL), jnp.float32),
        "g_mix": g((DEPTH, D_MODEL)),
        "g_ffn": g((DEPTH, D_MODEL)),
        "sb_w_qkv": w((N_A_LAYERS, D_MODEL, 3 * sb_w), D_MODEL),
        "sb_w_o": w((N_A_LAYERS, sb_w, D_MODEL), sb_w),
        "kv_g_src": g((D_MODEL,)),
        "kv_w_a": w((D_MODEL, KV_LORA_RANK + QK_ROPE_DIM), D_MODEL),
        "kv_g_a": g((KV_LORA_RANK,)),
        "kv_w_b": w((KV_LORA_RANK, MLA_HEADS * (QK_NOPE_DIM + V_HEAD_DIM)), KV_LORA_RANK),
        "kv_g_k_nope": g((QK_NOPE_DIM,)),
        "kv_g_k_pe": g((QK_ROPE_DIM,)),
        "mla_w_q_a": w((N_B_LAYERS, D_MODEL, Q_LORA_RANK), D_MODEL),
        "mla_g_q_a": g((N_B_LAYERS, Q_LORA_RANK)),
        "mla_w_q_b": w((N_B_LAYERS, Q_LORA_RANK, MLA_HEADS * (QK_NOPE_DIM + QK_ROPE_DIM)), Q_LORA_RANK),
        "mla_g_q_nope": g((N_B_LAYERS, QK_NOPE_DIM)),
        "mla_g_q_pe": g((N_B_LAYERS, QK_ROPE_DIM)),
        "mla_w_o": w((N_B_LAYERS, MLA_HEADS * V_HEAD_DIM, D_MODEL), MLA_HEADS * V_HEAD_DIM),
        "ffn_w_gate": w((N_DENSE_LAYERS, D_MODEL, D_FF_DENSE), D_MODEL),
        "ffn_w_up": w((N_DENSE_LAYERS, D_MODEL, D_FF_DENSE), D_MODEL),
        "ffn_w_down": w((N_DENSE_LAYERS, D_FF_DENSE, D_MODEL), D_FF_DENSE),
        "moe_w_router": w((N_MOE_LAYERS, D_MODEL, N_EXPERTS), D_MODEL),
        "moe_b_router": 0.01 * jax.random.normal(next(ks), (N_MOE_LAYERS, N_EXPERTS), jnp.float32),
        "moe_w_gate": w((N_MOE_LAYERS, N_EXPERTS, D_MODEL, D_FF_EXPERT), D_MODEL),
        "moe_w_up": w((N_MOE_LAYERS, N_EXPERTS, D_MODEL, D_FF_EXPERT), D_MODEL),
        "moe_w_down": w((N_MOE_LAYERS, N_EXPERTS, D_FF_EXPERT, D_MODEL), D_FF_EXPERT),
    }

def reference(x, g_mix, g_ffn, sb_w_qkv, sb_w_o,
              kv_g_src, kv_w_a, kv_g_a, kv_w_b, kv_g_k_nope, kv_g_k_pe,
              mla_w_q_a, mla_g_q_a, mla_w_q_b, mla_g_q_nope, mla_g_q_pe, mla_w_o,
              ffn_w_gate, ffn_w_up, ffn_w_down,
              moe_w_router, moe_b_router, moe_w_gate, moe_w_up, moe_w_down):
    b, s, d = x.shape
    cos, sin = rope_tables(s)
    k_nope = k_pe = v = None
    for i in range(DEPTH):
        if i < N_A_LAYERS:
            x = x + stick_breaking_attention(rmsnorm(x, g_mix[i]), sb_w_qkv[i], sb_w_o[i])
        else:
            if i == N_A_LAYERS:
                k_nope, k_pe, v = mla_shared_kv(x, kv_g_src, kv_w_a, kv_g_a, kv_w_b,
                                                kv_g_k_nope, kv_g_k_pe, cos, sin)
            j = i - N_A_LAYERS
            x = x + mla_attention(rmsnorm(x, g_mix[i]), mla_w_q_a[j], mla_g_q_a[j], mla_w_q_b[j],
                                  mla_g_q_nope[j], mla_g_q_pe[j], mla_w_o[j],
                                  k_nope, k_pe, v, cos, sin)
        hn = rmsnorm(x, g_ffn[i])
        if i % 2 == 0:
            x = x + swiglu(hn, ffn_w_gate[i // 2], ffn_w_up[i // 2], ffn_w_down[i // 2])
        else:
            m = i // 2
            x = x + moe_swiglu(hn.reshape(b * s, d), moe_w_router[m], moe_b_router[m],
                               moe_w_gate[m], moe_w_up[m], moe_w_down[m]).reshape(b, s, d)
    return x


_drawn_inputs = setup_inputs


def setup_inputs(seed=0):
    import zlib

    import numpy as np

    out = dict(_drawn_inputs(seed))
    spreads = {}
    factors = {'kv_g_src': 8.0,
     'kv_g_a': 6.13,
     'kv_g_k_nope': 8.0,
     'kv_g_k_pe': 8.0,
     'mla_g_q_a': 6.618,
     'mla_g_q_nope': 8.0,
     'mla_g_q_pe': 8.0,
     'moe_b_router': 101.207}
    for name, (base, spread) in spreads.items():
        noise = np.random.default_rng([zlib.crc32(name.encode()), seed]).standard_normal(out[name].shape)
        drawn = base * np.exp(spread * noise) if base else spread * noise
        out[name] = __import__('jax').numpy.asarray(drawn.astype(out[name].dtype))
    for name, factor in factors.items():
        out[name] = (out[name] * factor).astype(out[name].dtype)
    return out
```

```python
from contextlib import ExitStack

import concourse.bass as bass
from concourse import mybir

ALL = slice(None)
F32 = mybir.dt.float32
F32R = mybir.dt.float32r
I32 = mybir.dt.int32
U32 = mybir.dt.uint32
ALU = mybir.AluOpType
ACT = mybir.ActivationFunctionType
AXX = mybir.AxisListType.X

P = 128
D = 1024
S = 256
T = S // P
KD = D // P
HEADS = 16
HD = 64
ROPE = 32
QK = HD + ROPE
RQ = 384
RKV = 256
FD = 2816
FT = FD // P
FE = 3584
NE = 8
CH = 512
NC = FE // CH
EPS = 1e-6
FAR = 4096.0
OVER = S * 2 // (P + 1)
ITEMS = NE + OVER
FILLS = 7
NEG = -1e30

UNIT = 2048
RAW, HI, LO = 7, 3, 3

G_MIX0, G_FFN0, G_KV, G_MIX1, G_FFN1, G_KVA, G_QA, G_KN, G_QN = 0, 8, 16, 24, 32, 40, 42, 45, 46
NG = 47


def shape_unit(tile, n, *dims):
    names = "abcd"[:len(dims)]
    return tile[:, 0:n].rearrange(f"p ({' '.join(names)}) -> p {' '.join(names)}", **dict(zip(names, dims)))


def plan(w):
    out = []

    def rows(src, r0, n, c0, c1):
        return src[r0 * P:(r0 + n) * P, c0:c1].rearrange("(k p) n -> p k n", p=P)

    for c in range(6):
        for q in range(2):
            out.append(("qkv", (4, CH), rows(w["qkv"], 4 * q, 4, c * CH, c * CH + CH)))
    for q in range(4):
        out.append(("sbo", (2, D), rows(w["sbo"], 2 * q, 2, 0, D)))
    for c in range(5):
        for m in ("gate", "up"):
            for q in range(2):
                out.append((m, (4, CH), rows(w[m], 4 * q, 4, c * CH, c * CH + CH)))
    for q in range(2):
        out.append(("tail", (4, 2, 256), [rows(w[m], 4 * q, 4, 5 * CH, FD) for m in ("gate", "up")]))
    for q in range(FT // 2):
        out.append(("down", (2, D), rows(w["down"], 2 * q, 2, 0, D)))
    for q in range(2):
        out.append(("kva", (4, RKV + ROPE), rows(w["kva"], 4 * q, 4, 0, RKV + ROPE)))
    for q in range(2):
        out.append(("kvb", (2, D), rows(w["kvb"], 0, 2, q * D, q * D + D)))
    for q in range(2):
        out.append(("qa", (4, RQ), rows(w["qa"], 4 * q, 4, 0, RQ)))
    for q in range(3):
        out.append(("qb", (3, CH), rows(w["qb"], 0, 3, q * CH, q * CH + CH)))
    for q in range(4):
        out.append(("mlo", (2, D), rows(w["mlo"], 2 * q, 2, 0, D)))
    return out


def expert_plan():
    out = []
    for c in range(NC):
        out += [("gate", c, 0), ("gate", c, 1), ("up", c, 0), ("up", c, 1)]
        if c:
            out += [("down", c - 1, 0), ("down", c - 1, 1)]
    return out + [("down", NC - 1, 0), ("down", NC - 1, 1)]


def build(nc, x_d, gains_d, gpe_d, rope_d, gffn1_d, wr_d, br_d, w, eg, eu, ed, out_d):
    pre = plan(w)
    NPRE = len(pre)
    first = {}
    for u, (name, _, _) in enumerate(pre):
        first.setdefault(name, u)
    item_units = expert_plan()
    NI = len(item_units)
    assert NI % RAW == 0 and NI % HI == 0 and NI % LO == 0

    with ExitStack() as ctx:
        base = (nc.sbuf_base + 63) // 64 * 64
        end = nc.sbuf_usable_end
        at = [base]

        def put(name, shape, dt=F32, off=None):
            n = 4
            for s in shape[1:]:
                n *= s
            n = (n + 31) // 32 * 32
            o = at[0] if off is None else off
            if off is None:
                at[0] += n
            assert o + n <= end, (name, o + n - end)
            return nc.alloc_sbuf_tensor_at(name, shape, dt, offset=o)

        def sem(name):
            return ctx.enter_context(nc.semaphore(name))

        raw = [put(f"raw{i}", [P, UNIT]) for i in range(RAW)]
        hi = [put(f"hi{i}", [P, UNIT], F32R) for i in range(HI)]
        lo = [put(f"lo{i}", [P, UNIT], F32R) for i in range(LO)]
        x = put("x", [P, T, D])
        xs = put("xs", [P, T, D])
        xTh = put("xTh", [P, KD, S], F32R)
        xTl = put("xTl", [P, KD, S], F32R)
        ident = put("ident", [P, P])
        ones = put("ones", [P, P])
        before = put("before", [P, P])
        ntri = put("ntri", [P, P])
        nones = put("nones", [P, P])
        gains = put("gains", [P, NG])
        gpe = put("gpe", [P, 2, ROPE])
        rope = put("rope", [P, T, 2, ROPE])
        wr = put("wr", [P, KD, NE])
        wrh = put("wrh", [P, KD, NE], F32R)
        wrl = put("wrl", [P, KD, NE], F32R)
        br = put("br", [P, NE])
        iota8 = put("iota8", [P, NE])
        eps = put("eps", [P, 1])
        one = put("one", [P, 1])
        ss = put("ss", [P, 4])
        rt = put("rt", [P, 4])
        rs = put("rs", [P, 4])
        arena = (at[0] + 63) // 64 * 64

        def lay(*items):
            o, got = arena, []
            for name, shape, dt in items:
                got.append(put(name, shape, dt, off=o))
                n = 4
                for s in shape[1:]:
                    n *= s
                o += (n + 31) // 32 * 32
            return got

        qT, kT, v1, ab, ln_, spb, att = lay(
            ("qT", [P, KD, S], F32), ("kT", [P, KD, S], F32), ("v1", [P, T, D], F32),
            ("ab", [P, 4, 384], F32), ("ln", [P, 4, 384], F32), ("spb", [P, 4, 384], F32), ("att", [P, 4, 384], F32))
        fTh, fTl, sg, hm = lay(("fTh", [P, FT, S], F32R), ("fTl", [P, FT, S], F32R),
                               ("sg", [P, 4, S], F32), ("hm", [P, 4, S], F32))
        kf, q2, v2, kT2, qT2 = lay(
            ("kf", [P, T, HEADS, QK], F32), ("q2", [P, T, HEADS, QK], F32), ("v2", [P, T, HEADS, HD], F32),
            ("kT2", [P, HEADS, S], F32), ("qT2", [P, HEADS, S], F32))
        o = arena + 4 * (2 * T * HEADS * QK + T * HEADS * HD + HEADS * S)
        kva, qa = put("kva", [P, T, RKV + ROPE], off=o), put("qa", [P, T, RQ], off=o + 2304)
        cTh, cTl = put("cTh", [P, 2, S], F32R, off=o + 5376), put("cTl", [P, 2, S], F32R, off=o + 7424)
        aTh, aTl = put("aTh", [P, 3, S], F32R, off=o + 9472), put("aTl", [P, 3, S], F32R, off=o + 12544)
        o = arena + 4 * (2 * T * HEADS * QK + T * HEADS * HD)
        ra, rb = put("ra", [P, HEADS, ROPE], off=o), put("rb", [P, HEADS, ROPE], off=o + 2048)
        s16, r16, i16 = (put(n, [P, 4, HEADS], off=o + 4096 + 256 * k) for k, n in enumerate(("s16", "r16", "i16")))
        mask, pm, pt, mx, nm, sm, rc = lay(
            ("mask", [P, 384], F32), ("pm", [P, 4, 384], F32), ("pt", [P, 4, 384], F32),
            ("mx", [P, HEADS, 2], F32), ("nm", [P, HEADS, 2], F32), ("sm", [P, HEADS, 2], F32), ("rc", [P, HEADS, 2], F32))
        (gbc, iota, onehot, ST, xgh, xgl, sl, hb, hTh, hTl, ysb, lg, mv, mi, ix, is1, is2, msk, gte, pex, ged,
         posm, cnt, rank, sel, slot, gt, ef, junk, tab) = lay(
            ("gbc", [P, D], F32), ("iota", [P, P], F32), ("onehot", [P, T, P], F32), ("ST", [P, S], F32),
            ("xgh", [P, KD, P], F32R), ("xgl", [P, KD, P], F32R), ("sl", [P, 2, CH], F32), ("hb", [P, 2, CH], F32),
            ("hTh", [P, 2, CH], F32R), ("hTl", [P, 2, CH], F32R), ("ysb", [P, D], F32),
            ("lg", [P, T, NE], F32), ("mv", [P, T, 8], F32), ("mi", [P, T, 8], U32), ("ix", [P, T, 8], F32),
            ("is1", [P, T, NE], F32), ("is2", [P, T, NE], F32), ("msk", [P, T, NE], F32), ("gte", [P, T, NE], F32),
            ("pex", [P, T], F32), ("ged", [P, T, 4], F32), ("posm", [P, T, NE], F32), ("cnt", [P, NE], F32),
            ("rank", [P, NE + 1], F32), ("sel", [P, OVER, NE], F32), ("slot", [P, T, ITEMS + 1], F32),
            ("gt", [P, T, ITEMS + 1], F32), ("ef", [P, 8], F32), ("junk", [P, NE], F32), ("tab", [P, 8], I32))

        ps = ctx.enter_context(nc.psum_tensor("ps", [P, 8, CH], F32))

        raw_landed = [sem(f"raw_landed{i}") for i in range(RAW)]
        hi_ready, lo_ready, units_used = sem("hi_ready"), sem("lo_ready"), sem("units_used")
        consts_in, ones_set, consts_ready = sem("consts_in"), sem("ones_set"), sem("consts_ready")
        x_in = [sem(f"x_in{t}") for t in range(T)]
        dve_done, act_done, pool_done = sem("dve_done"), sem("act_done"), sem("pool_done")
        sumsq_ready, squares_ready, rms_ready, xs_ready = sem("sumsq_ready"), sem("squares_ready"), sem("rms_ready"), sem("xs_ready")
        xT_raw, xTh_ready, xT_ready = sem("xT_raw"), sem("xTh_ready"), sem("xT_ready")
        qkv_out = sem("qkv_out")
        z_ready, lnp_ready, sp_ready = sem("z_ready"), sem("lnp_ready"), sem("sp_ready")
        spm_ready, expo_ready, att_exp, att_ready = sem("spm_ready"), sem("expo_ready"), sem("att_exp"), sem("att_ready")
        oT_raw, oTh_ready, oT_ready = sem("oT_raw"), sem("oTh_ready"), sem("oT_ready")
        x_added = sem("x_added")
        silu_ready, h_ready, fTh_ready, fT_ready = (sem("silu_ready"), sem("h_ready"),
                                                              sem("fTh_ready"), sem("fT_ready"))
        low_out, low_scaled, lowT_raw, lowTh_ready, lowT_ready = (
            sem("low_out"), sem("low_scaled"), sem("lowT_raw"), sem("lowTh_ready"), sem("lowT_ready"))
        kvb_out, qb_out = sem("kvb_out"), sem("qb_out")
        kq_normed, kqT_raw, qT_out, kT_out = sem("kq_normed"), sem("kqT_raw"), sem("qT_out"), sem("kT_out")
        sc_ready, max_ready, p_exp, p_ready = sem("sc_ready"), sem("max_ready"), sem("p_exp"), sem("p_ready")
        pT_raw, pT_ready, mask_ready = sem("pT_raw"), sem("pT_ready"), sem("mask_ready")
        logits_ready, wr_ready, gap_ready, gexp_ready = sem("logits_ready"), sem("wr_ready"), sem("gap_ready"), sem("gexp_ready")
        msk_ready, pos_ready, route_ready, gbc_in, iota_ready = (
            sem("msk_ready"), sem("pos_ready"), sem("route_ready"), sem("gbc_in"), sem("iota_ready"))
        onehot_ready, xgh_ready, aux_filled, aux_read = sem("onehot_ready"), sem("xgh_ready"), sem("aux_filled"), sem("aux_read")
        esilu_ready, eh_ready, ehT_raw, ehTh_ready, ehT_ready = (
            sem("esilu_ready"), sem("eh_ready"), sem("ehT_raw"), sem("ehTh_ready"), sem("ehT_ready"))
        ysb_ready, out_done = sem("ysb_ready"), sem("out_done")

        def size(dims):
            n = 1
            for s in dims:
                n *= s
            return n

        def unit_floats(i):
            return size(pre[i][1])

        def halves(u, kind=None):
            dims = pre[u][1] if kind is None else ((2, D) if kind == "down" else (4, CH))
            return [shape_unit(r[u % len(r)], size(dims), *dims) for r in (hi, lo)]

        norm_after = {1: first["sbo"] + 4, 2: first["down"], 3: first["kva"] + 2, 4: NPRE}

        class Units:
            def __init__(self, one_unit):
                self.n, self.one_unit = 0, one_unit

            def until(self, n):
                while self.n < min(n, NPRE):
                    self.one_unit(self.n, self.n, unit_floats(self.n))
                    self.n += 1

        block = ctx.enter_context(nc.Block())

        @block.sync
        def _(sp):
            for t in range(T):
                sp.dma_start(x[:, t, :], x_d[t * P:(t + 1) * P, :]).then_inc(x_in[t], 16)
            for u, (_, dims, src) in enumerate(pre):
                if u >= RAW:
                    sp.wait_ge(lo_ready, u - RAW + 1)
                dst = shape_unit(raw[u % RAW], size(dims), *dims)
                if isinstance(src, list):
                    for m, part in enumerate(src):
                        sp.dma_start(dst[:, :, m, :], part).then_inc(raw_landed[u % RAW], 16)
                else:
                    sp.dma_start(dst, src).then_inc(raw_landed[u % RAW], 16)

            def load_item(j, e):
                for i, (kind, c, q) in enumerate(item_units):
                    s = (NPRE + i) % RAW
                    sp.wait_ge(lo_ready, j * NI + (NPRE + i - RAW + 1))
                    if kind == "down":
                        r0 = c * CH + q * 2 * P
                        sp.dma_start(shape_unit(raw[s], UNIT, 2, D),
                                     ed[e, r0:r0 + 2 * P, :].rearrange("(p k) n -> p k n", k=2)
                                     ).then_inc(raw_landed[s], 16)
                    else:
                        src = eg if kind == "gate" else eu
                        sp.dma_start(shape_unit(raw[s], UNIT, 4, CH),
                                     src[e, q * 4 * P:(q + 1) * 4 * P, c * CH:(c + 1) * CH].rearrange(
                                         "(k p) n -> p k n", p=P)).then_inc(raw_landed[s], 16)

            with sp.Fori(0, NE) as j:
                load_item(j, j)
            sp.wait_ge(route_ready, 1)
            over = sp.value_load(tab[0:1, 1:2], min_val=0, max_val=OVER)
            with sp.If(over > 0):
                with sp.Fori(0, over) as r:
                    e = sp.value_load(tab[0:1, bass.ds(r + 2, 1)], min_val=0, max_val=NE - 1)
                    load_item(r + NE, e)

            sp.wait_ge(aux_read, over * FILLS + (NE * FILLS + 6))
            for t in range(T):
                sp.dma_start(out_d[t * P:(t + 1) * P, :], x[:, t, :]).then_inc(out_done, 16)
            sp.wait_ge(out_done, 16 * T)

        def landed(eng, u, j=None):
            s = u % RAW
            tails = sum(pre[v][0] == "tail" for v in range(s, min(u + 1, NPRE), RAW))
            uses = 16 * (u // RAW + 1 + tails)
            eng.wait_ge(raw_landed[s], uses if j is None else j * (16 * NI // RAW) + uses)

        @block.scalar
        def _(act):
            for dst, src in ((gains[:], gains_d), (gpe[:], gpe_d), (rope[:], rope_d.rearrange("(t p) a r -> p t a r", p=P)),
                             (wr[:], wr_d.rearrange("(k p) e -> p k e", p=P)), (br[:], br_d.partition_broadcast(P))):
                act.dma_start(dst, src).then_inc(consts_in, 16)

            def round_unit(u, n, floats, j=None):
                landed(act, n, j)
                if j is None and u >= HI:
                    act.wait_ge(units_used, u - HI + 1)
                elif j is not None:
                    act.wait_ge(units_used, j * NI + (n - HI + 1))
                act.activation(hi[n % HI][:, 0:floats], raw[n % RAW][:, 0:floats], ACT.Copy).then_inc(hi_ready, 1)

            units = Units(round_unit)

            def root(k, cols):
                act.wait_ge(sumsq_ready, k)
                act.activation(rt[:, 0:cols], ss[:, 0:cols], ACT.Sqrt, bias=eps[:]).then_inc(rms_ready, 1)

            def mean_squares(n, k):
                for t in range(T):
                    if n:
                        act.wait_ge(x_added, T * (n - 1) + t + 1)
                        act.wait_ge(xT_raw, 4 * n if n < 3 else 16)
                    else:
                        act.wait_ge(x_in[t], 16)
                    act.activation(xs[:, t, :], x[:, t, :], ACT.Square, scale=D ** -0.5,
                                   accum_out=ss[:, t:t + 1]).then_inc(squares_ready, 1)
                act.wait_ge(squares_ready, T * (n + 1))
                act.activation(rt[:, 0:T], ss[:, 0:T], ACT.Sqrt, bias=eps[:]).then_inc(rms_ready, 1)

            def norm_transposed(n, g):
                for b in range(4):
                    act.wait_ge(xT_raw, 4 * n + b + 1)
                    if n:
                        act.wait_ge(units_used, norm_after[n])
                    for k in (2 * b, 2 * b + 1):
                        got = act.activation(xTh[:, k, :], ps[:, 4 + b, (k % 2) * S:(k % 2 + 1) * S], ACT.Copy,
                                             scale=gains[:, g + k:g + k + 1])
                    got.then_inc(xTh_ready, 1)

            act.wait_ge(consts_ready, 1)
            act.wait_ge(consts_in, 16 * 5)
            mean_squares(0, 1)
            units.until(3)
            norm_transposed(0, G_MIX0)
            for c in range(6):
                units.until(2 * c + 5)
                act.wait_ge(units_used, first["qkv"] + 2 * c + 2)
                b = 4 * (c % 2)
                if c < 4:
                    dst = (qT if c < 2 else kT)[:, 4 * (c % 2):4 * (c % 2) + 4, :]
                    act.activation(dst, ps[:, b:b + 4, 0:S], ACT.Copy, scale=HD ** -0.5 if c < 2 else 1.0).then_inc(qkv_out, 1)
                else:
                    act.activation(v1[:, :, (c - 4) * CH:(c - 3) * CH], ps[:, b:b + T, :], ACT.Copy).then_inc(qkv_out, 1)

            def log_part(h):
                act.wait_ge(z_ready, h + 1)
                act.activation(ab[:, h % 4, :], ps[:, h % 4, 0:384], ACT.Abs).then_inc(act_done, 1)
                act.wait_ge(act_done, 2 * h + 1)
                act.activation(ln_[:, h % 4, :], ab[:, h % 4, :], ACT.Exp, scale=-1.0).then_inc(act_done, 1)
                act.wait_ge(act_done, 2 * h + 2)
                act.activation(ln_[:, h % 4, :], ln_[:, h % 4, :], ACT.Ln, bias=one[:]).then_inc(lnp_ready, 1)

            def att_part(h):
                act.wait_ge(expo_ready, h + 1)
                act.activation(att[:, h % 4, :], ps[:, h % 4, 0:384], ACT.Exp).then_inc(att_exp, 1)

            def head_out(layer, p):
                act.wait_ge(oT_raw, 8 * layer + p + 1)
                act.activation(xTh[:, p, :], ps[:, 4 + p % 2, 0:S], ACT.Copy).then_inc(oTh_ready, 1)

            for i in range(HEADS + 4):
                if i < HEADS:
                    log_part(i)
                if 2 <= i < HEADS + 2:
                    att_part(i - 2)
                if i >= 5 and i % 2 == 1:
                    head_out(0, (i - 5) // 2)
            units.until(first["gate"] + 2)
            mean_squares(1, 2)
            units.until(first["gate"] + 3)
            norm_transposed(1, G_FFN0)
            for c in range(6):
                nt = 4 if c < 5 else 2
                last = first["gate"] + 4 * c + (3 if c < 5 else 1)
                units.until(last + 4)
                act.wait_ge(units_used, last + 1)
                if c:
                    act.wait_ge(h_ready, c)
                b = 4 * (c % 2)
                act.activation(sg[:, 0:nt, :], ps[:, b:b + nt, 0:S], ACT.Silu).then_inc(silu_ready, 1)
                act.wait_ge(h_ready, c + 1)
                act.activation(fTh[:, 4 * c:4 * c + nt, :], hm[:, 0:nt, :], ACT.Copy).then_inc(fTh_ready, 1)
            units.until(first["down"] + 11 + 2)
            mean_squares(2, 3)
            units.until(first["down"] + 11 + 3)
            norm_transposed(2, G_KV)
            units.until(first["kva"] + 1 + 4)
            act.wait_ge(units_used, first["kva"] + 2)
            act.activation(kva[:], ps[:, 0:T, 0:RKV + ROPE], ACT.Copy).then_inc(low_out, 1)
            root(1, 4)
            act.wait_ge(lowT_raw, 1)
            for k in range(2):
                got = act.activation(cTh[:, k, :], ps[:, 2, k * S:(k + 1) * S], ACT.Copy,
                                     scale=gains[:, G_KVA + k:G_KVA + k + 1])
            got.then_inc(lowTh_ready, 1)
            for q in range(2):
                units.until(first["kvb"] + q + 4)
                act.wait_ge(units_used, first["kvb"] + q + 1)
                for n in range(2):
                    for t in range(T):
                        b = (4 if q == 0 else 0) + 2 * n + t
                        src = ps[:, b, :].rearrange("p (h d) -> p h d", h=4)
                        hs = slice(8 * q + 4 * n, 8 * q + 4 * n + 4)
                        act.activation(v2[:, t, hs, :], src[:, :, HD:2 * HD], ACT.Copy)
                        act.activation(kf[:, t, hs, 0:HD], src[:, :, 0:HD], ACT.Copy).then_inc(kvb_out, 1)
            norm_transposed(3, G_MIX1)
            units.until(first["qa"] + 1 + 4)
            act.wait_ge(units_used, first["qa"] + 2)
            act.activation(qa[:], ps[:, 0:T, 0:RQ], ACT.Copy).then_inc(low_out, 1)
            root(2, T)
            act.wait_ge(lowT_raw, 2)
            for k in range(3):
                got = act.activation(aTh[:, k, :], ps[:, 2 + k // 2, (k % 2) * S:(k % 2 + 1) * S], ACT.Copy,
                                     scale=gains[:, G_QA + k:G_QA + k + 1])
            got.then_inc(lowTh_ready, 1)
            for q in range(3):
                units.until(first["qb"] + q + 4)
                act.wait_ge(units_used, first["qb"] + q + 1)
                b = 2 * (q % 2) + 4
                flat = q2[:].rearrange("p t h d -> p t (h d)")
                act.activation(flat[:, :, q * CH:(q + 1) * CH], ps[:, b:b + T, :], ACT.Copy).then_inc(qb_out, 1)
            act.wait_ge(sumsq_ready, 3)
            act.activation(r16[:, 0:2, :], s16[:, 0:2, :], ACT.Sqrt, bias=eps[:]).then_inc(rms_ready, 1)
            act.wait_ge(sumsq_ready, 4)
            act.activation(r16[:, 0:4, :], s16[:, 0:4, :], ACT.Sqrt, bias=eps[:]).then_inc(rms_ready, 1)
            for g in range(8):
                act.wait_ge(kqT_raw, 2 * g + 1)
                act.activation(qT2[0:QK, 2 * g:2 * g + 2, :], ps[0:QK, (2 * g) % 8, :].rearrange("p (h s) -> p h s", h=2),
                               ACT.Copy, scale=gains[0:QK, G_QN:G_QN + 1]).then_inc(qT_out, 1)

            scale = float(QK) ** -0.5

            def p_part(h):
                act.wait_ge(max_ready, h + 1)
                act.activation(pm[:, h % 4, 0:P], pm[:, h % 4, 0:P], ACT.Exp, scale=scale, bias=nm[:, h, 0:1],
                               accum_out=sm[:, h, 0:1]).then_inc(p_exp, 1)
                act.activation(pm[:, h % 4, P:384], pm[:, h % 4, P:384], ACT.Exp, scale=scale, bias=nm[:, h, 1:2],
                               accum_out=sm[:, h, 1:2]).then_inc(p_exp, 1)

            def pt_part(h):
                act.wait_ge(pT_raw, h + 1)
                act.activation(pt[:, h % 4, :], ps[:, 6 + h % 2, 0:384], ACT.Copy).then_inc(pT_ready, 1)

            for i in range(HEADS + 4):
                if i < HEADS:
                    p_part(i)
                if 2 <= i < HEADS + 2:
                    pt_part(i - 2)
                if i >= 5 and i % 2 == 1:
                    head_out(1, (i - 5) // 2)
            units.until(NPRE)
            mean_squares(3, 8)
            act.dma_start(gbc[:], gffn1_d.partition_broadcast(P)).then_inc(gbc_in, 16)
            norm_transposed(4, G_FFN1)
            act.wait_ge(gap_ready, 1)
            act.activation(pex[:], ged[:, :, 0], ACT.Exp).then_inc(gexp_ready, 1)
            act.wait_ge(route_ready, 1)
            items = act.value_load(tab[0:1, 0:1], min_val=NE, max_val=ITEMS)
            def gather_hi(half, fill, n, j):
                act.wait_ge(aux_filled, fill)
                if n is not None:
                    act.wait_ge(units_used, n)
                act.activation(xgh[:, 4 * half:4 * half + 4, :], ps[:, 7, :].rearrange("p (k s) -> p k s", s=P),
                               ACT.Copy).then_inc(xgh_ready, 1)

            def take_y(n):
                act.wait_ge(units_used, n)
                act.activation(ysb[:], ps[:, 4:6, :].rearrange("p b n -> p (b n)"), ACT.Copy).then_inc(ysb_ready, 1)

            for half in range(2):
                gather_hi(half, half + 1, None, None)
            with act.Fori(0, items) as j:
                done = [0]

                def item_until(n):
                    while done[0] < n:
                        round_unit(None, NPRE + done[0], UNIT, j)
                        done[0] += 1

                def h_hi(c):
                    act.wait_ge(ehT_raw, j * NC + (c + 1))
                    act.activation(hTh[:, c % 2, :], ps[:, 6, :], ACT.Copy).then_inc(ehTh_ready, 1)

                item_until(2)
                take_y(j * NI + NPRE)
                for c in range(NC):
                    if c:
                        item_until(6 * c + 2)
                        h_hi(c - 1)
                    item_until(6 * c + 4 if c else 6)
                    act.wait_ge(units_used, j * NI + (NPRE + (6 * c + 2 if c else 4)))
                    act.wait_ge(eh_ready, j * NC + max(c, 1))
                    act.activation(sl[:, c % 2, :], ps[:, 2 * (c % 2), :], ACT.Silu).then_inc(esilu_ready, 1)
                gather_hi(0, j * FILLS + 8, j * NI + (NPRE + 38), j)
                item_until(NI)
                h_hi(NC - 1)
                gather_hi(1, j * FILLS + 9, None, j)
            take_y(items * NI + NPRE)

        @block.vector
        def _(dve):
            steps = [0]

            def after(ins):
                steps[0] += 1
                ins.then_inc(dve_done, 1)
                dve.wait_ge(dve_done, steps[0])

            def subtract_unit(u, n, floats, j=None):
                dve.wait_ge(hi_ready, n + 1 if j is None else j * NI + (n + 1))
                dve.tensor_tensor(lo[n % LO][:, 0:floats], raw[n % RAW][:, 0:floats],
                                  hi[n % HI][:, 0:floats].bitcast(F32), ALU.subtract).then_inc(lo_ready, 1)

            units = Units(subtract_unit)

            def reciprocal_root(k, cols):
                dve.wait_ge(rms_ready, k)
                after(dve.reciprocal(rs[:, 0:cols], rt[:, 0:cols]))

            def normalise(k):
                reciprocal_root(k, T)
                for t in range(T):
                    dve.tensor_scalar(xs[:, t, :], x[:, t, :], rs[:, t:t + 1], None, ALU.mult).then_inc(xs_ready, 1)

            def norm_transposed(n, g):
                for b in range(4):
                    dve.wait_ge(xTh_ready, 4 * n + b + 1)
                    for k in (2 * b, 2 * b + 1):
                        got = dve.scalar_tensor_tensor(
                            out=xTl[:, k, :], in0=ps[:, 4 + b, (k % 2) * S:(k % 2 + 1) * S], scalar=gains[:, g + k:g + k + 1],
                            in1=xTh[:, k, :].bitcast(F32), op0=ALU.mult, op1=ALU.subtract)
                    got.then_inc(xT_ready, 1)

            def add_projection(n, name, count):
                dve.wait_ge(units_used, first[name] + count)
                for t in range(T):
                    dve.tensor_tensor(x[:, t, :], x[:, t, :], ps[:, 2 * t:2 * t + 2, :].rearrange("p b n -> p (b n)"),
                                      ALU.add).then_inc(x_added, 1)
                dve.wait_ge(x_added, T * (n + 1))

            dve.wait_ge(consts_ready, 1)
            dve.wait_ge(consts_in, 16 * 5)
            dve.tensor_copy(wrh[:], wr[:]).then_inc(wr_ready, 1)
            dve.wait_ge(wr_ready, 1)
            dve.tensor_tensor(wrl[:], wr[:], wrh[:].bitcast(F32), ALU.subtract).then_inc(wr_ready, 1)
            normalise(1)
            units.until(3)
            norm_transposed(0, G_MIX0)
            for c in range(6):
                units.until(2 * c + 5)

            def softplus_part(h):
                dve.wait_ge(lnp_ready, h + 1)
                dve.scalar_tensor_tensor(out=spb[:, h % 4, :], in0=ps[:, h % 4, 0:384], scalar=0.0, in1=ln_[:, h % 4, :],
                                         op0=ALU.max, op1=ALU.add).then_inc(sp_ready, 1)

            def head_out(layer, p):
                dve.wait_ge(oTh_ready, 8 * layer + p + 1)
                dve.tensor_tensor(xTl[:, p, :], ps[:, 4 + p % 2, 0:S], xTh[:, p, :].bitcast(F32),
                                  ALU.subtract).then_inc(oT_ready, 1)

            for i in range(HEADS + 4):
                if i < HEADS:
                    softplus_part(i)
                if i >= 5 and i % 2 == 1:
                    head_out(0, (i - 5) // 2)
            units.until(first["gate"] + 2)
            add_projection(0, "sbo", 4)
            normalise(2)
            units.until(first["gate"] + 3)
            norm_transposed(1, G_FFN0)
            for c in range(6):
                nt = 4 if c < 5 else 2
                last = first["gate"] + 4 * c + (3 if c < 5 else 1)
                units.until(last + 4)
                dve.wait_ge(silu_ready, c + 1)
                if c:
                    dve.wait_ge(fT_ready, c)
                b = 4 * (c % 2)
                dve.tensor_tensor(hm[:, 0:nt, :], sg[:, 0:nt, :], ps[:, b:b + nt, S:2 * S], ALU.mult).then_inc(h_ready, 1)
                dve.wait_ge(fTh_ready, c + 1)
                dve.tensor_tensor(fTl[:, 4 * c:4 * c + nt, :], hm[:, 0:nt, :], fTh[:, 4 * c:4 * c + nt, :].bitcast(F32),
                                  ALU.subtract).then_inc(fT_ready, 1)
            units.until(first["down"] + 11 + 2)
            add_projection(1, "down", 11)
            normalise(3)
            units.until(first["down"] + 11 + 3)
            norm_transposed(2, G_KV)
            units.until(first["kva"] + 1 + 4)
            dve.wait_ge(low_out, 1)
            for t in range(T):
                after(dve.tensor_tensor_reduce(ra[:].rearrange("p h r -> p (h r)")[:, 0:RKV], kva[:, t, 0:RKV], kva[:, t, 0:RKV],
                                               1.0 / RKV, 0.0, ALU.mult, ALU.add, ss[:, t:t + 1]))
                after(dve.tensor_tensor_reduce(rb[:, 0, :], kva[:, t, RKV:RKV + ROPE], kva[:, t, RKV:RKV + ROPE],
                                               1.0 / ROPE, 0.0, ALU.mult, ALU.add, ss[:, 2 + t:3 + t]))
            dve.engine_nop().then_inc(sumsq_ready, 1)
            reciprocal_root(4, 4)
            for t in range(T):
                dve.tensor_scalar(kva[:, t, 0:RKV], kva[:, t, 0:RKV], rs[:, t:t + 1], None, ALU.mult).then_inc(low_scaled, 1)
                after(dve.scalar_tensor_tensor(out=ra[:, t, :], in0=kva[:, t, RKV:RKV + ROPE], scalar=rs[:, 2 + t:3 + t],
                                               in1=gpe[:, 0, :], op0=ALU.mult, op1=ALU.mult))

            def rotate(dst, src, other, t, heads):
                cos = rope[:, t, 0, :].unsqueeze(1).to_broadcast([P, heads, ROPE])
                sin = rope[:, t, 1, :].unsqueeze(1).to_broadcast([P, heads, ROPE])
                half = ROPE // 2
                dve.tensor_tensor(other[:, :, 0:half], src[:, :, half:ROPE], sin[:, :, 0:half], ALU.mult)
                after(dve.tensor_tensor(other[:, :, half:ROPE], src[:, :, 0:half], sin[:, :, half:ROPE], ALU.mult))
                after(dve.tensor_tensor(src, src, cos, ALU.mult))
                after(dve.tensor_tensor(dst, src, other, ALU.add))

            for t in range(T):
                rotate(rb[:, 2 + t:3 + t, :], ra[:, t:t + 1, :], rb[:, t:t + 1, :], t, 1)
                for g in range(HEADS):
                    got = dve.tensor_copy(kf[:, t, g, HD:QK], rb[:, 2 + t, :])
                after(got)
            dve.wait_ge(lowTh_ready, 1)
            for k in range(2):
                got = dve.scalar_tensor_tensor(out=cTl[:, k, :], in0=ps[:, 2, k * S:(k + 1) * S],
                                               scalar=gains[:, G_KVA + k:G_KVA + k + 1], in1=cTh[:, k, :].bitcast(F32),
                                               op0=ALU.mult, op1=ALU.subtract)
            got.then_inc(lowT_ready, 1)
            for q in range(2):
                units.until(first["kvb"] + q + 4)
            norm_transposed(3, G_MIX1)
            units.until(first["qa"] + 1 + 4)

            sq = xs[:].rearrange("p t d -> p (t d)")

            def head_squares(src, dim, row):
                tmp = sq[:, 0:HEADS * dim].rearrange("p (h d) -> p h d", d=dim)
                after(dve.scalar_tensor_tensor(out=tmp, in0=src, scalar=1.0 / dim, in1=src, op0=ALU.mult, op1=ALU.mult))
                after(dve.tensor_reduce(s16[:, row, :], tmp, AXX, ALU.add))

            dve.wait_ge(low_out, 2)
            for t in range(T):
                after(dve.tensor_tensor_reduce(sq[:, 0:RQ], qa[:, t, :], qa[:, t, :], 1.0 / RQ, 0.0, ALU.mult, ALU.add,
                                               ss[:, t:t + 1]))
            dve.engine_nop().then_inc(sumsq_ready, 1)
            reciprocal_root(5, T)
            for t in range(T):
                dve.tensor_scalar(qa[:, t, :], qa[:, t, :], rs[:, t:t + 1], None, ALU.mult).then_inc(low_scaled, 1)
            dve.wait_ge(kvb_out, 8)
            for t in range(T):
                head_squares(kf[:, t, :, 0:HD], HD, t)
            dve.engine_nop().then_inc(sumsq_ready, 1)
            dve.wait_ge(lowTh_ready, 2)
            for k in range(3):
                got = dve.scalar_tensor_tensor(out=aTl[:, k, :], in0=ps[:, 2 + k // 2, (k % 2) * S:(k % 2 + 1) * S],
                                               scalar=gains[:, G_QA + k:G_QA + k + 1], in1=aTh[:, k, :].bitcast(F32),
                                               op0=ALU.mult, op1=ALU.subtract)
            got.then_inc(lowT_ready, 1)
            for q in range(3):
                units.until(first["qb"] + q + 4)
            dve.wait_ge(rms_ready, 6)
            after(dve.reciprocal(i16[:, 0:2, :], r16[:, 0:2, :]))

            def head_scale(src, dim, row):
                return dve.tensor_tensor(src, src, i16[:, row, :].unsqueeze(2).to_broadcast([P, HEADS, dim]), ALU.mult)

            for t in range(T):
                head_scale(kf[:, t, :, 0:HD], HD, t).then_inc(kq_normed, 1)
            dve.wait_ge(qb_out, 3)
            for t in range(T):
                head_squares(q2[:, t, :, 0:HD], HD, t)
                head_squares(q2[:, t, :, HD:QK], ROPE, 2 + t)
            dve.engine_nop().then_inc(sumsq_ready, 1)
            dve.wait_ge(rms_ready, 7)
            after(dve.reciprocal(i16[:], r16[:]))
            for t in range(T):
                after(head_scale(q2[:, t, :, 0:HD], HD, t))
                after(head_scale(q2[:, t, :, HD:QK], ROPE, 2 + t))
                after(dve.tensor_tensor(ra[:], q2[:, t, :, HD:QK],
                                        gpe[:, 1, :].unsqueeze(1).to_broadcast([P, HEADS, ROPE]), ALU.mult))
                rotate(q2[:, t, :, HD:QK], ra[:], rb[:], t, HEADS)
            dve.engine_nop().then_inc(kq_normed, 1)
            for g in range(8):
                dve.wait_ge(kqT_raw, 2 * g + 2)
                dve.tensor_scalar(kT2[0:QK, 2 * g:2 * g + 2, :],
                                  ps[0:QK, (2 * g + 1) % 8, :].rearrange("p (h s) -> p h s", h=2),
                                  gains[0:QK, G_KN:G_KN + 1], None, ALU.mult).then_inc(kT_out, 1)
            dve.wait_ge(mask_ready, 1)

            def max_part(h):
                dve.wait_ge(sc_ready, h + 1)
                after(dve.tensor_tensor(pm[:, h % 4, :], ps[:, h % 4, 0:384], mask[:], ALU.add))
                dve.tensor_reduce(mx[:, h, 0:1], pm[:, h % 4, 0:P], AXX, ALU.max)
                after(dve.tensor_reduce(mx[:, h, 1:2], pm[:, h % 4, P:384], AXX, ALU.max))
                dve.tensor_scalar(nm[:, h, :], mx[:, h, :], -float(QK) ** -0.5, None, ALU.mult).then_inc(max_ready, 1)

            def share_part(h):
                dve.wait_ge(p_exp, 2 * h + 2)
                after(dve.reciprocal(rc[:, h, :], sm[:, h, :]))
                dve.tensor_scalar(pm[:, h % 4, 0:P], pm[:, h % 4, 0:P], rc[:, h, 0:1], None, ALU.mult).then_inc(p_ready, 1)
                dve.tensor_scalar(pm[:, h % 4, P:384], pm[:, h % 4, P:384], rc[:, h, 1:2], None,
                                  ALU.mult).then_inc(p_ready, 1)

            for i in range(HEADS + 4):
                if i < HEADS:
                    max_part(i)
                if 1 <= i < HEADS + 1:
                    share_part(i - 1)
                if i >= 5 and i % 2 == 1:
                    head_out(1, (i - 5) // 2)
            units.until(NPRE)
            add_projection(2, "mlo", 4)
            normalise(8)
            norm_transposed(4, G_FFN1)
            dve.wait_ge(xT_raw, 20)
            dve.wait_ge(gbc_in, 16)
            for t in range(T):
                dve.tensor_tensor(xs[:, t, :], xs[:, t, :], gbc[:], ALU.mult)
            dve.wait_ge(logits_ready, 1)
            dve.wait_ge(iota_ready, 1)
            after(dve.tensor_tensor(lg[:], ps[:, 0, 0:T * NE].rearrange("p (t e) -> p t e", t=T),
                                    br[:].unsqueeze(1).to_broadcast([P, T, NE]), ALU.add))
            for t in range(T):
                after(dve.max(mv[:, t, :], lg[:, t, :]))
                after(dve.max_index(mi[:, t, :], mv[:, t, :], lg[:, t, :]))
            dve.tensor_tensor(ged[:, :, 0], mv[:, :, 1], mv[:, :, 0], ALU.subtract).then_inc(gap_ready, 1)
            after(dve.tensor_copy(ix[:], mi[:]))
            for t in range(T):
                dve.tensor_scalar(is1[:, t, :], iota8[:], ix[:, t, 0:1], None, ALU.is_equal)
                after(dve.tensor_scalar(is2[:, t, :], iota8[:], ix[:, t, 1:2], None, ALU.is_equal))
            dve.tensor_tensor(msk[:], is1[:], is2[:], ALU.add).then_inc(msk_ready, 1)
            dve.wait_ge(gexp_ready, 1)
            after(dve.tensor_scalar(ged[:, :, 1], pex[:], 1.0, None, ALU.add))
            after(dve.reciprocal(ged[:, :, 2], ged[:, :, 1]))
            after(dve.tensor_tensor(ged[:, :, 3], ged[:, :, 2], pex[:], ALU.mult))
            for t in range(T):
                after(dve.tensor_scalar(gte[:, t, :], is1[:, t, :], ged[:, t, 2:3], None, ALU.mult))
                after(dve.scalar_tensor_tensor(out=gte[:, t, :], in0=is2[:, t, :], scalar=ged[:, t, 3:4], in1=gte[:, t, :],
                                               op0=ALU.mult, op1=ALU.add))
            dve.wait_ge(pos_ready, 1)
            for t in range(T):
                after(dve.scalar_tensor_tensor(out=posm[:, t, :], in0=msk[:, t, :], scalar=-FAR,
                                               in1=ps[:, 1, t * NE:(t + 1) * NE], op0=ALU.mult, op1=ALU.add))
                after(dve.tensor_scalar(posm[:, t, :], posm[:, t, :], FAR, None, ALU.add))
            after(dve.tensor_scalar(cnt[:], ps[:, 1, 2 * NE:3 * NE], float(P), None, ALU.is_gt))
            after(dve.memset(rank[:], 0.0))
            for e in range(NE):
                after(dve.tensor_tensor(rank[:, e + 1:e + 2], rank[:, e:e + 1], cnt[:, e:e + 1], ALU.add))
            for r in range(OVER):
                after(dve.scalar_tensor_tensor(out=sel[:, r, :], in0=rank[:, 0:NE], scalar=float(r), in1=cnt[:],
                                               op0=ALU.is_equal, op1=ALU.mult))
            after(dve.tensor_copy(slot[:, :, 0:NE], posm[:]))
            after(dve.memset(slot[:, :, ITEMS:], -1.0))
            after(dve.memset(gt[:, :, 0:1], 0.0))
            after(dve.memset(ST[:], 0.0))
            after(dve.tensor_copy(gt[:, :, 1:NE + 1], gte[:]))
            for r in range(OVER):
                for t in range(T):
                    after(dve.tensor_tensor_reduce(junk[:], posm[:, t, :], sel[:, r, :], 1.0, -float(P), ALU.mult, ALU.add,
                                                   slot[:, t, NE + r:NE + r + 1]))
                    after(dve.tensor_tensor_reduce(junk[:], gte[:, t, :], sel[:, r, :], 1.0, 0.0, ALU.mult, ALU.add,
                                                   gt[:, t, NE + r + 1:NE + r + 2]))
                after(dve.tensor_tensor_reduce(junk[:], iota8[:], sel[:, r, :], 1.0, 0.0, ALU.mult, ALU.add,
                                               ef[:, 2 + r:3 + r]))
            after(dve.tensor_copy(ef[:, 1:2], rank[:, NE:NE + 1]))
            after(dve.tensor_scalar(ef[:, 0:1], rank[:, NE:NE + 1], float(NE), None, ALU.add))
            dve.tensor_copy(tab[:, 0:2 + OVER], ef[:, 0:2 + OVER]).then_inc(route_ready, 1)
            dve.wait_ge(route_ready, 1)
            items = dve.value_load(tab[0:1, 0:1], min_val=NE, max_val=ITEMS)
            for counts_from_one in (eh_ready, ehT_ready):
                dve.nop().then_inc(counts_from_one, 1)

            def build_onehot(col):
                for t in range(T):
                    got = dve.tensor_scalar(onehot[:, t, :], iota[:], slot[:, t, col], None, ALU.is_equal)
                got.then_inc(onehot_ready, 1)

            def gather_lo(half, ready, fill):
                dve.wait_ge(xgh_ready, ready)
                dve.tensor_tensor(xgl[:, 4 * half:4 * half + 4, :], ps[:, 7, :].rearrange("p (k s) -> p k s", s=P),
                                  xgh[:, 4 * half:4 * half + 4, :].bitcast(F32), ALU.subtract).then_inc(aux_read, 1)

            def add_back(n, fill, col):
                t, half = n // 2, n % 2
                dve.wait_ge(aux_filled, fill)
                xo = x[:, t, half * CH:(half + 1) * CH]
                dve.scalar_tensor_tensor(out=xo, in0=ps[:, 7, :], scalar=gt[:, t, col], in1=xo,
                                         op0=ALU.mult, op1=ALU.add).then_inc(aux_read, 1)

            build_onehot(slice(0, 1))
            for half in range(2):
                gather_lo(half, half + 1, half + 1)
            with dve.Fori(0, items) as j:
                done = [0]

                def item_until(n):
                    while done[0] < n:
                        subtract_unit(None, NPRE + done[0], UNIT, j)
                        done[0] += 1

                def h_lo(c):
                    dve.wait_ge(ehTh_ready, j * NC + (c + 1))
                    dve.tensor_tensor(hTl[:, c % 2, :], ps[:, 6, :], hTh[:, c % 2, :].bitcast(F32),
                                      ALU.subtract).then_inc(ehT_ready, 1)

                for c in range(NC):
                    if c:
                        item_until(6 * c + 2)
                        h_lo(c - 1)
                    else:
                        item_until(4)
                    if c < 2:
                        add_back(2 * c, j * FILLS + (3 + 2 * c), bass.ds(j, 1))
                    if c == 2:
                        dve.wait_ge(aux_filled, j * FILLS + 7)
                        dve.tensor_copy(ST[:], ps[:, 7, 0:S]).then_inc(aux_read, 1)
                        build_onehot(bass.ds(j + 1, 1))
                    item_until(6 * c + 4 if c else 6)
                    dve.wait_ge(esilu_ready, j * NC + (c + 1))
                    dve.tensor_tensor(hb[:, c % 2, :], sl[:, c % 2, :], ps[:, 2 * (c % 2) + 1, :], ALU.mult).then_inc(eh_ready, 1)
                    if c < 2:
                        add_back(2 * c + 1, j * FILLS + (4 + 2 * c), bass.ds(j, 1))
                gather_lo(0, j * 2 + 3, None)
                item_until(NI)
                h_lo(NC - 1)
                gather_lo(1, j * 2 + 4, None)
            for n in range(4):
                add_back(n, items * FILLS + (3 + n), bass.ds(items, 1))

        @block.gpsimd
        def _(pool):
            for tile, value in ((ident, 0.0), (ones, 1.0), (before, 1.0), (ntri, -1.0), (nones, -1.0), (eps, EPS), (one, 1.0)):
                pool.memset(tile[:], value).then_inc(ones_set, 1)
            pool.wait_ge(ones_set, 7)
            pool.affine_select(out=ident[:], in_=ident[:], compare_op=ALU.not_equal, fill=1.0, base=0,
                               pattern=[[-1, P]], channel_multiplier=1)
            pool.affine_select(out=before[:], in_=before[:], compare_op=ALU.is_gt, fill=0.0, base=0,
                               pattern=[[1, P]], channel_multiplier=-1)
            pool.iota(iota8[:], pattern=[[1, NE]], base=0, channel_multiplier=0, allow_small_or_imprecise_dtypes=True)
            pool.affine_select(out=ntri[:], in_=ntri[:], compare_op=ALU.is_ge, fill=0.0, base=0,
                               pattern=[[-1, P]], channel_multiplier=1).then_inc(consts_ready, 1)

            def diagonal(tile):
                v = tile.rearrange("p (b n) -> p b n", b=3)[:, 0:3:2, :]
                return pool.affine_select(out=v, in_=v, compare_op=ALU.is_gt, fill=0.0, base=0,
                                          pattern=[[0, 2], [1, P]], channel_multiplier=-1)

            for i in range(HEADS + 2):
                if i < HEADS:
                    pool.wait_ge(sp_ready, i + 1)
                    diagonal(spb[:, i % 4, :]).then_inc(spm_ready, 1)
                if i >= 2:
                    pool.wait_ge(att_exp, i - 1)
                    diagonal(att[:, (i - 2) % 4, :]).then_inc(att_ready, 1)
            pool.wait_ge(kqT_raw, 16)
            pool.memset(mask[:], 0.0).then_inc(pool_done, 1)
            pool.wait_ge(pool_done, 1)
            v = mask[:].rearrange("p (b n) -> p b n", b=3)[:, 0:3:2, :]
            pool.affine_select(out=v, in_=v, compare_op=ALU.is_ge, fill=NEG, base=0,
                               pattern=[[0, 2], [-1, P]], channel_multiplier=1).then_inc(mask_ready, 1)
            pool.wait_ge(x_added, 3 * T)
            pool.iota(iota[:], pattern=[[1, P]], base=0, channel_multiplier=0,
                      allow_small_or_imprecise_dtypes=True).then_inc(iota_ready, 1)

        @block.tensor
        def _(pe):
            def three(out, a, b, start, stop):
                pe.matmul(out, a[0], b[0], start=start, stop=False, skip_group_check=True)
                pe.matmul(out, a[0], b[1], start=False, stop=False, skip_group_check=True)
                return pe.matmul(out, a[1], b[0], start=False, stop=stop, skip_group_check=True)

            def both(h, l, *at):
                return h[at], l[at]

            def transpose_x(n):
                for t in range(T):
                    pe.wait_ge(xs_ready, T * (n if n < 3 else n - 1) + t + 1)
                    for k in range(KD):
                        o = (k % 2) * S + t * P
                        got = pe.transpose(ps[:, 4 + k // 2, o:o + P], xs[:, t, k * P:(k + 1) * P], ident[:])
                        if t == T - 1 and k % 2:
                            got.then_inc(xT_raw, 1)

            def split(u):
                pe.wait_ge(lo_ready, u + 1)
                return halves(u)

            def projection(name, a_h, a_l, tiles, wait_rows):
                for q in range(tiles // 2):
                    wh, wl = split(first[name] + q)
                    for kk in range(2):
                        k = 2 * q + kk
                        wait_rows(k)
                        for t in range(T):
                            for half in range(2):
                                got = three(ps[:, 2 * t + half, :], both(a_h, a_l, ALL, k, slice(t * P, t * P + P)),
                                            both(wh, wl, ALL, kk, slice(half * CH, half * CH + CH)), k == 0, k == tiles - 1)
                    got.then_inc(units_used, 1)

            pe.wait_ge(consts_ready, 1)
            transpose_x(0)
            for c in range(6):
                b = 4 * (c % 2)
                if c >= 2:
                    pe.wait_ge(qkv_out, c - 1)
                for q in range(2):
                    wh, wl = split(first["qkv"] + 2 * c + q)
                    pe.wait_ge(xT_ready, 2 * q + 2)
                    for m in range(4 if c < 4 else T):
                        for kk in range(4):
                            k = 4 * q + kk
                            if c < 4:
                                got = three(ps[:, b + m, 0:S], both(wh, wl, ALL, kk, slice(m * P, m * P + P)),
                                            both(xTh, xTl, ALL, k, slice(0, S)), k == 0, k == 7)
                            else:
                                got = three(ps[:, b + m, :], both(xTh, xTl, ALL, k, slice(m * P, m * P + P)),
                                            both(wh, wl, ALL, kk, slice(0, CH)), k == 0, k == 7)
                    got.then_inc(units_used, 1)

            pe.wait_ge(qkv_out, 6)

            def z_part(h):
                if h >= 4:
                    pe.wait_ge(att_exp, h - 3)
                r = slice(HD * (h % 2), HD * (h % 2) + HD)
                pe.matmul(ps[:, h % 4, 0:S], kT[r, h // 2, 0:P], qT[r, h // 2, :], start=True, stop=False, skip_group_check=True)
                pe.matmul(ps[:, h % 4, S:384], kT[r, h // 2, P:S], qT[r, h // 2, P:S], start=False, stop=False,
                          skip_group_check=True).then_inc(z_ready, 1)

            def sum_part(h):
                pe.wait_ge(spm_ready, h + 1)
                sp0, sp1 = spb[:, h % 4, 0:S], spb[:, h % 4, S:384]
                pe.matmul(ps[:, h % 4, 0:S], ntri[:], sp0, start=False, stop=False, skip_group_check=True)
                pe.matmul(ps[:, h % 4, P:S], nones[:], sp1, start=False, stop=False, skip_group_check=True)
                pe.matmul(ps[:, h % 4, S:384], ntri[:], sp1, start=False, stop=True, skip_group_check=True).then_inc(expo_ready, 1)

            def v_part(layer, h, values, probs, ready):
                p, r = h // 2, slice(HD * (h % 2), HD * (h % 2) + HD)
                pe.wait_ge(ready, h + 1)
                if h % 2 == 0 and p >= 2:
                    pe.wait_ge(oT_ready, 8 * layer + p - 1)
                pe.matmul(ps[r, 4 + p % 2, 0:S], values(0, h), probs[:, h % 4, 0:S], start=True, stop=False, skip_group_check=True)
                got = pe.matmul(ps[r, 4 + p % 2, P:S], values(1, h), probs[:, h % 4, S:384], start=False, stop=True,
                                skip_group_check=True)
                if h % 2:
                    got.then_inc(oT_raw, 1)

            for i in range(HEADS + 3):
                if i < HEADS:
                    z_part(i)
                if 2 <= i < HEADS + 2:
                    sum_part(i - 2)
                if i >= 3:
                    v_part(0, i - 3, lambda t, h: v1[:, t, h * HD:(h + 1) * HD], att, att_ready)
            projection("sbo", xTh, xTl, KD, lambda k: pe.wait_ge(oT_ready, k + 1))
            transpose_x(1)
            for c in range(6):
                b = 4 * (c % 2)
                if c >= 2:
                    pe.wait_ge(h_ready, c - 1)
                u0 = first["gate"] + 4 * c
                if c < 5:
                    for n in range(2):
                        for q in range(2):
                            wh, wl = split(u0 + 2 * n + q)
                            pe.wait_ge(xT_ready, 4 + 2 * q + 2)
                            for m in range(4):
                                for kk in range(4):
                                    k = 4 * q + kk
                                    got = three(ps[:, b + m, n * S:(n + 1) * S], both(wh, wl, ALL, kk, slice(m * P, m * P + P)),
                                                both(xTh, xTl, ALL, k, slice(0, S)), k == 0 and n == 0, k == 7)
                            got.then_inc(units_used, 1)
                else:
                    for q in range(2):
                        wh, wl = split(u0 + q)
                        for m in range(2):
                            for kk in range(4):
                                for n in range(2):
                                    k = 4 * q + kk
                                    got = three(ps[:, b + m, n * S:(n + 1) * S], both(wh, wl, ALL, kk, n, slice(m * P, m * P + P)),
                                                both(xTh, xTl, ALL, k, slice(0, S)), k == 0 and n == 0, k == 7)
                        got.then_inc(units_used, 1)
            pe.wait_ge(h_ready, 5)
            projection("down", fTh, fTl, FT, lambda k: pe.wait_ge(fT_ready, k // 4 + 1))
            transpose_x(2)

            def low(name, cols, a_h, a_l, bank, norm):
                for q in range(2):
                    wh, wl = split(first[name] + q)
                    pe.wait_ge(xT_ready, 4 * norm + 2 * q + 2)
                    for t in range(T):
                        for kk in range(4):
                            k = 4 * q + kk
                            got = three(ps[:, bank + t, 0:cols], both(a_h, a_l, ALL, k, slice(t * P, t * P + P)),
                                        both(wh, wl, ALL, kk, slice(0, cols)), k == 0, k == 7)
                    got.then_inc(units_used, 1)

            def low_transposed(src, tiles, scaled):
                pe.wait_ge(low_scaled, scaled)
                for k in range(tiles):
                    for t in range(T):
                        o = (k % 2) * S + t * P
                        got = pe.transpose(ps[:, 2 + k // 2, o:o + P], src[:, t, k * P:(k + 1) * P], ident[:])
                got.then_inc(lowT_raw, 1)

            low("kva", RKV + ROPE, xTh, xTl, 0, 2)
            low_transposed(kva, 2, 2)
            pe.wait_ge(lowT_ready, 1)
            for q in range(2):
                wh, wl = split(first["kvb"] + q)
                for n in range(2):
                    for t in range(T):
                        for k in range(2):
                            got = three(ps[:, (4 if q == 0 else 0) + 2 * n + t, :], both(cTh, cTl, ALL, k, slice(t * P, t * P + P)),
                                        both(wh, wl, ALL, k, slice(n * CH, n * CH + CH)), k == 0, k == 1)
                got.then_inc(units_used, 1)
            pe.wait_ge(kvb_out, 4)
            transpose_x(3)
            pe.wait_ge(kvb_out, 8)
            low("qa", RQ, xTh, xTl, 0, 3)
            low_transposed(qa, 3, 4)
            pe.wait_ge(lowT_ready, 2)
            for q in range(3):
                wh, wl = split(first["qb"] + q)
                if q == 2:
                    pe.wait_ge(qb_out, 1)
                for t in range(T):
                    for k in range(3):
                        got = three(ps[:, 4 + 2 * (q % 2) + t, :], both(aTh, aTl, ALL, k, slice(t * P, t * P + P)),
                                    both(wh, wl, ALL, k, slice(0, CH)), k == 0, k == 2)
                got.then_inc(units_used, 1)
            pe.wait_ge(kq_normed, 3)
            for g in range(16):
                src = q2 if g % 2 == 0 else kf
                if g >= 8:
                    pe.wait_ge(qT_out if g % 2 == 0 else kT_out, (g - 8) // 2 + 1)
                for n in range(2):
                    for t in range(T):
                        o = n * S + t * P
                        got = pe.transpose(ps[0:QK, g % 8, o:o + P], src[:, t, 2 * (g // 2) + n, :], ident[:])
                got.then_inc(kqT_raw, 1)

            pe.wait_ge(qT_out, 8)
            pe.wait_ge(kT_out, 8)

            def score_part(h):
                if h >= 4:
                    pe.wait_ge(max_ready, h - 3)
                pe.matmul(ps[:, h % 4, 0:P], qT2[0:QK, h, 0:P], kT2[0:QK, h, 0:P], start=True, stop=True, skip_group_check=True)
                pe.matmul(ps[:, h % 4, P:384], qT2[0:QK, h, P:S], kT2[0:QK, h, :], start=True, stop=True,
                          skip_group_check=True).then_inc(sc_ready, 1)

            def turn_part(h):
                pe.wait_ge(p_ready, 2 * h + 2)
                if h >= 2:
                    pe.wait_ge(pT_ready, h - 1)
                for b in range(3):
                    got = pe.transpose(ps[:, 6 + h % 2, b * P:(b + 1) * P], pm[:, h % 4, b * P:(b + 1) * P], ident[:])
                got.then_inc(pT_raw, 1)

            for i in range(HEADS + 3):
                if i < HEADS:
                    score_part(i)
                if 2 <= i < HEADS + 2:
                    turn_part(i - 2)
                if i >= 3:
                    v_part(1, i - 3, lambda t, h: v2[:, t, h, :], pt, pT_ready)
            projection("mlo", xTh, xTl, KD, lambda k: pe.wait_ge(oT_ready, 8 + k + 1))
            transpose_x(4)
            pe.wait_ge(xT_ready, 20)
            pe.wait_ge(wr_ready, 2)
            for t in range(T):
                for k in range(KD):
                    got = three(ps[:, 0, t * NE:(t + 1) * NE], both(xTh, xTl, ALL, k, slice(t * P, t * P + P)),
                                both(wrh, wrl, ALL, k), k == 0, k == KD - 1)
            got.then_inc(logits_ready, 1)
            pe.wait_ge(msk_ready, 1)
            pe.matmul(ps[:, 1, 0:NE], before[:], msk[:, 0, :], start=True, stop=True)
            pe.matmul(ps[:, 1, NE:2 * NE], before[:], msk[:, 1, :], start=True, stop=False)
            pe.matmul(ps[:, 1, NE:2 * NE], ones[:], msk[:, 0, :], start=False, stop=True)
            pe.matmul(ps[:, 1, 2 * NE:3 * NE], ones[:], msk[:, 0, :], start=True, stop=False)
            pe.matmul(ps[:, 1, 2 * NE:3 * NE], ones[:], msk[:, 1, :], start=False, stop=True).then_inc(pos_ready, 1)
            pe.wait_ge(route_ready, 1)
            items = pe.value_load(tab[0:1, 0:1], min_val=NE, max_val=ITEMS)

            def gather(half, fill, onehots):
                if fill is not None:
                    pe.wait_ge(aux_read, fill)
                pe.wait_ge(onehot_ready, onehots)
                for kk in range(4):
                    k = 4 * half + kk
                    for t in range(T):
                        got = pe.matmul(ps[:, 7, kk * P:(kk + 1) * P], xs[:, t, k * P:(k + 1) * P], onehot[:, t, :],
                                        start=t == 0, stop=t == T - 1)
                got.then_inc(aux_filled, 1)

            def back(n, fill, ys):
                t, half = n // 2, n % 2
                pe.wait_ge(aux_read, fill)
                pe.wait_ge(ysb_ready, ys)
                pe.matmul(ps[:, 7, :], ST[:, t * P:(t + 1) * P], ysb[:, half * CH:(half + 1) * CH],
                          start=True, stop=True).then_inc(aux_filled, 1)

            gather(0, None, 1)
            gather(1, 1, 1)
            with pe.Fori(0, items) as j:
                pe.wait_ge(aux_read, j * FILLS + 2)
                done = [0]

                def item_split(kind):
                    n = NPRE + done[0]
                    done[0] += 1
                    pe.wait_ge(lo_ready, j * NI + (n + 1))
                    return halves(n, kind)

                def hidden(c, n):
                    for q in range(2):
                        wh, wl = item_split("gate")
                        for kk in range(4):
                            k = 4 * q + kk
                            got = three(ps[:, 2 * (c % 2) + n, :], both(xgh, xgl, ALL, k), both(wh, wl, ALL, kk), k == 0, k == 7)
                        got.then_inc(units_used, 1)

                def turn(c):
                    pe.wait_ge(eh_ready, j * NC + (c + 2))
                    pe.wait_ge(ehT_ready, j * NC + (c + 1))
                    for q in range(2):
                        for k in range(2):
                            i = 2 * q + k
                            got = pe.transpose(ps[:, 6, i * P:(i + 1) * P], hb[:, c % 2, 2 * P * q + k:2 * P * (q + 1):2], ident[:])
                    got.then_inc(ehT_raw, 1)

                def down(c):
                    pe.wait_ge(ehT_ready, j * NC + (c + 2))
                    for q in range(2):
                        wh, wl = item_split("down")
                        for k in range(2):
                            i = 2 * q + k
                            for half in range(2):
                                got = three(ps[:, 4 + half, :], both(hTh, hTl, ALL, c % 2, slice(i * P, (i + 1) * P)),
                                            both(wh, wl, ALL, k, slice(half * CH, (half + 1) * CH)),
                                            c == 0 and i == 0, c == NC - 1 and i == 3)
                        got.then_inc(units_used, 1)

                for c in range(NC):
                    pe.wait_ge(eh_ready, j * NC + max(c, 1))
                    hidden(c, 0)
                    if c:
                        turn(c - 1)
                    if c < 2:
                        back(2 * c, j * FILLS + (2 + 2 * c), j + 1)
                    if c == 2:
                        pe.wait_ge(aux_read, j * FILLS + 6)
                        for t in range(T):
                            got = pe.transpose(ps[:, 7, t * P:(t + 1) * P], onehot[:, t, :], ident[:])
                        got.then_inc(aux_filled, 1)
                    if c == NC - 1:
                        gather(0, j * FILLS + 7, j + 2)
                    hidden(c, 1)
                    if c < 2:
                        back(2 * c + 1, j * FILLS + (3 + 2 * c), j + 1)
                    if c:
                        down(c - 1)
                turn(NC - 1)
                gather(1, j * FILLS + 8, j + 2)
                down(NC - 1)
            for n in range(4):
                back(n, items * FILLS + (2 + n), items + 1)


def rope_table():
    import numpy as np

    freq = np.float32(10000.0) ** (-np.arange(0, ROPE, 2, dtype=np.float32) / np.float32(ROPE))
    ang = np.arange(S, dtype=np.float32)[:, None] * freq[None, :]
    cos, sin = np.cos(ang), np.sin(ang)
    return np.stack([np.concatenate([cos, cos], 1), np.concatenate([-sin, sin], 1)], 1).astype(np.float32)


def kernel(**inputs):
    import numpy as np
    import concourse.bacc as bacc
    from concourse.bass_utils import run_bass_kernel_spmd

    f = {k: np.ascontiguousarray(v) for k, v in inputs.items()}
    rest = np.ones((1, ROPE + 32), np.float32)
    gains = np.concatenate([
        f["g_mix"][0].reshape(KD, P), f["g_ffn"][0].reshape(KD, P), f["kv_g_src"].reshape(KD, P),
        f["g_mix"][1].reshape(KD, P), f["g_ffn"][1].reshape(KD, P), f["kv_g_a"].reshape(2, P),
        f["mla_g_q_a"].reshape(3, P), np.concatenate([f["kv_g_k_nope"].reshape(1, HD), rest], 1),
        np.concatenate([f["mla_g_q_nope"].reshape(1, HD), rest], 1)]).T
    gpe = np.broadcast_to(np.stack([f["kv_g_k_pe"], f["mla_g_q_pe"][0]])[None], (P, 2, ROPE))
    arrays = {
        "x": f["x"][0], "gains": gains, "gpe": gpe, "rope": rope_table(), "g_ffn1": f["g_ffn"][1],
        "w_router": f["moe_w_router"][0], "b_router": f["moe_b_router"][0],
        "w_qkv": f["sb_w_qkv"][0], "w_sbo": f["sb_w_o"][0], "w_gate": f["ffn_w_gate"][0], "w_up": f["ffn_w_up"][0],
        "w_down": f["ffn_w_down"][0], "w_kva": f["kv_w_a"], "w_kvb": f["kv_w_b"], "w_qa": f["mla_w_q_a"][0],
        "w_qb": f["mla_w_q_b"][0], "w_mlo": f["mla_w_o"][0],
        "e_gate": f["moe_w_gate"][0], "e_up": f["moe_w_up"][0], "e_down": f["moe_w_down"][0],
    }
    arrays = {k: np.ascontiguousarray(v) for k, v in arrays.items()}
    nc = bacc.Bacc("TRN2", target_bir_lowering=False, num_devices=1)
    d = {k: nc.dram_tensor(k, a.shape, F32, kind="ExternalInput").ap() for k, a in arrays.items()}
    out = nc.dram_tensor("out", (S, D), F32, kind="ExternalOutput").ap()
    build(nc, d["x"], d["gains"], d["gpe"], d["rope"], d["g_ffn1"], d["w_router"], d["b_router"],
          {k[2:]: d[k] for k in d if k.startswith("w_") and k != "w_router"}, d["e_gate"], d["e_up"], d["e_down"], out)
    r = run_bass_kernel_spmd(nc, [arrays], core_ids=[0])
    return r.results[0]["out"].reshape(1, S, D)
```

```python
from contextlib import ExitStack

import concourse.bass as bass
from concourse import mybir

ALL = slice(None)
F32 = mybir.dt.float32
F32R = mybir.dt.float32r
I32 = mybir.dt.int32
U32 = mybir.dt.uint32
ALU = mybir.AluOpType
ACT = mybir.ActivationFunctionType
AXX = mybir.AxisListType.X

P = 128
D = 1024
S = 256
T = S // P
KD = D // P
HEADS = 16
HD = 64
ROPE = 32
QK = HD + ROPE
QH = 4
KH = 8
RQ = 384
RKV = 256
FD = 2816
FT = FD // P
FE = 3584
NE = 8
CH = 512
NC = FE // CH
EPS = 1e-6
FAR = 4096.0
OVER = S * 2 // (P + 1)
ITEMS = NE + OVER
FILLS = 7
NEG = -1e30

UNIT = 2048
RAW, HI, LO = 7, 3, 3

G_MIX0, G_FFN0, G_KV, G_MIX1, G_FFN1, G_KVA, G_QA, G_KN, G_QN = 0, 8, 16, 24, 32, 40, 42, 45, 46
NG = 47


def shape_unit(tile, n, *dims):
    names = "abcd"[:len(dims)]
    return tile[:, 0:n].rearrange(f"p ({' '.join(names)}) -> p {' '.join(names)}", **dict(zip(names, dims)))


def plan(w):
    out = []

    def rows(src, r0, n, c0, c1):
        return src[r0 * P:(r0 + n) * P, c0:c1].rearrange("(k p) n -> p k n", p=P)

    for c in range(6):
        for q in range(2):
            out.append(("qkv", (4, CH), rows(w["qkv"], 4 * q, 4, c * CH, c * CH + CH)))
    for q in range(4):
        out.append(("sbo", (2, D), rows(w["sbo"], 2 * q, 2, 0, D)))
    for c in range(5):
        for m in ("gate", "up"):
            for q in range(2):
                out.append((m, (4, CH), rows(w[m], 4 * q, 4, c * CH, c * CH + CH)))
    for q in range(2):
        out.append(("tail", (4, 2, 256), [rows(w[m], 4 * q, 4, 5 * CH, FD) for m in ("gate", "up")]))
    for q in range(FT // 2):
        out.append(("down", (2, D), rows(w["down"], 2 * q, 2, 0, D)))
    for q in range(2):
        out.append(("kva", (4, RKV + ROPE), rows(w["kva"], 4 * q, 4, 0, RKV + ROPE)))
    for q in range(2):
        out.append(("qa", (4, RQ), rows(w["qa"], 4 * q, 4, 0, RQ)))
    for q in range(2):
        out.append(("kvb", (2, D), rows(w["kvb"], 0, 2, q * D, q * D + D)))
    for q in range(HEADS // QH):
        out.append(("qb", (3, QH * QK), rows(w["qb"], 0, 3, q * QH * QK, (q + 1) * QH * QK)))
    for q in range(4):
        out.append(("mlo", (2, D), rows(w["mlo"], 2 * q, 2, 0, D)))
    return out


def expert_plan():
    out = []
    for c in range(NC):
        out += [("gate", c, 0), ("gate", c, 1), ("up", c, 0), ("up", c, 1)]
        if c:
            out += [("down", c - 1, 0), ("down", c - 1, 1)]
    return out + [("down", NC - 1, 0), ("down", NC - 1, 1)]


def build(nc, x_d, gains_d, gpe_d, rope_d, gffn1_d, wr_d, br_d, w, eg, eu, ed, out_d):
    pre = plan(w)
    NPRE = len(pre)
    first = {}
    for u, (name, _, _) in enumerate(pre):
        first.setdefault(name, u)
    item_units = expert_plan()
    NI = len(item_units)
    assert NI % RAW == 0 and NI % HI == 0 and NI % LO == 0

    with ExitStack() as ctx:
        base = (nc.sbuf_base + 63) // 64 * 64
        end = nc.sbuf_usable_end
        at = [base]

        def put(name, shape, dt=F32, off=None):
            n = 4
            for s in shape[1:]:
                n *= s
            n = (n + 31) // 32 * 32
            o = at[0] if off is None else off
            if off is None:
                at[0] += n
            assert o + n <= end, (name, o + n - end)
            return nc.alloc_sbuf_tensor_at(name, shape, dt, offset=o)

        def sem(name):
            return ctx.enter_context(nc.semaphore(name))

        raw = [put(f"raw{i}", [P, UNIT]) for i in range(RAW)]
        hi = [put(f"hi{i}", [P, UNIT], F32R) for i in range(HI)]
        lo = [put(f"lo{i}", [P, UNIT], F32R) for i in range(LO)]
        x = put("x", [P, T, D])
        xs = put("xs", [P, T, D])
        xTh = put("xTh", [P, KD, S], F32R)
        xTl = put("xTl", [P, KD, S], F32R)
        ident = put("ident", [P, P])
        ones = put("ones", [P, P])
        before = put("before", [P, P])
        ntri = put("ntri", [P, P])
        nones = put("nones", [P, P])
        gains = put("gains", [P, NG])
        gpe = put("gpe", [P, 2, ROPE])
        rope = put("rope", [P, T, 2, ROPE])
        wr = put("wr", [P, KD, NE])
        wrh = put("wrh", [P, KD, NE], F32R)
        wrl = put("wrl", [P, KD, NE], F32R)
        br = put("br", [P, NE])
        iota8 = put("iota8", [P, NE])
        eps = put("eps", [P, 1])
        one = put("one", [P, 1])
        ss = put("ss", [P, 8])
        rt = put("rt", [P, 8])
        rs = put("rs", [P, 8])
        hs = put("hs", [P, 6, 16])
        hr = put("hr", [P, 6, 16])
        hi_ = put("hrec", [P, 6, 16])
        ropeg = put("ropeg", [P, 2, T, 2, ROPE])
        swapped = put("swapped", [P, T, QH, ROPE])
        arena = (at[0] + 63) // 64 * 64

        def lay(*items):
            o, got = arena, []
            for name, shape, dt in items:
                got.append(put(name, shape, dt, off=o))
                n = 4
                for s in shape[1:]:
                    n *= s
                o += (n + 31) // 32 * 32
            return got

        qT, kT, v1, ab, ln_, spb, att = lay(
            ("qT", [P, KD, S], F32), ("kT", [P, KD, S], F32), ("v1", [P, T, D], F32),
            ("ab", [P, 4, 384], F32), ("ln", [P, 4, 384], F32), ("spb", [P, 4, 384], F32), ("att", [P, 4, 384], F32))
        fTh, fTl, sg, hm = lay(("fTh", [P, FT, S], F32R), ("fTl", [P, FT, S], F32R),
                               ("sg", [P, 4, S], F32), ("hm", [P, 4, S], F32))
        kf, q2, v2, kT2, qT2 = lay(
            ("kf", [P, T, HEADS, QK], F32), ("q2", [P, T, HEADS, QK], F32), ("v2", [P, T, HEADS, HD], F32),
            ("kT2", [P, HEADS, S], F32), ("qT2", [P, HEADS, S], F32))
        o = arena + 4 * (2 * T * HEADS * QK + T * HEADS * HD + HEADS * S)
        kva, qa = put("kva", [P, T, RKV + ROPE], off=o), put("qa", [P, T, RQ], off=o + 2304)
        cTh, cTl = put("cTh", [P, 2, S], F32R, off=o + 5376), put("cTl", [P, 2, S], F32R, off=o + 7424)
        aTh, aTl = put("aTh", [P, 3, S], F32R, off=o + 9472), put("aTl", [P, 3, S], F32R, off=o + 12544)
        o = arena + 4 * (2 * T * HEADS * QK + T * HEADS * HD)
        x2h, x2l = put("x2h", [P, KD, S], F32R, off=o), put("x2l", [P, KD, S], F32R, off=o + 4 * KD * S)
        mask, pm, pt, nm, sm, rc = lay(
            ("mask", [P, 384], F32), ("pm", [P, 4, 384], F32), ("pt", [P, 4, 384], F32),
            ("nm", [P, HEADS, 2], F32), ("sm", [P, HEADS, 2], F32), ("rc", [P, HEADS, 2], F32))
        (gbc, iota, onehot, ST, xgh, xgl, sl, hb, hTh, hTl, ysb, lg, mv, mi, ix, is1, is2, msk, gte, pex, ged,
         posm, cnt, rank, sel, slot, gt, ef, junk, tab) = lay(
            ("gbc", [P, D], F32), ("iota", [P, P], F32), ("onehot", [P, T, P], F32), ("ST", [P, S], F32),
            ("xgh", [P, KD, P], F32R), ("xgl", [P, KD, P], F32R), ("sl", [P, 2, CH], F32), ("hb", [P, 2, CH], F32),
            ("hTh", [P, 2, CH], F32R), ("hTl", [P, 2, CH], F32R), ("ysb", [P, D], F32),
            ("lg", [P, T, NE], F32), ("mv", [P, T, 8], F32), ("mi", [P, T, 8], U32), ("ix", [P, T, 8], F32),
            ("is1", [P, T, NE], F32), ("is2", [P, T, NE], F32), ("msk", [P, T, NE], F32), ("gte", [P, T, NE], F32),
            ("pex", [P, T], F32), ("ged", [P, T, 4], F32), ("posm", [P, T, NE], F32), ("cnt", [P, NE], F32),
            ("rank", [P, NE + 1], F32), ("sel", [P, OVER, NE], F32), ("slot", [P, T, ITEMS + 1], F32),
            ("gt", [P, T, ITEMS + 1], F32), ("ef", [P, 8], F32), ("junk", [P, NE], F32), ("tab", [P, 8], I32))

        ps = ctx.enter_context(nc.psum_tensor("ps", [P, 8, CH], F32))

        raw_landed = [sem(f"raw_landed{i}") for i in range(RAW)]
        hi_ready, lo_ready, units_used = sem("hi_ready"), sem("lo_ready"), sem("units_used")
        router_in, consts_in, ones_set, consts_ready = sem("router_in"), sem("consts_in"), sem("ones_set"), sem("consts_ready")
        x_in = [sem(f"x_in{t}") for t in range(T)]
        dve_done, act_done, pool_done = sem("dve_done"), sem("act_done"), sem("pool_done")
        sumsq_ready, squares_ready, rms_ready, xs_ready = sem("sumsq_ready"), sem("squares_ready"), sem("rms_ready"), sem("xs_ready")
        row0_ready, norm_root = sem("row0_ready"), sem("norm_root")
        xT_raw, xTh_ready, xT_ready = sem("xT_raw"), sem("xTh_ready"), sem("xT_ready")
        qkv_out = sem("qkv_out")
        z_ready, lnp_ready, sp_ready = sem("z_ready"), sem("lnp_ready"), sem("sp_ready")
        spm_ready, expo_ready, att_exp, att_ready = sem("spm_ready"), sem("expo_ready"), sem("att_exp"), sem("att_ready")
        oT_raw, oTh_ready, oT_ready = sem("oT_raw"), sem("oTh_ready"), sem("oT_ready")
        x_added = sem("x_added")
        silu_ready, h_ready, fTh_ready, fT_ready = (sem("silu_ready"), sem("h_ready"),
                                                              sem("fTh_ready"), sem("fT_ready"))
        low_squares, low_scaled, lowT_raw, lowTh_ready, lowT_ready = (
            sem("low_squares"), sem("low_scaled"), sem("lowT_raw"), sem("lowTh_ready"), sem("lowT_ready"))
        rope_ready, kpe_ready, v_out = sem("rope_ready"), sem("kpe_ready"), sem("v_out")
        heads_squared, k_normed, q_scaled, q_normed = sem("heads_squared"), sem("k_normed"), sem("q_scaled"), sem("q_normed")
        kqT_raw, qT_out, kT_out = sem("kqT_raw"), sem("qT_out"), sem("kT_out")
        sc_ready, max_ready, p_exp, p_ready = sem("sc_ready"), sem("max_ready"), sem("p_exp"), sem("p_ready")
        pT_raw, pT_ready, mask_ready = sem("pT_raw"), sem("pT_ready"), sem("mask_ready")
        logits_ready, wr_ready, gap_ready, gexp_ready = sem("logits_ready"), sem("wr_ready"), sem("gap_ready"), sem("gexp_ready")
        msk_ready, pos_ready, route_ready, gbc_in, iota_ready = (
            sem("msk_ready"), sem("pos_ready"), sem("route_ready"), sem("gbc_in"), sem("iota_ready"))
        onehot_ready, xgh_ready, aux_filled, aux_read = sem("onehot_ready"), sem("xgh_ready"), sem("aux_filled"), sem("aux_read")
        esilu_ready, eh_ready, ehT_raw, ehTh_ready, ehT_ready = (
            sem("esilu_ready"), sem("eh_ready"), sem("ehT_raw"), sem("ehTh_ready"), sem("ehT_ready"))
        ysb_ready, out_done = sem("ysb_ready"), sem("out_done")

        def size(dims):
            n = 1
            for s in dims:
                n *= s
            return n

        def unit_floats(i):
            return size(pre[i][1])

        def halves(u, kind=None):
            dims = pre[u][1] if kind is None else ((2, D) if kind == "down" else (4, CH))
            return [shape_unit(r[u % len(r)], size(dims), *dims) for r in (hi, lo)]

        norm_after = {1: first["sbo"] + 4, 2: first["down"], 3: first["kva"], 4: NPRE}

        def turned(n, b):
            return 4 * (n if n < 3 else n - 1) + b

        class Units:
            def __init__(self, one_unit):
                self.n, self.one_unit = 0, one_unit

            def until(self, n):
                while self.n < min(n, NPRE):
                    self.one_unit(self.n, self.n, unit_floats(self.n))
                    self.n += 1

        block = ctx.enter_context(nc.Block())

        @block.sync
        def _(sp):
            for t in range(T):
                sp.dma_start(x[:, t, :], x_d[t * P:(t + 1) * P, :]).then_inc(x_in[t], 16)
            for dst, src in ((gains[:], gains_d), (gpe[:], gpe_d), (rope[:], rope_d.rearrange("(t p) a r -> p t a r", p=P))):
                sp.dma_start(dst, src).then_inc(consts_in, 16)
            for u, (_, dims, src) in enumerate(pre):
                if u >= RAW:
                    sp.wait_ge(lo_ready, u - RAW + 1)
                dst = shape_unit(raw[u % RAW], size(dims), *dims)
                if isinstance(src, list):
                    for m, part in enumerate(src):
                        sp.dma_start(dst[:, :, m, :], part).then_inc(raw_landed[u % RAW], 16)
                else:
                    sp.dma_start(dst, src).then_inc(raw_landed[u % RAW], 16)

            def load_item(j, e):
                for i, (kind, c, q) in enumerate(item_units):
                    s = (NPRE + i) % RAW
                    sp.wait_ge(lo_ready, j * NI + (NPRE + i - RAW + 1))
                    if kind == "down":
                        r0 = c * CH + q * 2 * P
                        sp.dma_start(shape_unit(raw[s], UNIT, 2, D),
                                     ed[e, r0:r0 + 2 * P, :].rearrange("(p k) n -> p k n", k=2)
                                     ).then_inc(raw_landed[s], 16)
                    else:
                        src = eg if kind == "gate" else eu
                        sp.dma_start(shape_unit(raw[s], UNIT, 4, CH),
                                     src[e, q * 4 * P:(q + 1) * 4 * P, c * CH:(c + 1) * CH].rearrange(
                                         "(k p) n -> p k n", p=P)).then_inc(raw_landed[s], 16)

            with sp.Fori(0, NE) as j:
                load_item(j, j)
            sp.wait_ge(route_ready, 1)
            over = sp.value_load(tab[0:1, 1:2], min_val=0, max_val=OVER)
            with sp.If(over > 0):
                with sp.Fori(0, over) as r:
                    e = sp.value_load(tab[0:1, bass.ds(r + 2, 1)], min_val=0, max_val=NE - 1)
                    load_item(r + NE, e)

            sp.wait_ge(aux_read, over * FILLS + (NE * FILLS + 6))
            for t in range(T):
                sp.dma_start(out_d[t * P:(t + 1) * P, :], x[:, t, :]).then_inc(out_done, 16)
            sp.wait_ge(out_done, 16 * T)

        def landed(eng, u, j=None):
            s = u % RAW
            tails = sum(pre[v][0] == "tail" for v in range(s, min(u + 1, NPRE), RAW))
            uses = 16 * (u // RAW + 1 + tails)
            eng.wait_ge(raw_landed[s], uses if j is None else j * (16 * NI // RAW) + uses)

        @block.scalar
        def _(act):
            for dst, src in ((wr[:], wr_d.rearrange("(k p) e -> p k e", p=P)), (br[:], br_d.partition_broadcast(P))):
                act.dma_start(dst, src).then_inc(router_in, 16)

            def round_unit(u, n, floats, j=None):
                landed(act, n, j)
                if j is None and u >= HI:
                    act.wait_ge(units_used, u - HI + 1)
                elif j is not None:
                    act.wait_ge(units_used, j * NI + (n - HI + 1))
                act.activation(hi[n % HI][:, 0:floats], raw[n % RAW][:, 0:floats], ACT.Copy).then_inc(hi_ready, 1)

            units = Units(round_unit)

            def mean_squares(n):
                for t in range(T):
                    k = T * (n - (n > 2)) + t
                    if n:
                        act.wait_ge(x_added, k - T + 1)
                        act.wait_ge(xT_raw, turned(n, 0))
                    else:
                        act.wait_ge(x_in[t], 16)
                    act.activation(xs[:, t, :], x[:, t, :], ACT.Square, scale=D ** -0.5,
                                   accum_out=ss[:, t:t + 1]).then_inc(squares_ready, 1)
                    act.wait_ge(squares_ready, k + 1)
                    act.activation(rt[:, t:t + 1], ss[:, t:t + 1], ACT.Sqrt, bias=eps[:]).then_inc(norm_root, 1)

            def norm_transposed(n, g):
                dst = x2h if n == 3 else xTh
                for b in range(4):
                    if n != 3:
                        act.wait_ge(xT_raw, turned(n, b + 1))
                    else:
                        act.wait_ge(xT_ready, 4 * 2 + b + 1)
                    if n:
                        act.wait_ge(units_used, norm_after[n])
                    for k in (2 * b, 2 * b + 1):
                        got = act.activation(dst[:, k, :], ps[:, 4 + b, (k % 2) * S:(k % 2 + 1) * S], ACT.Copy,
                                             scale=gains[:, g + k:g + k + 1])
                    got.then_inc(xTh_ready, 1)

            act.wait_ge(consts_ready, 1)
            mean_squares(0)
            act.wait_ge(consts_in, 16 * 3)
            units.until(3)
            norm_transposed(0, G_MIX0)
            for c in range(6):
                units.until(2 * c + 5)
                act.wait_ge(units_used, first["qkv"] + 2 * c + 2)
                b = 4 * (c % 2)
                if c < 4:
                    dst = (qT if c < 2 else kT)[:, 4 * (c % 2):4 * (c % 2) + 4, :]
                    act.activation(dst, ps[:, b:b + 4, 0:S], ACT.Copy, scale=HD ** -0.5 if c < 2 else 1.0).then_inc(qkv_out, 1)
                else:
                    act.activation(v1[:, :, (c - 4) * CH:(c - 3) * CH], ps[:, b:b + T, :], ACT.Copy).then_inc(qkv_out, 1)

            def log_part(h):
                act.wait_ge(z_ready, h + 1)
                act.activation(ab[:, h % 4, :], ps[:, h % 4, 0:384], ACT.Abs).then_inc(act_done, 1)
                act.wait_ge(act_done, 2 * h + 1)
                act.activation(ln_[:, h % 4, :], ab[:, h % 4, :], ACT.Exp, scale=-1.0).then_inc(act_done, 1)
                act.wait_ge(act_done, 2 * h + 2)
                act.activation(ln_[:, h % 4, :], ln_[:, h % 4, :], ACT.Ln, bias=one[:]).then_inc(lnp_ready, 1)

            def att_part(h):
                act.wait_ge(expo_ready, h + 1)
                act.activation(att[:, h % 4, :], ps[:, h % 4, 0:384], ACT.Exp).then_inc(att_exp, 1)

            def head_out(layer, p):
                act.wait_ge(oT_raw, 8 * layer + p + 1)
                act.activation(xTh[:, p, :], ps[:, 4 + p % 2, 0:S], ACT.Copy).then_inc(oTh_ready, 1)

            for i in range(HEADS + 4):
                if i < HEADS:
                    log_part(i)
                if 2 <= i < HEADS + 2:
                    att_part(i - 2)
                if i >= 5 and i % 2 == 1:
                    head_out(0, (i - 5) // 2)
            units.until(first["gate"] + 2)
            mean_squares(1)
            units.until(first["gate"] + 3)
            norm_transposed(1, G_FFN0)
            for c in range(6):
                nt = 4 if c < 5 else 2
                last = first["gate"] + 4 * c + (3 if c < 5 else 1)
                units.until(last + 4)
                act.wait_ge(units_used, last + 1)
                if c:
                    act.wait_ge(h_ready, c)
                b = 4 * (c % 2)
                act.activation(sg[:, 0:nt, :], ps[:, b:b + nt, 0:S], ACT.Silu).then_inc(silu_ready, 1)
                act.wait_ge(h_ready, c + 1)
                act.activation(fTh[:, 4 * c:4 * c + nt, :], hm[:, 0:nt, :], ACT.Copy).then_inc(fTh_ready, 1)
            units.until(first["down"] + 11 + 2)
            mean_squares(2)
            units.until(first["down"] + 11 + 3)
            norm_transposed(2, G_KV)
            norm_transposed(3, G_MIX1)
            sq = xs[:].rearrange("p t d -> p (t d)")

            def low_roots(done, parts):
                for bank, cols, col, place in parts:
                    n = cols.stop - cols.start
                    act.activation(sq[:, place:place + n], ps[:, bank, cols], ACT.Square, scale=n ** -0.5,
                                   accum_out=ss[:, col:col + 1]).then_inc(low_squares, 1)
                act.wait_ge(low_squares, done + len(parts))
                a, b = parts[0][2], parts[-1][2] + 1
                act.activation(rt[:, a:b], ss[:, a:b], ACT.Sqrt, bias=eps[:]).then_inc(rms_ready, 1)

            def low_hi(k_tiles, dst, g, bank, n):
                act.wait_ge(lowT_raw, n)
                for k in range(k_tiles):
                    got = act.activation(dst[:, k, :], ps[:, bank + k // 2, (k % 2) * S:(k % 2 + 1) * S], ACT.Copy,
                                         scale=gains[:, g + k:g + k + 1])
                got.then_inc(lowTh_ready, 1)

            def heads_square(i, src, n):
                act.activation(sq[:, (i % 2) * D:(i % 2) * D + n], src, ACT.Square).then_inc(heads_squared, 1)

            def heads_root(i, parts):
                act.wait_ge(sumsq_ready, i + 1)
                for a, b, dim in parts:
                    got = act.activation(hr[:, i, a:b], hs[:, i, a:b], ACT.Sqrt, bias=eps[:], scale=1.0 / dim)
                got.then_inc(rms_ready, 1)

            units.until(first["kva"] + 4)
            act.wait_ge(units_used, first["kva"] + 2)
            low_roots(0, [(0, slice(0, RKV), 2, 0), (1, slice(0, RKV), 3, RKV),
                          (0, slice(RKV, RKV + ROPE), 4, 2 * RKV), (1, slice(RKV, RKV + ROPE), 5, 2 * RKV + ROPE)])
            units.until(first["kva"] + 5)
            low_hi(2, cTh, G_KVA, 0, 1)
            units.until(first["qa"] + 4)
            act.wait_ge(units_used, first["qa"] + 2)
            low_roots(4, [(2, slice(0, RQ), 6, D), (3, slice(0, RQ), 7, D + RQ)])
            units.until(first["qa"] + 5)
            low_hi(3, aTh, G_QA, 2, 2)
            for q in range(2):
                act.wait_ge(units_used, first["kvb"] + q + 1)
                b = 4 if q == 0 else 0
                heads = ps[:, b:b + 4, :].rearrange("p b (h d) -> p b h d", h=4)
                heads_square(q, heads[:, :, :, 0:HD], 4 * 4 * HD)
                for n in range(2):
                    hh = slice(KH * q + 4 * n, KH * q + 4 * n + 4)
                    got = act.activation(v2[:, :, hh, :], heads[:, 2 * n:2 * n + 2, :, HD:2 * HD], ACT.Copy)
                got.then_inc(v_out, 1)
                heads_root(q, [(0, 16, HD)])
                units.until(first["kvb"] + q + 4)

            def k_out(g):
                act.wait_ge(kqT_raw, g + 1)
                act.activation(kT2[0:QK, 2 * g:2 * g + 2, :], ps[0:QK, g % 4, :].rearrange("p (h s) -> p h s", h=2),
                               ACT.Copy, scale=gains[0:QK, G_KN:G_KN + 1]).then_inc(kT_out, 1)

            for q in range(HEADS // QH):
                act.wait_ge(units_used, first["qb"] + q + 1)
                b = 4 + 2 * (q % 2)
                heads_square(2 + q, ps[:, b:b + T, 0:QH * QK], T * QH * QK)
                units.until(first["qb"] + q + 4)
                heads_root(2 + q, [(0, 8, HD), (8, 16, ROPE)])
                if q % 2:
                    for g in range(2 * (q - 1), 2 * (q - 1) + 4):
                        k_out(g)

            def p_part(h):
                act.wait_ge(max_ready, h + 1)
                act.activation(pm[:, h % 4, 0:P], pm[:, h % 4, 0:P], ACT.Exp, scale=-1.0, bias=nm[:, h, 0:1],
                               accum_out=sm[:, h, 0:1]).then_inc(p_exp, 1)
                act.activation(pm[:, h % 4, P:384], pm[:, h % 4, P:384], ACT.Exp, scale=-1.0, bias=nm[:, h, 1:2],
                               accum_out=sm[:, h, 1:2]).then_inc(p_exp, 1)

            def pt_part(h):
                act.wait_ge(pT_raw, h + 1)
                act.activation(pt[:, h % 4, :], ps[:, 6 + h % 2, 0:384], ACT.Copy).then_inc(pT_ready, 1)

            for i in range(HEADS + 4):
                if i < HEADS:
                    p_part(i)
                if 2 <= i < HEADS + 2:
                    pt_part(i - 2)
                if i >= 5 and i % 2 == 1:
                    head_out(1, (i - 5) // 2)
            units.until(NPRE)
            mean_squares(4)
            act.dma_start(gbc[:], gffn1_d.partition_broadcast(P)).then_inc(gbc_in, 16)
            norm_transposed(4, G_FFN1)
            act.wait_ge(gap_ready, 1)
            act.activation(pex[:], ged[:, :, 0], ACT.Exp).then_inc(gexp_ready, 1)
            act.wait_ge(route_ready, 1)
            items = act.value_load(tab[0:1, 0:1], min_val=NE, max_val=ITEMS)
            def gather_hi(half, fill, n, j):
                act.wait_ge(aux_filled, fill)
                if n is not None:
                    act.wait_ge(units_used, n)
                act.activation(xgh[:, 4 * half:4 * half + 4, :], ps[:, 7, :].rearrange("p (k s) -> p k s", s=P),
                               ACT.Copy).then_inc(xgh_ready, 1)

            def take_y(n):
                act.wait_ge(units_used, n)
                act.activation(ysb[:], ps[:, 4:6, :].rearrange("p b n -> p (b n)"), ACT.Copy).then_inc(ysb_ready, 1)

            for half in range(2):
                gather_hi(half, half + 1, None, None)
            with act.Fori(0, items) as j:
                done = [0]

                def item_until(n):
                    while done[0] < n:
                        round_unit(None, NPRE + done[0], UNIT, j)
                        done[0] += 1

                def h_hi(c):
                    act.wait_ge(ehT_raw, j * NC + (c + 1))
                    act.activation(hTh[:, c % 2, :], ps[:, 6, :], ACT.Copy).then_inc(ehTh_ready, 1)

                item_until(2)
                take_y(j * NI + NPRE)
                for c in range(NC):
                    if c:
                        item_until(6 * c + 2)
                        h_hi(c - 1)
                    item_until(6 * c + 4 if c else 6)
                    act.wait_ge(units_used, j * NI + (NPRE + (6 * c + 2 if c else 4)))
                    act.wait_ge(eh_ready, j * NC + max(c, 1))
                    act.activation(sl[:, c % 2, :], ps[:, 2 * (c % 2), :], ACT.Silu).then_inc(esilu_ready, 1)
                gather_hi(0, j * FILLS + 8, j * NI + (NPRE + 38), j)
                item_until(NI)
                h_hi(NC - 1)
                gather_hi(1, j * FILLS + 9, None, j)
            take_y(items * NI + NPRE)

        @block.vector
        def _(dve):
            steps = [0]

            def after(ins):
                steps[0] += 1
                ins.then_inc(dve_done, 1)
                dve.wait_ge(dve_done, steps[0])

            def subtract_unit(u, n, floats, j=None):
                dve.wait_ge(hi_ready, n + 1 if j is None else j * NI + (n + 1))
                dve.tensor_tensor(lo[n % LO][:, 0:floats], raw[n % RAW][:, 0:floats],
                                  hi[n % HI][:, 0:floats].bitcast(F32), ALU.subtract).then_inc(lo_ready, 1)

            units = Units(subtract_unit)

            def normalise(n):
                for t in range(T):
                    dve.wait_ge(norm_root, T * (n - (n > 2)) + t + 1)
                    after(dve.reciprocal(rs[:, t:t + 1], rt[:, t:t + 1]))
                    dve.tensor_scalar(xs[:, t, :], x[:, t, :], rs[:, t:t + 1], None, ALU.mult).then_inc(xs_ready, 1)

            def norm_transposed(n, g):
                h, l = (x2h, x2l) if n == 3 else (xTh, xTl)
                for b in range(4):
                    dve.wait_ge(xTh_ready, 4 * n + b + 1)
                    for k in (2 * b, 2 * b + 1):
                        got = dve.scalar_tensor_tensor(
                            out=l[:, k, :], in0=ps[:, 4 + b, (k % 2) * S:(k % 2 + 1) * S], scalar=gains[:, g + k:g + k + 1],
                            in1=h[:, k, :].bitcast(F32), op0=ALU.mult, op1=ALU.subtract)
                    got.then_inc(xT_ready, 1)

            def add_projection(n, name, count):
                for t in range(T):
                    if t == 0:
                        dve.wait_ge(row0_ready, n + 1)
                    else:
                        dve.wait_ge(units_used, first[name] + count)
                    dve.tensor_tensor(x[:, t, :], x[:, t, :], ps[:, 2 * t:2 * t + 2, :].rearrange("p b n -> p (b n)"),
                                      ALU.add).then_inc(x_added, 1)

            normalise(0)
            units.until(3)
            dve.wait_ge(consts_in, 16 * 3)
            norm_transposed(0, G_MIX0)
            for c in range(6):
                units.until(2 * c + 5)

            dve.wait_ge(router_in, 16 * 2)
            dve.tensor_copy(wrh[:], wr[:]).then_inc(wr_ready, 1)
            dve.wait_ge(wr_ready, 1)
            dve.tensor_tensor(wrl[:], wr[:], wrh[:].bitcast(F32), ALU.subtract).then_inc(wr_ready, 1)

            def softplus_part(h):
                dve.wait_ge(lnp_ready, h + 1)
                dve.scalar_tensor_tensor(out=spb[:, h % 4, :], in0=ps[:, h % 4, 0:384], scalar=0.0, in1=ln_[:, h % 4, :],
                                         op0=ALU.max, op1=ALU.add).then_inc(sp_ready, 1)

            def head_out(layer, p):
                dve.wait_ge(oTh_ready, 8 * layer + p + 1)
                dve.tensor_tensor(xTl[:, p, :], ps[:, 4 + p % 2, 0:S], xTh[:, p, :].bitcast(F32),
                                  ALU.subtract).then_inc(oT_ready, 1)

            for i in range(HEADS + 4):
                if i < HEADS:
                    softplus_part(i)
                if i >= 5 and i % 2 == 1:
                    head_out(0, (i - 5) // 2)
            units.until(first["gate"] + 2)
            add_projection(0, "sbo", 4)
            normalise(1)
            units.until(first["gate"] + 3)
            norm_transposed(1, G_FFN0)
            for c in range(6):
                nt = 4 if c < 5 else 2
                last = first["gate"] + 4 * c + (3 if c < 5 else 1)
                units.until(last + 4)
                dve.wait_ge(silu_ready, c + 1)
                if c:
                    dve.wait_ge(fT_ready, c)
                b = 4 * (c % 2)
                dve.tensor_tensor(hm[:, 0:nt, :], sg[:, 0:nt, :], ps[:, b:b + nt, S:2 * S], ALU.mult).then_inc(h_ready, 1)
                dve.wait_ge(fTh_ready, c + 1)
                dve.tensor_tensor(fTl[:, 4 * c:4 * c + nt, :], hm[:, 0:nt, :], fTh[:, 4 * c:4 * c + nt, :].bitcast(F32),
                                  ALU.subtract).then_inc(fT_ready, 1)
            units.until(first["down"] + 11 + 2)
            add_projection(1, "down", 11)
            normalise(2)
            units.until(first["down"] + 11 + 3)
            norm_transposed(2, G_KV)
            norm_transposed(3, G_MIX1)
            sq = xs[:].rearrange("p t d -> p (t d)")

            def low_reciprocal(a, b, n):
                dve.wait_ge(rms_ready, n)
                after(dve.reciprocal(rs[:, a:b], rt[:, a:b]))

            def low_lo(k_tiles, h, l, g, bank, n):
                dve.wait_ge(lowTh_ready, n)
                for k in range(k_tiles):
                    got = dve.scalar_tensor_tensor(out=l[:, k, :], in0=ps[:, bank + k // 2, (k % 2) * S:(k % 2 + 1) * S],
                                                   scalar=gains[:, g + k:g + k + 1], in1=h[:, k, :].bitcast(F32),
                                                   op0=ALU.mult, op1=ALU.subtract)
                got.then_inc(lowT_ready, 1)

            def heads_reciprocal(i):
                dve.wait_ge(rms_ready, 3 + i)
                after(dve.reciprocal(hi_[:, i, :], hr[:, i, :]))

            units.until(first["kva"] + 4)
            low_reciprocal(2, 6, 1)
            for t in range(T):
                dve.tensor_scalar(kva[:, t, 0:RKV], ps[:, t, 0:RKV], rs[:, 2 + t:3 + t], None, ALU.mult)
                dve.tensor_scalar(kva[:, t, RKV:RKV + ROPE], ps[:, t, RKV:RKV + ROPE], rs[:, 4 + t:5 + t], None,
                                  ALU.mult).then_inc(low_scaled, 1)
            units.until(first["kva"] + 5)
            low_lo(2, cTh, cTl, G_KVA, 0, 1)
            units.until(first["qa"] + 4)
            low_reciprocal(6, 8, 2)
            for t in range(T):
                dve.tensor_scalar(qa[:, t, :], ps[:, 2 + t, 0:RQ], rs[:, 6 + t:7 + t], None, ALU.mult).then_inc(low_scaled, 1)
            units.until(first["qa"] + 5)
            low_lo(3, aTh, aTl, G_QA, 2, 2)
            for q in range(2):
                b = 4 if q == 0 else 0
                dve.wait_ge(heads_squared, q + 1)
                dve.tensor_reduce(hs[:, q, :], sq[:, q * D:q * D + 16 * HD].rearrange("p (h d) -> p h d", d=HD), AXX,
                                  ALU.add).then_inc(sumsq_ready, 1)
                heads_reciprocal(q)
                heads = ps[:, b:b + 4, :].rearrange("p b (h d) -> p b h d", h=4)
                for n in range(2):
                    got = dve.tensor_tensor(
                        kf[:, :, KH * q + 4 * n:KH * q + 4 * n + 4, 0:HD], heads[:, 2 * n:2 * n + 2, :, 0:HD],
                        hi_[:, q, 8 * n:8 * n + 8].rearrange("p (t h) -> p t h", t=T).unsqueeze(3).to_broadcast([P, T, 4, HD]),
                        ALU.mult)
                got.then_inc(k_normed, 1)
                units.until(first["kvb"] + q + 4)
            for q in range(HEADS // QH):
                b = 4 + 2 * (q % 2)
                i = 2 + q
                dve.wait_ge(heads_squared, i + 1)
                squares = sq[:, (i % 2) * D:(i % 2) * D + T * QH * QK].rearrange("p (h d) -> p h d", d=QK)
                dve.tensor_reduce(hs[:, i, 0:8], squares[:, :, 0:HD], AXX, ALU.add)
                dve.tensor_reduce(hs[:, i, 8:16], squares[:, :, HD:QK], AXX, ALU.add).then_inc(sumsq_ready, 1)
                units.until(first["qb"] + q + 3)
                heads_reciprocal(i)
                heads = ps[:, b:b + T, 0:QH * QK].rearrange("p t (h d) -> p t h d", h=QH)
                for part, (c0, c1) in ((1, (HD, QK)), (0, (0, HD))):
                    got = dve.tensor_tensor(
                        q2[:, :, QH * q:QH * q + QH, c0:c1], heads[:, :, :, c0:c1],
                        hi_[:, i, 8 * part:8 * part + 8].rearrange("p (t h) -> p t h", t=T).unsqueeze(3).to_broadcast(
                            [P, T, QH, c1 - c0]), ALU.mult)
                    got.then_inc(q_scaled, 1)
            units.until(first["qb"] + 6)
            for g in range(8):
                dve.wait_ge(kqT_raw, 8 + g + 1)
                dve.tensor_scalar(qT2[0:QK, 2 * g:2 * g + 2, :],
                                  ps[0:QK, 4 + g % 4, :].rearrange("p (h s) -> p h s", h=2),
                                  gains[0:QK, G_QN:G_QN + 1], None, ALU.mult).then_inc(qT_out, 1)
            dve.wait_ge(mask_ready, 1)

            def max_part(h):
                dve.wait_ge(sc_ready, h + 1)
                for n, cols in enumerate((slice(0, P), slice(P, 384))):
                    got = dve.tensor_tensor_reduce(pm[:, h % 4, cols], ps[:, h % 4, cols], mask[:, cols],
                                                   -float(QK) ** -0.5, 3e38, ALU.add, ALU.min, nm[:, h, n:n + 1])
                got.then_inc(max_ready, 1)

            def share_part(h):
                dve.wait_ge(p_exp, 2 * h + 2)
                after(dve.reciprocal(rc[:, h, :], sm[:, h, :]))
                dve.tensor_scalar(pm[:, h % 4, 0:P], pm[:, h % 4, 0:P], rc[:, h, 0:1], None, ALU.mult).then_inc(p_ready, 1)
                dve.tensor_scalar(pm[:, h % 4, P:384], pm[:, h % 4, P:384], rc[:, h, 1:2], None,
                                  ALU.mult).then_inc(p_ready, 1)

            for i in range(HEADS + 4):
                if i < HEADS:
                    max_part(i)
                if 1 <= i < HEADS + 1:
                    share_part(i - 1)
                if i >= 5 and i % 2 == 1:
                    head_out(1, (i - 5) // 2)
            units.until(NPRE)
            add_projection(2, "mlo", 4)
            normalise(4)
            norm_transposed(4, G_FFN1)
            dve.wait_ge(xT_raw, turned(4, 4))
            dve.wait_ge(gbc_in, 16)
            for t in range(T):
                dve.tensor_tensor(xs[:, t, :], xs[:, t, :], gbc[:], ALU.mult)
            dve.wait_ge(logits_ready, 1)
            dve.wait_ge(iota_ready, 1)
            after(dve.tensor_tensor(lg[:], ps[:, 0, 0:T * NE].rearrange("p (t e) -> p t e", t=T),
                                    br[:].unsqueeze(1).to_broadcast([P, T, NE]), ALU.add))
            for t in range(T):
                after(dve.max(mv[:, t, :], lg[:, t, :]))
                after(dve.max_index(mi[:, t, :], mv[:, t, :], lg[:, t, :]))
            dve.tensor_tensor(ged[:, :, 0], mv[:, :, 1], mv[:, :, 0], ALU.subtract).then_inc(gap_ready, 1)
            after(dve.tensor_copy(ix[:], mi[:]))
            for t in range(T):
                dve.tensor_scalar(is1[:, t, :], iota8[:], ix[:, t, 0:1], None, ALU.is_equal)
                after(dve.tensor_scalar(is2[:, t, :], iota8[:], ix[:, t, 1:2], None, ALU.is_equal))
            dve.tensor_tensor(msk[:], is1[:], is2[:], ALU.add).then_inc(msk_ready, 1)
            dve.wait_ge(gexp_ready, 1)
            after(dve.tensor_scalar(ged[:, :, 1], pex[:], 1.0, None, ALU.add))
            after(dve.reciprocal(ged[:, :, 2], ged[:, :, 1]))
            after(dve.tensor_tensor(ged[:, :, 3], ged[:, :, 2], pex[:], ALU.mult))
            for t in range(T):
                after(dve.tensor_scalar(gte[:, t, :], is1[:, t, :], ged[:, t, 2:3], None, ALU.mult))
                after(dve.scalar_tensor_tensor(out=gte[:, t, :], in0=is2[:, t, :], scalar=ged[:, t, 3:4], in1=gte[:, t, :],
                                               op0=ALU.mult, op1=ALU.add))
            dve.wait_ge(pos_ready, 1)
            for t in range(T):
                after(dve.scalar_tensor_tensor(out=posm[:, t, :], in0=msk[:, t, :], scalar=-FAR,
                                               in1=ps[:, 1, t * NE:(t + 1) * NE], op0=ALU.mult, op1=ALU.add))
                after(dve.tensor_scalar(posm[:, t, :], posm[:, t, :], FAR, None, ALU.add))
            after(dve.tensor_scalar(cnt[:], ps[:, 1, 2 * NE:3 * NE], float(P), None, ALU.is_gt))
            after(dve.memset(rank[:], 0.0))
            for e in range(NE):
                after(dve.tensor_tensor(rank[:, e + 1:e + 2], rank[:, e:e + 1], cnt[:, e:e + 1], ALU.add))
            for r in range(OVER):
                after(dve.scalar_tensor_tensor(out=sel[:, r, :], in0=rank[:, 0:NE], scalar=float(r), in1=cnt[:],
                                               op0=ALU.is_equal, op1=ALU.mult))
            after(dve.tensor_copy(slot[:, :, 0:NE], posm[:]))
            after(dve.memset(slot[:, :, ITEMS:], -1.0))
            after(dve.memset(gt[:, :, 0:1], 0.0))
            after(dve.memset(ST[:], 0.0))
            after(dve.tensor_copy(gt[:, :, 1:NE + 1], gte[:]))
            for r in range(OVER):
                for t in range(T):
                    after(dve.tensor_tensor_reduce(junk[:], posm[:, t, :], sel[:, r, :], 1.0, -float(P), ALU.mult, ALU.add,
                                                   slot[:, t, NE + r:NE + r + 1]))
                    after(dve.tensor_tensor_reduce(junk[:], gte[:, t, :], sel[:, r, :], 1.0, 0.0, ALU.mult, ALU.add,
                                                   gt[:, t, NE + r + 1:NE + r + 2]))
                after(dve.tensor_tensor_reduce(junk[:], iota8[:], sel[:, r, :], 1.0, 0.0, ALU.mult, ALU.add,
                                               ef[:, 2 + r:3 + r]))
            after(dve.tensor_copy(ef[:, 1:2], rank[:, NE:NE + 1]))
            after(dve.tensor_scalar(ef[:, 0:1], rank[:, NE:NE + 1], float(NE), None, ALU.add))
            dve.tensor_copy(tab[:, 0:2 + OVER], ef[:, 0:2 + OVER]).then_inc(route_ready, 1)
            dve.wait_ge(route_ready, 1)
            items = dve.value_load(tab[0:1, 0:1], min_val=NE, max_val=ITEMS)
            for counts_from_one in (eh_ready, ehT_ready):
                dve.nop().then_inc(counts_from_one, 1)

            def build_onehot(col):
                for t in range(T):
                    got = dve.tensor_scalar(onehot[:, t, :], iota[:], slot[:, t, col], None, ALU.is_equal)
                got.then_inc(onehot_ready, 1)

            def gather_lo(half, ready, fill):
                dve.wait_ge(xgh_ready, ready)
                dve.tensor_tensor(xgl[:, 4 * half:4 * half + 4, :], ps[:, 7, :].rearrange("p (k s) -> p k s", s=P),
                                  xgh[:, 4 * half:4 * half + 4, :].bitcast(F32), ALU.subtract).then_inc(aux_read, 1)

            def add_back(n, fill, col):
                t, half = n // 2, n % 2
                dve.wait_ge(aux_filled, fill)
                xo = x[:, t, half * CH:(half + 1) * CH]
                dve.scalar_tensor_tensor(out=xo, in0=ps[:, 7, :], scalar=gt[:, t, col], in1=xo,
                                         op0=ALU.mult, op1=ALU.add).then_inc(aux_read, 1)

            build_onehot(slice(0, 1))
            for half in range(2):
                gather_lo(half, half + 1, half + 1)
            with dve.Fori(0, items) as j:
                done = [0]

                def item_until(n):
                    while done[0] < n:
                        subtract_unit(None, NPRE + done[0], UNIT, j)
                        done[0] += 1

                def h_lo(c):
                    dve.wait_ge(ehTh_ready, j * NC + (c + 1))
                    dve.tensor_tensor(hTl[:, c % 2, :], ps[:, 6, :], hTh[:, c % 2, :].bitcast(F32),
                                      ALU.subtract).then_inc(ehT_ready, 1)

                for c in range(NC):
                    if c:
                        item_until(6 * c + 2)
                        h_lo(c - 1)
                    else:
                        item_until(4)
                    if c < 2:
                        add_back(2 * c, j * FILLS + (3 + 2 * c), bass.ds(j, 1))
                    if c == 2:
                        dve.wait_ge(aux_filled, j * FILLS + 7)
                        dve.tensor_copy(ST[:], ps[:, 7, 0:S]).then_inc(aux_read, 1)
                        build_onehot(bass.ds(j + 1, 1))
                    item_until(6 * c + 4 if c else 6)
                    dve.wait_ge(esilu_ready, j * NC + (c + 1))
                    dve.tensor_tensor(hb[:, c % 2, :], sl[:, c % 2, :], ps[:, 2 * (c % 2) + 1, :], ALU.mult).then_inc(eh_ready, 1)
                    if c < 2:
                        add_back(2 * c + 1, j * FILLS + (4 + 2 * c), bass.ds(j, 1))
                gather_lo(0, j * 2 + 3, None)
                item_until(NI)
                h_lo(NC - 1)
                gather_lo(1, j * 2 + 4, None)
            for n in range(4):
                add_back(n, items * FILLS + (3 + n), bass.ds(items, 1))

        @block.gpsimd
        def _(pool):
            for tile, value in ((ident, 0.0), (ones, 1.0), (before, 1.0), (ntri, -1.0), (nones, -1.0), (eps, EPS), (one, 1.0)):
                pool.memset(tile[:], value).then_inc(ones_set, 1)
            pool.wait_ge(ones_set, 7)
            pool.affine_select(out=ident[:], in_=ident[:], compare_op=ALU.not_equal, fill=1.0, base=0,
                               pattern=[[-1, P]], channel_multiplier=1)
            pool.affine_select(out=before[:], in_=before[:], compare_op=ALU.is_gt, fill=0.0, base=0,
                               pattern=[[1, P]], channel_multiplier=-1)
            pool.iota(iota8[:], pattern=[[1, NE]], base=0, channel_multiplier=0, allow_small_or_imprecise_dtypes=True)
            pool.affine_select(out=ntri[:], in_=ntri[:], compare_op=ALU.is_ge, fill=0.0, base=0,
                               pattern=[[-1, P]], channel_multiplier=1).then_inc(consts_ready, 1)

            steps = [0]

            def after(ins):
                steps[0] += 1
                ins.then_inc(pool_done, 1)
                pool.wait_ge(pool_done, steps[0])

            pool.wait_ge(consts_in, 16 * 3)
            half = ROPE // 2
            for m in range(2):
                for t in range(T):
                    pool.tensor_tensor(ropeg[:, m, t, 0, :], rope[:, t, 0, :], gpe[:, m, :], ALU.mult)
                    pool.tensor_tensor(ropeg[:, m, t, 1, 0:half], rope[:, t, 1, 0:half], gpe[:, m, half:ROPE], ALU.mult)
                    got = pool.tensor_tensor(ropeg[:, m, t, 1, half:ROPE], rope[:, t, 1, half:ROPE], gpe[:, m, 0:half], ALU.mult)
            got.then_inc(rope_ready, 1)

            def rotate(v, other, m):
                n = v.shape[2]

                def factor(which, a, b):
                    return ropeg[:, m, :, which, a:b].unsqueeze(2).to_broadcast([P, T, n, b - a])

                pool.tensor_tensor(other[:, :, :, 0:half], v[:, :, :, half:ROPE], factor(1, 0, half), ALU.mult)
                after(pool.tensor_tensor(other[:, :, :, half:ROPE], v[:, :, :, 0:half], factor(1, half, ROPE), ALU.mult))
                after(pool.tensor_tensor(v, v, factor(0, 0, ROPE), ALU.mult))
                return pool.tensor_tensor(v, v, other, ALU.add)

            def diagonal(tile):
                v = tile.rearrange("p (b n) -> p b n", b=3)[:, 0:3:2, :]
                return pool.affine_select(out=v, in_=v, compare_op=ALU.is_gt, fill=0.0, base=0,
                                          pattern=[[0, 2], [1, P]], channel_multiplier=-1)

            for i in range(HEADS + 2):
                if i < HEADS:
                    pool.wait_ge(sp_ready, i + 1)
                    diagonal(spb[:, i % 4, :]).then_inc(spm_ready, 1)
                if i >= 2:
                    pool.wait_ge(att_exp, i - 1)
                    diagonal(att[:, (i - 2) % 4, :]).then_inc(att_ready, 1)
            pool.wait_ge(rope_ready, 1)
            pool.wait_ge(low_scaled, 2)
            kpe = kva[:, :, RKV:RKV + ROPE].unsqueeze(2)
            after(rotate(kpe, swapped[:, :, 0:1, :], 0))
            pool.tensor_copy(kf[:, :, :, HD:QK], kpe.to_broadcast([P, T, HEADS, ROPE])).then_inc(kpe_ready, 1)
            for q in range(HEADS // QH):
                pool.wait_ge(q_scaled, 2 * q + 1)
                if q:
                    pool.wait_ge(q_normed, q)
                rotate(q2[:, :, QH * q:QH * q + QH, HD:QK], swapped[:], 1).then_inc(q_normed, 1)
            pool.wait_ge(kqT_raw, 16)
            after(pool.memset(mask[:], 0.0))
            v = mask[:].rearrange("p (b n) -> p b n", b=3)[:, 0:3:2, :]
            pool.affine_select(out=v, in_=v, compare_op=ALU.is_ge, fill=NEG, base=0,
                               pattern=[[0, 2], [-1, P]], channel_multiplier=1).then_inc(mask_ready, 1)
            pool.wait_ge(x_added, 3 * T)
            pool.iota(iota[:], pattern=[[1, P]], base=0, channel_multiplier=0,
                      allow_small_or_imprecise_dtypes=True).then_inc(iota_ready, 1)

        @block.tensor
        def _(pe):
            def three(out, a, b, start, stop):
                pe.matmul(out, a[0], b[0], start=start, stop=False, skip_group_check=True)
                pe.matmul(out, a[0], b[1], start=False, stop=False, skip_group_check=True)
                return pe.matmul(out, a[1], b[0], start=False, stop=stop, skip_group_check=True)

            def both(h, l, *at):
                return h[at], l[at]

            def transpose_x(n):
                for t in range(T):
                    pe.wait_ge(xs_ready, T * (n - (n > 2)) + t + 1)
                    for k in range(KD):
                        o = (k % 2) * S + t * P
                        got = pe.transpose(ps[:, 4 + k // 2, o:o + P], xs[:, t, k * P:(k + 1) * P], ident[:])
                        if t == T - 1 and k % 2:
                            got.then_inc(xT_raw, 1)

            def split(u):
                pe.wait_ge(lo_ready, u + 1)
                return halves(u)

            def projection(name, a_h, a_l, tiles, wait_rows):
                def product(k, kk, t, wh, wl):
                    for half in range(2):
                        got = three(ps[:, 2 * t + half, :], both(a_h, a_l, ALL, k, slice(t * P, t * P + P)),
                                    both(wh, wl, ALL, kk, slice(half * CH, half * CH + CH)), k == 0, k == tiles - 1)
                    return got

                for q in range(tiles // 2 - 1):
                    wh, wl = split(first[name] + q)
                    for kk in range(2):
                        wait_rows(2 * q + kk)
                        for t in range(T):
                            got = product(2 * q + kk, kk, t, wh, wl)
                    got.then_inc(units_used, 1)
                wh, wl = split(first[name] + tiles // 2 - 1)
                for t in range(T):
                    for kk in range(2):
                        if t == 0:
                            wait_rows(tiles - 2 + kk)
                        got = product(tiles - 2 + kk, kk, t, wh, wl)
                    got.then_inc(row0_ready if t == 0 else units_used, 1)

            pe.wait_ge(consts_ready, 1)
            transpose_x(0)
            for c in range(6):
                b = 4 * (c % 2)
                if c >= 2:
                    pe.wait_ge(qkv_out, c - 1)
                for q in range(2):
                    wh, wl = split(first["qkv"] + 2 * c + q)
                    pe.wait_ge(xT_ready, 2 * q + 2)
                    for m in range(4 if c < 4 else T):
                        for kk in range(4):
                            k = 4 * q + kk
                            if c < 4:
                                got = three(ps[:, b + m, 0:S], both(wh, wl, ALL, kk, slice(m * P, m * P + P)),
                                            both(xTh, xTl, ALL, k, slice(0, S)), k == 0, k == 7)
                            else:
                                got = three(ps[:, b + m, :], both(xTh, xTl, ALL, k, slice(m * P, m * P + P)),
                                            both(wh, wl, ALL, kk, slice(0, CH)), k == 0, k == 7)
                    got.then_inc(units_used, 1)

            pe.wait_ge(qkv_out, 6)

            def z_part(h):
                if h >= 4:
                    pe.wait_ge(att_exp, h - 3)
                r = slice(HD * (h % 2), HD * (h % 2) + HD)
                pe.matmul(ps[:, h % 4, 0:S], kT[r, h // 2, 0:P], qT[r, h // 2, :], start=True, stop=False, skip_group_check=True)
                pe.matmul(ps[:, h % 4, S:384], kT[r, h // 2, P:S], qT[r, h // 2, P:S], start=False, stop=False,
                          skip_group_check=True).then_inc(z_ready, 1)

            def sum_part(h):
                pe.wait_ge(spm_ready, h + 1)
                sp0, sp1 = spb[:, h % 4, 0:S], spb[:, h % 4, S:384]
                pe.matmul(ps[:, h % 4, 0:S], ntri[:], sp0, start=False, stop=False, skip_group_check=True)
                pe.matmul(ps[:, h % 4, P:S], nones[:], sp1, start=False, stop=False, skip_group_check=True)
                pe.matmul(ps[:, h % 4, S:384], ntri[:], sp1, start=False, stop=True, skip_group_check=True).then_inc(expo_ready, 1)

            def v_part(layer, h, values, probs, ready):
                p, r = h // 2, slice(HD * (h % 2), HD * (h % 2) + HD)
                pe.wait_ge(ready, h + 1)
                if h % 2 == 0 and p >= 2:
                    pe.wait_ge(oT_ready, 8 * layer + p - 1)
                pe.matmul(ps[r, 4 + p % 2, 0:S], values(0, h), probs[:, h % 4, 0:S], start=True, stop=False, skip_group_check=True)
                got = pe.matmul(ps[r, 4 + p % 2, P:S], values(1, h), probs[:, h % 4, S:384], start=False, stop=True,
                                skip_group_check=True)
                if h % 2:
                    got.then_inc(oT_raw, 1)

            for i in range(HEADS + 3):
                if i < HEADS:
                    z_part(i)
                if 2 <= i < HEADS + 2:
                    sum_part(i - 2)
                if i >= 3:
                    v_part(0, i - 3, lambda t, h: v1[:, t, h * HD:(h + 1) * HD], att, att_ready)
            projection("sbo", xTh, xTl, KD, lambda k: pe.wait_ge(oT_ready, k + 1))
            transpose_x(1)
            for c in range(6):
                b = 4 * (c % 2)
                if c >= 2:
                    pe.wait_ge(h_ready, c - 1)
                u0 = first["gate"] + 4 * c
                if c < 5:
                    for n in range(2):
                        for q in range(2):
                            wh, wl = split(u0 + 2 * n + q)
                            pe.wait_ge(xT_ready, 4 + 2 * q + 2)
                            for m in range(4):
                                for kk in range(4):
                                    k = 4 * q + kk
                                    got = three(ps[:, b + m, n * S:(n + 1) * S], both(wh, wl, ALL, kk, slice(m * P, m * P + P)),
                                                both(xTh, xTl, ALL, k, slice(0, S)), k == 0 and n == 0, k == 7)
                            got.then_inc(units_used, 1)
                else:
                    for q in range(2):
                        wh, wl = split(u0 + q)
                        for m in range(2):
                            for kk in range(4):
                                for n in range(2):
                                    k = 4 * q + kk
                                    got = three(ps[:, b + m, n * S:(n + 1) * S], both(wh, wl, ALL, kk, n, slice(m * P, m * P + P)),
                                                both(xTh, xTl, ALL, k, slice(0, S)), k == 0 and n == 0, k == 7)
                        got.then_inc(units_used, 1)
            pe.wait_ge(h_ready, 5)
            projection("down", fTh, fTl, FT, lambda k: pe.wait_ge(fT_ready, k // 4 + 1))
            transpose_x(2)

            def low(u, q, cols, a_h, a_l, bank, norm):
                wh, wl = split(u + q)
                pe.wait_ge(xT_ready, 4 * norm + 2 * q + 2)
                for t in range(T):
                    for kk in range(4):
                        k = 4 * q + kk
                        got = three(ps[:, bank + t, 0:cols], both(a_h, a_l, ALL, k, slice(t * P, t * P + P)),
                                    both(wh, wl, ALL, kk, slice(0, cols)), k == 0, k == 7)
                got.then_inc(units_used, 1)

            def low_transposed(src, tiles, scaled, bank):
                pe.wait_ge(low_scaled, scaled)
                for k in range(tiles):
                    for t in range(T):
                        o = (k % 2) * S + t * P
                        got = pe.transpose(ps[:, bank + k // 2, o:o + P], src[:, t, k * P:(k + 1) * P], ident[:])
                got.then_inc(lowT_raw, 1)

            def kv_heads(q, bank, between=None):
                wh, wl = split(first["kvb"] + q)
                for n in range(2):
                    for t in range(T):
                        for k in range(2):
                            got = three(ps[:, bank + 2 * n + t, :], both(cTh, cTl, ALL, k, slice(t * P, t * P + P)),
                                        both(wh, wl, ALL, k, slice(n * CH, n * CH + CH)), k == 0, k == 1)
                    if n == 0 and between:
                        between()
                got.then_inc(units_used, 1)

            def q_heads(q):
                wh, wl = split(first["qb"] + q)
                if q < 2:
                    pe.wait_ge(k_normed, 1)
                    pe.wait_ge(v_out, 1)
                else:
                    pe.wait_ge(q_scaled, 2 * (q - 1))
                for t in range(T):
                    for k in range(3):
                        got = three(ps[:, 4 + 2 * (q % 2) + t, 0:QH * QK], both(aTh, aTl, ALL, k, slice(t * P, t * P + P)),
                                    both(wh, wl, ALL, k, slice(0, QH * QK)), k == 0, k == 2)
                got.then_inc(units_used, 1)

            def turn_heads(src, g, bank):
                for n in range(2):
                    for t in range(T):
                        o = n * S + t * P
                        got = pe.transpose(ps[0:QK, bank, o:o + P], src[:, t, 2 * g + n, :], ident[:])
                got.then_inc(kqT_raw, 1)

            for q in range(2):
                low(first["kva"], q, RKV + ROPE, xTh, xTl, 0, 2)
            low(first["qa"], 0, RQ, x2h, x2l, 2, 3)
            low_transposed(kva, 2, 2, 0)
            low(first["qa"], 1, RQ, x2h, x2l, 2, 3)
            pe.wait_ge(lowT_ready, 1)
            kv_heads(0, 4, between=lambda: low_transposed(qa, 3, 4, 2))
            pe.wait_ge(lowT_ready, 2)
            kv_heads(1, 0)
            q_heads(0)
            q_heads(1)
            pe.wait_ge(kpe_ready, 1)
            pe.wait_ge(k_normed, 2)
            pe.wait_ge(v_out, 2)
            for g in range(4):
                turn_heads(kf, g, g)
            q_heads(2)
            q_heads(3)
            for g in range(4, 8):
                pe.wait_ge(kT_out, g - 3)
                turn_heads(kf, g, g - 4)
            for g in range(8):
                pe.wait_ge(q_normed, g // 2 + 1)
                if g < 4:
                    pe.wait_ge(q_scaled, 8)
                else:
                    pe.wait_ge(qT_out, g - 3)
                turn_heads(q2, g, 4 + g % 4)

            pe.wait_ge(qT_out, 8)
            pe.wait_ge(kT_out, 8)

            def score_part(h):
                if h >= 4:
                    pe.wait_ge(max_ready, h - 3)
                pe.matmul(ps[:, h % 4, 0:P], qT2[0:QK, h, 0:P], kT2[0:QK, h, 0:P], start=True, stop=True, skip_group_check=True)
                pe.matmul(ps[:, h % 4, P:384], qT2[0:QK, h, P:S], kT2[0:QK, h, :], start=True, stop=True,
                          skip_group_check=True).then_inc(sc_ready, 1)

            def turn_part(h):
                pe.wait_ge(p_ready, 2 * h + 2)
                if h >= 2:
                    pe.wait_ge(pT_ready, h - 1)
                for b in range(3):
                    got = pe.transpose(ps[:, 6 + h % 2, b * P:(b + 1) * P], pm[:, h % 4, b * P:(b + 1) * P], ident[:])
                got.then_inc(pT_raw, 1)

            for i in range(HEADS + 3):
                if i < HEADS:
                    score_part(i)
                if 2 <= i < HEADS + 2:
                    turn_part(i - 2)
                if i >= 3:
                    v_part(1, i - 3, lambda t, h: v2[:, t, h, :], pt, pT_ready)
            projection("mlo", xTh, xTl, KD, lambda k: pe.wait_ge(oT_ready, 8 + k + 1))
            transpose_x(4)
            pe.wait_ge(xT_ready, 20)
            pe.wait_ge(wr_ready, 2)
            for t in range(T):
                for k in range(KD):
                    got = three(ps[:, 0, t * NE:(t + 1) * NE], both(xTh, xTl, ALL, k, slice(t * P, t * P + P)),
                                both(wrh, wrl, ALL, k), k == 0, k == KD - 1)
            got.then_inc(logits_ready, 1)
            pe.wait_ge(msk_ready, 1)
            pe.matmul(ps[:, 1, 0:NE], before[:], msk[:, 0, :], start=True, stop=True)
            pe.matmul(ps[:, 1, NE:2 * NE], before[:], msk[:, 1, :], start=True, stop=False)
            pe.matmul(ps[:, 1, NE:2 * NE], ones[:], msk[:, 0, :], start=False, stop=True)
            pe.matmul(ps[:, 1, 2 * NE:3 * NE], ones[:], msk[:, 0, :], start=True, stop=False)
            pe.matmul(ps[:, 1, 2 * NE:3 * NE], ones[:], msk[:, 1, :], start=False, stop=True).then_inc(pos_ready, 1)
            pe.wait_ge(route_ready, 1)
            items = pe.value_load(tab[0:1, 0:1], min_val=NE, max_val=ITEMS)

            def gather(half, fill, onehots):
                if fill is not None:
                    pe.wait_ge(aux_read, fill)
                pe.wait_ge(onehot_ready, onehots)
                for kk in range(4):
                    k = 4 * half + kk
                    for t in range(T):
                        got = pe.matmul(ps[:, 7, kk * P:(kk + 1) * P], xs[:, t, k * P:(k + 1) * P], onehot[:, t, :],
                                        start=t == 0, stop=t == T - 1)
                got.then_inc(aux_filled, 1)

            def back(n, fill, ys):
                t, half = n // 2, n % 2
                pe.wait_ge(aux_read, fill)
                pe.wait_ge(ysb_ready, ys)
                pe.matmul(ps[:, 7, :], ST[:, t * P:(t + 1) * P], ysb[:, half * CH:(half + 1) * CH],
                          start=True, stop=True).then_inc(aux_filled, 1)

            gather(0, None, 1)
            gather(1, 1, 1)
            with pe.Fori(0, items) as j:
                pe.wait_ge(aux_read, j * FILLS + 2)
                done = [0]

                def item_split(kind):
                    n = NPRE + done[0]
                    done[0] += 1
                    pe.wait_ge(lo_ready, j * NI + (n + 1))
                    return halves(n, kind)

                def hidden(c, n):
                    for q in range(2):
                        wh, wl = item_split("gate")
                        for kk in range(4):
                            k = 4 * q + kk
                            got = three(ps[:, 2 * (c % 2) + n, :], both(xgh, xgl, ALL, k), both(wh, wl, ALL, kk), k == 0, k == 7)
                        got.then_inc(units_used, 1)

                def turn(c):
                    pe.wait_ge(eh_ready, j * NC + (c + 2))
                    pe.wait_ge(ehT_ready, j * NC + (c + 1))
                    for q in range(2):
                        for k in range(2):
                            i = 2 * q + k
                            got = pe.transpose(ps[:, 6, i * P:(i + 1) * P], hb[:, c % 2, 2 * P * q + k:2 * P * (q + 1):2], ident[:])
                    got.then_inc(ehT_raw, 1)

                def down(c):
                    pe.wait_ge(ehT_ready, j * NC + (c + 2))
                    for q in range(2):
                        wh, wl = item_split("down")
                        for k in range(2):
                            i = 2 * q + k
                            for half in range(2):
                                got = three(ps[:, 4 + half, :], both(hTh, hTl, ALL, c % 2, slice(i * P, (i + 1) * P)),
                                            both(wh, wl, ALL, k, slice(half * CH, (half + 1) * CH)),
                                            c == 0 and i == 0, c == NC - 1 and i == 3)
                        got.then_inc(units_used, 1)

                for c in range(NC):
                    pe.wait_ge(eh_ready, j * NC + max(c, 1))
                    hidden(c, 0)
                    if c:
                        turn(c - 1)
                    if c < 2:
                        back(2 * c, j * FILLS + (2 + 2 * c), j + 1)
                    if c == 2:
                        pe.wait_ge(aux_read, j * FILLS + 6)
                        for t in range(T):
                            got = pe.transpose(ps[:, 7, t * P:(t + 1) * P], onehot[:, t, :], ident[:])
                        got.then_inc(aux_filled, 1)
                    if c == NC - 1:
                        gather(0, j * FILLS + 7, j + 2)
                    hidden(c, 1)
                    if c < 2:
                        back(2 * c + 1, j * FILLS + (3 + 2 * c), j + 1)
                    if c:
                        down(c - 1)
                turn(NC - 1)
                gather(1, j * FILLS + 8, j + 2)
                down(NC - 1)
            for n in range(4):
                back(n, items * FILLS + (2 + n), items + 1)


def rope_table():
    import numpy as np

    freq = np.float32(10000.0) ** (-np.arange(0, ROPE, 2, dtype=np.float32) / np.float32(ROPE))
    ang = np.arange(S, dtype=np.float32)[:, None] * freq[None, :]
    cos, sin = np.cos(ang), np.sin(ang)
    return np.stack([np.concatenate([cos, cos], 1), np.concatenate([-sin, sin], 1)], 1).astype(np.float32)


def kernel(**inputs):
    import numpy as np
    import concourse.bacc as bacc
    from concourse.bass_utils import run_bass_kernel_spmd

    f = {k: np.ascontiguousarray(v) for k, v in inputs.items()}
    rest = np.ones((1, ROPE + 32), np.float32)
    gains = np.concatenate([
        f["g_mix"][0].reshape(KD, P), f["g_ffn"][0].reshape(KD, P), f["kv_g_src"].reshape(KD, P),
        f["g_mix"][1].reshape(KD, P), f["g_ffn"][1].reshape(KD, P), f["kv_g_a"].reshape(2, P),
        f["mla_g_q_a"].reshape(3, P), np.concatenate([f["kv_g_k_nope"].reshape(1, HD), rest], 1),
        np.concatenate([f["mla_g_q_nope"].reshape(1, HD), rest], 1)]).T
    gpe = np.broadcast_to(np.stack([f["kv_g_k_pe"], f["mla_g_q_pe"][0]])[None], (P, 2, ROPE))
    arrays = {
        "x": f["x"][0], "gains": gains, "gpe": gpe, "rope": rope_table(), "g_ffn1": f["g_ffn"][1],
        "w_router": f["moe_w_router"][0], "b_router": f["moe_b_router"][0],
        "w_qkv": f["sb_w_qkv"][0], "w_sbo": f["sb_w_o"][0], "w_gate": f["ffn_w_gate"][0], "w_up": f["ffn_w_up"][0],
        "w_down": f["ffn_w_down"][0], "w_kva": f["kv_w_a"], "w_kvb": f["kv_w_b"], "w_qa": f["mla_w_q_a"][0],
        "w_qb": f["mla_w_q_b"][0], "w_mlo": f["mla_w_o"][0],
        "e_gate": f["moe_w_gate"][0], "e_up": f["moe_w_up"][0], "e_down": f["moe_w_down"][0],
    }
    arrays = {k: np.ascontiguousarray(v) for k, v in arrays.items()}
    nc = bacc.Bacc("TRN2", target_bir_lowering=False, num_devices=1)
    d = {k: nc.dram_tensor(k, a.shape, F32, kind="ExternalInput").ap() for k, a in arrays.items()}
    out = nc.dram_tensor("out", (S, D), F32, kind="ExternalOutput").ap()
    build(nc, d["x"], d["gains"], d["gpe"], d["rope"], d["g_ffn1"], d["w_router"], d["b_router"],
          {k[2:]: d[k] for k in d if k.startswith("w_") and k != "w_router"}, d["e_gate"], d["e_up"], d["e_down"], out)
    r = run_bass_kernel_spmd(nc, [arrays], core_ids=[0])
    return r.results[0]["out"].reshape(1, S, D)
```

```python
from contextlib import ExitStack

import concourse.bass as bass
from concourse import mybir

ALL = slice(None)
F32 = mybir.dt.float32
F32R = mybir.dt.float32r
I32 = mybir.dt.int32
U32 = mybir.dt.uint32
ALU = mybir.AluOpType
ACT = mybir.ActivationFunctionType
AXX = mybir.AxisListType.X

P = 128
D = 1024
S = 256
T = S // P
KD = D // P
HEADS = 16
GH = 4
GROUPS = HEADS // GH
QKV_CHUNKS = (0, 2, 1, 3, 4, 5)
HD = 64
ROPE = 32
QK = HD + ROPE
QH = 4
KH = 8
RQ = 384
RKV = 256
FD = 2816
FT = FD // P
FE = 3584
NE = 8
CH = 512
NC = FE // CH
EPS = 1e-6
FAR = 4096.0
OVER = S * 2 // (P + 1)
ITEMS = NE + OVER
FILLS = 7
NEG = -1e30

UNIT = 2048
RAW, HI, LO = 7, 3, 3
EXTRA = 4
ERAW = RAW + EXTRA

G_MIX0, G_FFN0, G_KV, G_MIX1, G_FFN1, G_KVA, G_QA, G_KN, G_QN = 0, 8, 16, 24, 32, 40, 42, 45, 46
NG = 47


def shape_unit(tile, n, *dims):
    names = "abcd"[:len(dims)]
    return tile[:, 0:n].rearrange(f"p ({' '.join(names)}) -> p {' '.join(names)}", **dict(zip(names, dims)))


def plan(w):
    out = []

    def rows(src, r0, n, c0, c1):
        return src[r0 * P:(r0 + n) * P, c0:c1].rearrange("(k p) n -> p k n", p=P)

    for c in QKV_CHUNKS:
        for q in range(2):
            out.append(("qkv", (4, CH), rows(w["qkv"], 4 * q, 4, c * CH, c * CH + CH)))
    for q in range(4):
        out.append(("sbo", (2, D), rows(w["sbo"], 2 * q, 2, 0, D)))
    for c in range(5):
        for m in ("gate", "up"):
            for q in range(2):
                out.append((m, (4, CH), rows(w[m], 4 * q, 4, c * CH, c * CH + CH)))
    for q in range(2):
        out.append(("tail", (4, 2, 256), [rows(w[m], 4 * q, 4, 5 * CH, FD) for m in ("gate", "up")]))
    for q in range(FT // 2):
        out.append(("down", (2, D), rows(w["down"], 2 * q, 2, 0, D)))
    for q in range(2):
        out.append(("kva", (4, RKV + ROPE), rows(w["kva"], 4 * q, 4, 0, RKV + ROPE)))
    for q in range(2):
        out.append(("qa", (4, RQ), rows(w["qa"], 4 * q, 4, 0, RQ)))
    for q in range(2):
        out.append(("kvb", (2, D), rows(w["kvb"], 0, 2, q * D, q * D + D)))
    for q in range(HEADS // QH):
        out.append(("qb", (3, QH * QK), rows(w["qb"], 0, 3, q * QH * QK, (q + 1) * QH * QK)))
    for q in range(4):
        out.append(("mlo", (2, D), rows(w["mlo"], 2 * q, 2, 0, D)))
    return out


def expert_plan():
    out = []
    for c in range(NC):
        out += [("gate", c, 0), ("gate", c, 1), ("up", c, 0), ("up", c, 1)]
        if c:
            out += [("down", c - 1, 0), ("down", c - 1, 1)]
    return out + [("down", NC - 1, 0), ("down", NC - 1, 1)]


def build(nc, x_d, gains_d, gpe_d, rope_d, gffn1_d, wr_d, br_d, w, eg, eu, ed, out_d):
    pre = plan(w)
    NPRE = len(pre)
    first = {}
    for u, (name, _, _) in enumerate(pre):
        first.setdefault(name, u)
    item_units = expert_plan()
    NI = len(item_units)
    assert NPRE % RAW == 0 and NI % HI == 0 and NI % LO == 0

    with ExitStack() as ctx:
        base = (nc.sbuf_base + 63) // 64 * 64
        end = nc.sbuf_usable_end // 32 * 32
        at = [base]

        def put(name, shape, dt=F32, off=None):
            n = 4
            for s in shape[1:]:
                n *= s
            n = (n + 31) // 32 * 32
            o = at[0] if off is None else off
            if off is None:
                at[0] += n
            assert o + n <= end, (name, o + n - end)
            return nc.alloc_sbuf_tensor_at(name, shape, dt, offset=o)

        def sem(name):
            return ctx.enter_context(nc.semaphore(name))

        raw = [put(f"raw{i}", [P, UNIT]) for i in range(RAW)]
        hi = [put(f"hi{i}", [P, UNIT], F32R) for i in range(HI)]
        lo = [put(f"lo{i}", [P, UNIT], F32R) for i in range(LO)]
        x = put("x", [P, T, D])
        xs_at = at[0]
        xs = put("xs", [P, T, D])
        xT_at = at[0]
        xTh = put("xTh", [P, KD, S], F32R)
        xTl = put("xTl", [P, KD, S], F32R)
        ident = put("ident", [P, P])
        ones = put("ones", [P, P])
        before = put("before", [P, P])
        ntri = put("ntri", [P, P])
        nones = put("nones", [P, P])
        gains = put("gains", [P, NG])
        gpe = put("gpe", [P, 2, ROPE])
        rope = put("rope", [P, T, 2, ROPE])
        wr = put("wr", [P, KD, NE])
        wrh = put("wrh", [P, KD, NE], F32R)
        wrl = put("wrl", [P, KD, NE], F32R)
        br = put("br", [P, NE])
        iota8 = put("iota8", [P, NE])
        eps = put("eps", [P, 1])
        one = put("one", [P, 1])
        ss = put("ss", [P, 8])
        rt = put("rt", [P, 8])
        rs = put("rs", [P, 8])
        hs = put("hs", [P, 6, 16])
        hr = put("hr", [P, 6, 16])
        hi_ = put("hrec", [P, 6, 16])
        ropeg = put("ropeg", [P, 2, T, 2, ROPE])
        swapped = put("swapped", [P, T, QH, ROPE])
        arena = (at[0] + 63) // 64 * 64

        def lay(*items):
            o, got = arena, []
            for name, shape, dt in items:
                got.append(put(name, shape, dt, off=o))
                n = 4
                for s in shape[1:]:
                    n *= s
                places[name] = o
                o += (n + 31) // 32 * 32
            places["end"] = o
            return got

        places = {}

        qT, kT, v1, lnp, spb, att = lay(
            ("qT", [P, KD, S], F32), ("kT", [P, KD, S], F32), ("v1", [P, T, D], F32),
            ("lnp", [P, 2, 3, CH], F32), ("spb", [P, 2, 3, CH], F32), ("att", [P, 2, 3, CH], F32))
        PARTS = (2, 0, 1)
        fTh, fTl, sg, hm = lay(("fTh", [P, FT, S], F32R), ("fTl", [P, FT, S], F32R),
                               ("sg", [P, 4, S], F32), ("hm", [P, 4, S], F32))
        kf, q2, v2, kT2, qT2 = lay(
            ("kf", [P, T, HEADS, QK], F32), ("q2", [P, T, HEADS, QK], F32), ("v2", [P, T, HEADS, HD], F32),
            ("kT2", [P, HEADS, S], F32), ("qT2", [P, HEADS, S], F32))
        o = arena + 4 * (2 * T * HEADS * QK + T * HEADS * HD + HEADS * S)
        kva, qa = put("kva", [P, T, RKV + ROPE], off=o), put("qa", [P, T, RQ], off=o + 2304)
        cTh, cTl = put("cTh", [P, 2, S], F32R, off=o + 5376), put("cTl", [P, 2, S], F32R, off=o + 7424)
        aTh, aTl = put("aTh", [P, 3, S], F32R, off=o + 9472), put("aTl", [P, 3, S], F32R, off=o + 12544)
        o = arena + 4 * (2 * T * HEADS * QK + T * HEADS * HD)
        x2h, x2l = put("x2h", [P, KD, S], F32R, off=o), put("x2l", [P, KD, S], F32R, off=o + 4 * KD * S)
        mask, pm, pt, nm, sm, rc = lay(
            ("mask", [P, 384], F32), ("pm", [P, 4, 384], F32), ("pt", [P, 4, 384], F32),
            ("nm", [P, HEADS, 2], F32), ("sm", [P, HEADS, 2], F32), ("rc", [P, HEADS, 2], F32))
        (iota, onehot, ST, xgh, xgl, xsh, xsl, lg, mv, mi, ix, chosen, msk, far,
         gap, pex, gden, gates, gparts, cnt, rank, sel, slot, gt, ef,
         picked, pickede, pslot, tab) = lay(
            ("iota", [P, P], F32), ("onehot", [P, T, P], F32R), ("ST", [P, S], F32R),
            ("xgh", [P, KD, P], F32R), ("xgl", [P, KD, P], F32R), 
            ("xsh", [P, T, D], F32R), ("xsl", [P, T, D], F32R),
            ("lg", [P, T, NE], F32), ("mv", [P, T, 8], F32), ("mi", [P, T, 8], U32), ("ix", [P, T, 8], F32),
            ("chosen", [P, T, 2, NE], F32), ("msk", [P, T, NE], F32), ("far", [P, T, NE], F32), ("gap", [P, T], F32),
            ("pex", [P, T], F32), ("gden", [P, T], F32), ("gates", [P, T, 2], F32), ("gparts", [P, T, 2, NE], F32),
            ("cnt", [P, NE], F32), ("rank", [P, 4, NE + 1], F32), ("sel", [P, OVER, NE], F32),
            ("slot", [P, T, ITEMS + 1], F32), ("gt", [P, T, ITEMS + 1], F32), ("ef", [P, 8], F32),
            ("picked", [P, T, OVER, NE], F32), ("pickede", [P, OVER, NE], F32), ("pslot", [P, T, OVER], F32), ("tab", [P, 8], I32))
        experts_end = places["end"]
        extra = [put(f"extra{i}", [P, UNIT], off=end - (EXTRA - i) * 4 * UNIT) for i in range(EXTRA)]
        assert end - EXTRA * 4 * UNIT >= experts_end
        gbc, lgT = put("gbc", [P, D], off=places["xgl"]), put("lgT", [P, S], off=places["xgh"])
        ysbh, ysbl = put("ysbh", [P, D], F32R, off=xT_at), put("ysbl", [P, D], F32R, off=xT_at + 4 * D)
        hTh, hTl = (put(n, [P, 2, CH], F32R, off=xT_at + 8 * D + 8 * CH * k) for k, n in enumerate(("hTh", "hTl")))
        sl, hb = put("sl", [P, 2, CH], off=xs_at), put("hb", [P, 2, CH], off=xs_at + 8 * CH)

        ps = ctx.enter_context(nc.psum_tensor("ps", [P, 8, CH], F32))

        raw_landed = [sem(f"raw_landed{i}") for i in range(ERAW)]
        hi_ready, lo_ready, units_used = sem("hi_ready"), sem("lo_ready"), sem("units_used")
        router_in, consts_in, ones_set, consts_ready = sem("router_in"), sem("consts_in"), sem("ones_set"), sem("consts_ready")
        x_in = [sem(f"x_in{t}") for t in range(T)]
        dve_done, act_done, pool_done = sem("dve_done"), sem("act_done"), sem("pool_done")
        sumsq_ready, squares_ready, rms_ready, xs_ready = sem("sumsq_ready"), sem("squares_ready"), sem("rms_ready"), sem("xs_ready")
        row0_ready, norm_root = sem("row0_ready"), sem("norm_root")
        xT_raw, xTh_ready, xT_ready = sem("xT_raw"), sem("xTh_ready"), sem("xT_ready")
        qkv_out = sem("qkv_out")
        z_ready, negabs_ready, lnp_ready, sp_ready = sem("z_ready"), sem("negabs_ready"), sem("lnp_ready"), sem("sp_ready")
        spm_ready, expo_ready, att_exp, att_ready = sem("spm_ready"), sem("expo_ready"), sem("att_exp"), sem("att_ready")
        oT_raw, oTh_ready, oT_ready = sem("oT_raw"), sem("oTh_ready"), sem("oT_ready")
        x_added = sem("x_added")
        silu_ready, h_ready, fTh_ready, fT_ready = (sem("silu_ready"), sem("h_ready"),
                                                              sem("fTh_ready"), sem("fT_ready"))
        low_squares, low_scaled, lowT_raw, lowTh_ready, lowT_ready = (
            sem("low_squares"), sem("low_scaled"), sem("lowT_raw"), sem("lowTh_ready"), sem("lowT_ready"))
        rope_ready, kpe_ready, v_out = sem("rope_ready"), sem("kpe_ready"), sem("v_out")
        heads_squared, k_normed, q_scaled, q_normed = sem("heads_squared"), sem("k_normed"), sem("q_scaled"), sem("q_normed")
        kqT_raw, qT_even_out, qT_odd_out, kT_out = sem("kqT_raw"), sem("qT_even_out"), sem("qT_odd_out"), sem("kT_out")
        sc_ready, max_ready, p_exp, p_ready = sem("sc_ready"), sem("max_ready"), sem("p_exp"), sem("p_ready")
        pT_raw, pT_ready, mask_ready = sem("pT_raw"), sem("pT_ready"), sem("mask_ready")
        rows_gained, rows_hi, rows_ready = sem("rows_gained"), sem("rows_hi"), sem("rows_ready")
        logitsT_ready, logitsT_out = sem("logitsT_ready"), sem("logitsT_out")
        logits_ready, wr_ready, gap_ready, gexp_ready = sem("logits_ready"), sem("wr_ready"), sem("gap_ready"), sem("gexp_ready")
        msk_ready, pos_ready, route_ready, gbc_in, iota_ready = (
            sem("msk_ready"), sem("pos_ready"), sem("route_ready"), sem("gbc_in"), sem("iota_ready"))
        onehot_ready, xgh_ready, aux_filled, aux_read = sem("onehot_ready"), sem("xgh_ready"), sem("aux_filled"), sem("aux_read")
        esilu_ready, eh_ready, ehT_raw, ehTh_ready, ehT_ready = (
            sem("esilu_ready"), sem("eh_ready"), sem("ehT_raw"), sem("ehTh_ready"), sem("ehT_ready"))
        ysbh_ready, ysb_ready, result_back, result_added, out_done = sem("ysbh_ready"), sem("ysb_ready"), sem("result_back"), sem("result_added"), sem("out_done")

        def size(dims):
            n = 1
            for s in dims:
                n *= s
            return n

        def raw_of(n, j=None):
            if j is None:
                return raw[n % RAW]
            return (raw + extra)[(n - NPRE) % ERAW]

        def unit_floats(i):
            return size(pre[i][1])

        def halves(u, kind=None):
            dims = pre[u][1] if kind is None else ((2, D) if kind == "down" else (4, CH))
            return [shape_unit(r[u % len(r)], size(dims), *dims) for r in (hi, lo)]

        def column(j, n):
            return slice(n, n + 1) if isinstance(j, int) and j == 0 else bass.ds(j + n, 1)

        BEFORE_NORM, AFTER_TURN = {0: 12, 1: 10, 2: 10, 4: 10}, {0: 18, 1: 8, 2: 8, 4: 5}
        Q_BANKS = (4, 5, 0, 1, 2, 3, 6, 7)

        norm_after = {1: first["sbo"] + 4, 2: first["down"], 3: first["kva"], 4: NPRE}

        def turned(n, b):
            return 4 * (n if n < 3 else n - 1) + b

        class Units:
            def __init__(self, one_unit):
                self.n, self.one_unit = 0, one_unit

            def until(self, n):
                while self.n < min(n, NPRE):
                    self.one_unit(self.n, self.n, unit_floats(self.n))
                    self.n += 1

        block = ctx.enter_context(nc.Block())

        @block.sync
        def _(sp):
            for t in range(T):
                sp.dma_start(x[:, t, :], x_d[t * P:(t + 1) * P, :]).then_inc(x_in[t], 16)
            for dst, src in ((gains[:], gains_d), (gpe[:], gpe_d), (rope[:], rope_d.rearrange("(t p) a r -> p t a r", p=P))):
                sp.dma_start(dst, src).then_inc(consts_in, 16)
            for u, (_, dims, src) in enumerate(pre):
                if u >= RAW:
                    sp.wait_ge(lo_ready, u - RAW + 1)
                dst = shape_unit(raw[u % RAW], size(dims), *dims)
                if isinstance(src, list):
                    for m, part in enumerate(src):
                        sp.dma_start(dst[:, :, m, :], part).then_inc(raw_landed[u % RAW], 16)
                else:
                    sp.dma_start(dst, src).then_inc(raw_landed[u % RAW], 16)

            def load_item(j, e):
                for i, (kind, c, q) in enumerate(item_units):
                    n = NPRE + i
                    s = i % ERAW
                    landing = raw_landed[s]
                    if i >= ERAW:
                        sp.wait_ge(lo_ready, j * NI + (n - ERAW + 1))
                    elif not isinstance(j, int):
                        last = max(v for v in range(s, NI, ERAW))
                        sp.wait_ge(lo_ready, j * NI + (NPRE + last - NI + 1))
                    elif i < RAW:
                        sp.wait_ge(lo_ready, n - RAW + 1)
                    else:
                        sp.wait_ge(units_used, first["mlo"] + 1)
                    slot_of = raw_of(n, j)
                    if kind == "down":
                        r0 = c * CH + q * 2 * P
                        sp.dma_start(shape_unit(slot_of, UNIT, 2, D),
                                     ed[e, r0:r0 + 2 * P, :].rearrange("(p k) n -> p k n", k=2)
                                     ).then_inc(landing, 16)
                    else:
                        src = eg if kind == "gate" else eu
                        sp.dma_start(shape_unit(slot_of, UNIT, 4, CH),
                                     src[e, q * 4 * P:(q + 1) * 4 * P, c * CH:(c + 1) * CH].rearrange(
                                         "(k p) n -> p k n", p=P)).then_inc(landing, 16)

            load_item(0, 0)
            with sp.Fori(1, NE) as j:
                load_item(j, j)
            sp.wait_ge(route_ready, 1)
            over = sp.value_load(tab[0:1, 1:2], min_val=0, max_val=OVER)
            with sp.If(over > 0):
                with sp.Fori(0, over) as r:
                    e = sp.value_load(tab[0:1, bass.ds(r + 2, 1)], min_val=0, max_val=NE - 1)
                    load_item(r + NE, e)

            for n in range(2 * T):
                half, t = divmod(n, T)
                cols = slice(half * CH, (half + 1) * CH)
                sp.wait_ge(result_added, n + 1)
                sp.dma_start(out_d[t * P:(t + 1) * P, cols], x[:, t, cols]).then_inc(out_done, 16)
            sp.wait_ge(out_done, 16 * 2 * T)

        def landed(eng, u, j=None):
            if j is None:
                s, uses = u % RAW, u // RAW + 1
                tails = sum(pre[v][0] == "tail" for v in range(s, u + 1, RAW))
                eng.wait_ge(raw_landed[s], 16 * (uses + tails))
                return
            i = u - NPRE
            s = i % ERAW
            earlier = NPRE // RAW + sum(pre[v][0] == "tail" for v in range(s, NPRE, RAW)) if s < RAW else 0
            eng.wait_ge(raw_landed[s], j * (16 * len(range(s, NI, ERAW))) + 16 * (earlier + i // ERAW + 1))

        @block.scalar
        def _(act):
            for dst, src in ((wr[:], wr_d.rearrange("(k p) e -> p k e", p=P)), (br[:], br_d.partition_broadcast(P))):
                act.dma_start(dst, src).then_inc(router_in, 16)

            def round_unit(u, n, floats, j=None):
                landed(act, n, j)
                if j is None and u >= HI:
                    act.wait_ge(units_used, u - HI + 1)
                elif j is not None:
                    act.wait_ge(units_used, j * NI + (n - HI + 1))
                act.activation(hi[n % HI][:, 0:floats], raw_of(n, j)[:, 0:floats], ACT.Copy).then_inc(hi_ready, 1)

            units = Units(round_unit)

            def mean_squares(n):
                for t in range(T):
                    k = T * (n - (n > 2)) + t
                    if n:
                        act.wait_ge(x_added, k - T + 1)
                        act.wait_ge(xT_raw, turned(n, 0))
                    else:
                        act.wait_ge(x_in[t], 16)
                    act.activation(xs[:, t, :], x[:, t, :], ACT.Square, scale=D ** -0.5,
                                   accum_out=ss[:, t:t + 1]).then_inc(squares_ready, 1)
                    act.wait_ge(squares_ready, k + 1)
                    act.activation(rt[:, t:t + 1], ss[:, t:t + 1], ACT.Sqrt, bias=eps[:]).then_inc(norm_root, 1)

            def norm_transposed(n, g):
                dst = x2h if n == 3 else xTh
                for b in range(4):
                    if n != 3:
                        act.wait_ge(xT_raw, turned(n, b + 1))
                    else:
                        act.wait_ge(xT_ready, 4 * 2 + b + 1)
                    if n:
                        act.wait_ge(units_used, norm_after[n])
                    for k in (2 * b, 2 * b + 1):
                        got = act.activation(dst[:, k, :], ps[:, 4 + b, (k % 2) * S:(k % 2 + 1) * S], ACT.Copy,
                                             scale=gains[:, g + k:g + k + 1])
                    got.then_inc(xTh_ready, 1)

            act.wait_ge(consts_ready, 1)
            mean_squares(0)
            act.wait_ge(consts_in, 16 * 3)
            units.until(1)
            norm_transposed(0, G_MIX0)
            for i, c in enumerate(QKV_CHUNKS[:4]):
                units.until(2 * i + 5)
                act.wait_ge(units_used, first["qkv"] + 2 * i + 2)
                b = 4 * (i % 2)
                dst = (qT if c < 2 else kT)[:, 4 * (c % 2):4 * (c % 2) + 4, :]
                act.activation(dst, ps[:, b:b + 4, 0:S], ACT.Copy, scale=HD ** -0.5 if c < 2 else 1.0).then_inc(qkv_out, 1)

            def v_out_part(n):
                units.until(2 * (4 + n) + 5)
                act.wait_ge(units_used, first["qkv"] + 2 * (4 + n) + 2)
                act.activation(v1[:, :, n * CH:(n + 1) * CH], ps[:, 6:6 + T, :], ACT.Copy).then_inc(qkv_out, 1)

            def exp_part(g):
                for i, b in enumerate(PARTS):
                    act.wait_ge(negabs_ready, 3 * g + i + 1)
                    act.activation(lnp[:, g % 2, b, :], lnp[:, g % 2, b, :], ACT.Exp).then_inc(act_done, 1)

            def log_part(g):
                for i, b in enumerate(PARTS):
                    act.wait_ge(act_done, 3 * g + i + 1)
                    act.activation(lnp[:, g % 2, b, :], lnp[:, g % 2, b, :], ACT.Ln, bias=one[:]).then_inc(lnp_ready, 1)

            def att_part(g):
                for i, b in enumerate(PARTS):
                    act.wait_ge(expo_ready, 3 * g + i + 1)
                    act.activation(att[:, g % 2, b, :], ps[:, 3 * (g % 2) + b, :], ACT.Exp).then_inc(att_exp, 1)

            def head_out(layer, p):
                act.wait_ge(oT_raw, 8 * layer + p + 1)
                act.activation(xTh[:, p, :], ps[:, (6, 4)[layer] + p % 2, 0:S], ACT.Copy).then_inc(oTh_ready, 1)

            def group_out(g):
                for p in range(GH // 2):
                    head_out(0, g * GH // 2 + p)

            for g in range(GROUPS + 1):
                if g < GROUPS:
                    exp_part(g)
                if g:
                    att_part(g - 1)
                if g < GROUPS:
                    log_part(g)
                if g < 2:
                    v_out_part(g)
                if g >= 2:
                    group_out(g - 2)
            group_out(GROUPS - 1)
            units.until(first["gate"] + 2)
            mean_squares(1)
            norm_transposed(1, G_FFN0)
            for c in range(6):
                nt = 4 if c < 5 else 2
                last = first["gate"] + 4 * c + (3 if c < 5 else 1)
                units.until(last + 4)
                act.wait_ge(units_used, last + 1)
                if c:
                    act.wait_ge(h_ready, c)
                b = 4 * (c % 2)
                act.activation(sg[:, 0:nt, :], ps[:, b:b + nt, 0:S], ACT.Silu).then_inc(silu_ready, 1)
                act.wait_ge(h_ready, c + 1)
                act.activation(fTh[:, 4 * c:4 * c + nt, :], hm[:, 0:nt, :], ACT.Copy).then_inc(fTh_ready, 1)
            units.until(first["down"] + 11 + 2)
            mean_squares(2)
            norm_transposed(2, G_KV)
            units.until(first["down"] + 11 + 3)
            norm_transposed(3, G_MIX1)
            sq = xs[:].rearrange("p t d -> p (t d)")

            def low_roots(done, parts):
                for bank, cols, col, place in parts:
                    n = cols.stop - cols.start
                    act.activation(sq[:, place:place + n], ps[:, bank, cols], ACT.Square, scale=n ** -0.5,
                                   accum_out=ss[:, col:col + 1]).then_inc(low_squares, 1)
                act.wait_ge(low_squares, done + len(parts))
                a, b = parts[0][2], parts[-1][2] + 1
                act.activation(rt[:, a:b], ss[:, a:b], ACT.Sqrt, bias=eps[:]).then_inc(rms_ready, 1)

            def low_hi(k_tiles, dst, g, bank, n):
                act.wait_ge(lowT_raw, n)
                for k in range(k_tiles):
                    got = act.activation(dst[:, k, :], ps[:, bank + k // 2, (k % 2) * S:(k % 2 + 1) * S], ACT.Copy,
                                         scale=gains[:, g + k:g + k + 1])
                got.then_inc(lowTh_ready, 1)

            def heads_square(i, src, n):
                act.activation(sq[:, (i % 2) * D:(i % 2) * D + n], src, ACT.Square).then_inc(heads_squared, 1)

            def heads_root(i, parts):
                act.wait_ge(sumsq_ready, i + 1)
                for a, b, dim in parts:
                    got = act.activation(hr[:, i, a:b], hs[:, i, a:b], ACT.Sqrt, bias=eps[:], scale=1.0 / dim)
                got.then_inc(rms_ready, 1)

            units.until(first["kva"] + 4)
            act.wait_ge(units_used, first["kva"] + 2)
            low_roots(0, [(0, slice(0, RKV), 2, 0), (1, slice(0, RKV), 3, RKV),
                          (0, slice(RKV, RKV + ROPE), 4, 2 * RKV), (1, slice(RKV, RKV + ROPE), 5, 2 * RKV + ROPE)])
            units.until(first["kva"] + 5)
            low_hi(2, cTh, G_KVA, 0, 1)
            units.until(first["qa"] + 4)
            act.wait_ge(units_used, first["qa"] + 2)
            low_roots(4, [(2, slice(0, RQ), 6, D), (3, slice(0, RQ), 7, D + RQ)])
            units.until(first["qa"] + 5)
            low_hi(3, aTh, G_QA, 2, 2)
            for q in range(2):
                act.wait_ge(units_used, first["kvb"] + q + 1)
                b = 4 if q == 0 else 0
                heads = ps[:, b:b + 4, :].rearrange("p b (h d) -> p b h d", h=4)
                heads_square(q, heads[:, :, :, 0:HD], 4 * 4 * HD)
                for n in range(2):
                    hh = slice(KH * q + 4 * n, KH * q + 4 * n + 4)
                    got = act.activation(v2[:, :, hh, :], heads[:, 2 * n:2 * n + 2, :, HD:2 * HD], ACT.Copy)
                got.then_inc(v_out, 1)
                heads_root(q, [(0, 16, HD)])
                units.until(first["kvb"] + q + 4)

            def k_out(g):
                act.wait_ge(kqT_raw, g + 1)
                act.activation(kT2[0:QK, 2 * g:2 * g + 2, :], ps[0:QK, g % 4, :].rearrange("p (h s) -> p h s", h=2),
                               ACT.Copy, scale=gains[0:QK, G_KN:G_KN + 1]).then_inc(kT_out, 1)

            for q in range(HEADS // QH):
                act.wait_ge(units_used, first["qb"] + q + 1)
                b = 4 + 2 * (q % 2)
                heads_square(2 + q, ps[:, b:b + T, 0:QH * QK], T * QH * QK)
                units.until(first["qb"] + 4)
                heads_root(2 + q, [(0, 8, HD), (8, 16, ROPE)])
                if q % 2:
                    for g in range(2 * (q - 1), 2 * (q - 1) + 4):
                        k_out(g)

            def q_out(g):
                act.wait_ge(kqT_raw, 8 + g + 1)
                act.activation(qT2[0:QK, 2 * g:2 * g + 2, :], ps[0:QK, Q_BANKS[g], :].rearrange("p (h s) -> p h s", h=2),
                               ACT.Copy, scale=gains[0:QK, G_QN:G_QN + 1]).then_inc(qT_odd_out, 1)

            for g in range(1, 8, 2):
                q_out(g)

            def p_part(h):
                act.wait_ge(max_ready, h + 1)
                act.activation(pm[:, h % 4, 0:P], pm[:, h % 4, 0:P], ACT.Exp, scale=-1.0, bias=nm[:, h, 0:1],
                               accum_out=sm[:, h, 0:1]).then_inc(p_exp, 1)
                act.activation(pm[:, h % 4, P:384], pm[:, h % 4, P:384], ACT.Exp, scale=-1.0, bias=nm[:, h, 1:2],
                               accum_out=sm[:, h, 1:2]).then_inc(p_exp, 1)

            def pt_part(h):
                act.wait_ge(pT_raw, h + 1)
                act.activation(pt[:, h % 4, :], ps[:, 6 + h % 2, 0:384], ACT.Copy).then_inc(pT_ready, 1)

            for i in range(HEADS + 5):
                if i < HEADS:
                    p_part(i)
                if i >= 6 and i % 2 == 0:
                    head_out(1, (i - 6) // 2)
                if 3 <= i < HEADS + 3:
                    pt_part(i - 3)
                if i == HEADS - 3:
                    units.until(first["mlo"] + 1)
            units.until(NPRE)
            mean_squares(4)
            act.dma_start(gbc[:], gffn1_d.partition_broadcast(P)).then_inc(gbc_in, 16)
            norm_transposed(4, G_FFN1)

            def rows_high(t):
                act.wait_ge(rows_gained, t + 1)
                act.activation(xsh[:, t, :], xs[:, t, :], ACT.Copy).then_inc(rows_hi, 1)

            round_unit(None, NPRE, UNIT, 0)
            rows_high(0)
            act.wait_ge(logitsT_ready, 1)
            act.activation(lgT[0:NE, :], ps[0:NE, 0, 0:S], ACT.Copy).then_inc(logitsT_out, 1)
            rows_high(1)
            for n in range(NPRE + 1, NPRE + HI):
                round_unit(None, n, UNIT, 0)
            act.wait_ge(gap_ready, 1)
            act.activation(pex[:], gap[:], ACT.Exp).then_inc(gexp_ready, 1)
            def gather_hi(half, fill, n, bank=7):
                act.wait_ge(aux_filled, fill)
                if n is not None:
                    act.wait_ge(units_used, n)
                act.activation(xgh[:, 4 * half:4 * half + 4, :], ps[:, bank, :].rearrange("p (k s) -> p k s", s=P),
                               ACT.Copy).then_inc(xgh_ready, 1)

            def take_y(n):
                act.wait_ge(units_used, n)
                act.activation(ysbh[:], ps[:, 4:6, :].rearrange("p b n -> p (b n)"), ACT.Copy).then_inc(ysbh_ready, 1)

            for half in range(2):
                gather_hi(half, half + 1, None, 7 - half)

            def item(j, started=0):
                done = [started]

                def item_until(n):
                    while done[0] < n:
                        round_unit(None, NPRE + done[0], UNIT, j)
                        done[0] += 1

                def h_hi(c):
                    act.wait_ge(ehT_raw, j * NC + (c + 1))
                    act.activation(hTh[:, c % 2, :], ps[:, 6, :], ACT.Copy).then_inc(ehTh_ready, 1)

                item_until(2)
                if not isinstance(j, int):
                    take_y(j * NI + NPRE)
                for c in range(NC):
                    if c:
                        item_until(6 * c + 2)
                        h_hi(c - 1)
                    item_until(6 * c + 4 if c else 6)
                    act.wait_ge(units_used, j * NI + (NPRE + (6 * c + 2 if c else 4)))
                    act.wait_ge(eh_ready, j * NC + max(c, 1))
                    act.activation(sl[:, c % 2, :], ps[:, 2 * (c % 2), :], ACT.Silu).then_inc(esilu_ready, 1)
                gather_hi(0, j * FILLS + 4, j * NI + (NPRE + 38))
                item_until(NI)
                h_hi(NC - 1)
                gather_hi(1, j * FILLS + 5, None)

            item(0, HI)
            act.wait_ge(route_ready, 1)
            items = act.value_load(tab[0:1, 0:1], min_val=NE, max_val=ITEMS)
            with act.Fori(1, items) as j:
                item(j)
            act.wait_ge(units_used, items * NI + NPRE)
            for half in range(2):
                act.activation(ysbh[:, half * CH:(half + 1) * CH], ps[:, 4 + half, :], ACT.Copy).then_inc(ysbh_ready, 1)

        @block.vector
        def _(dve):
            steps = [0]

            def after(ins):
                steps[0] += 1
                ins.then_inc(dve_done, 1)
                dve.wait_ge(dve_done, steps[0])

            def subtract_unit(u, n, floats, j=None):
                dve.wait_ge(hi_ready, n + 1 if j is None else j * NI + (n + 1))
                dve.tensor_tensor(lo[n % LO][:, 0:floats], raw_of(n, j)[:, 0:floats],
                                  hi[n % HI][:, 0:floats].bitcast(F32), ALU.subtract).then_inc(lo_ready, 1)

            units = Units(subtract_unit)

            def normalise(n):
                for t in range(T):
                    dve.wait_ge(norm_root, T * (n - (n > 2)) + t + 1)
                    after(dve.reciprocal(rs[:, t:t + 1], rt[:, t:t + 1]))
                    dve.tensor_scalar(xs[:, t, :], x[:, t, :], rs[:, t:t + 1], None, ALU.mult).then_inc(xs_ready, 1)

            def norm_transposed(n, g):
                h, l = (x2h, x2l) if n == 3 else (xTh, xTl)
                for b in range(4):
                    dve.wait_ge(xTh_ready, 4 * n + b + 1)
                    for k in (2 * b, 2 * b + 1):
                        got = dve.scalar_tensor_tensor(
                            out=l[:, k, :], in0=ps[:, 4 + b, (k % 2) * S:(k % 2 + 1) * S], scalar=gains[:, g + k:g + k + 1],
                            in1=h[:, k, :].bitcast(F32), op0=ALU.mult, op1=ALU.subtract)
                    got.then_inc(xT_ready, 1)

            def add_projection(n, name, count):
                for t in range(T):
                    if t == 0:
                        dve.wait_ge(row0_ready, n + 1)
                    else:
                        dve.wait_ge(units_used, first[name] + count)
                    dve.tensor_tensor(x[:, t, :], x[:, t, :], ps[:, 2 * t:2 * t + 2, :].rearrange("p b n -> p (b n)"),
                                      ALU.add).then_inc(x_added, 1)

            normalise(0)
            units.until(1)
            dve.wait_ge(consts_in, 16 * 3)
            norm_transposed(0, G_MIX0)
            for c in range(4):
                units.until(2 * c + 5)
            dve.wait_ge(router_in, 16 * 2)
            dve.tensor_copy(wrh[:], wr[:]).then_inc(wr_ready, 1)
            dve.wait_ge(wr_ready, 1)
            dve.tensor_tensor(wrl[:], wr[:], wrh[:].bitcast(F32), ALU.subtract).then_inc(wr_ready, 1)

            def split_scores(g):
                dve.wait_ge(z_ready, 2 * g + 2)
                for b in PARTS:
                    got = dve.tensor_scalar(spb[:, g % 2, b, :], ps[:, 3 * (g % 2) + b, :], 0.0, None, ALU.max)
                after(got)
                for b in PARTS:
                    dve.scalar_tensor_tensor(out=lnp[:, g % 2, b, :], in0=spb[:, g % 2, b, :], scalar=-2.0,
                                             in1=ps[:, 3 * (g % 2) + b, :], op0=ALU.mult, op1=ALU.add).then_inc(negabs_ready, 1)

            def softplus_part(g):
                for i, b in enumerate(PARTS):
                    dve.wait_ge(lnp_ready, 3 * g + i + 1)
                    dve.tensor_tensor(spb[:, g % 2, b, :], spb[:, g % 2, b, :], lnp[:, g % 2, b, :], ALU.add).then_inc(sp_ready, 1)

            def head_out(layer, p):
                dve.wait_ge(oTh_ready, 8 * layer + p + 1)
                dve.tensor_tensor(xTl[:, p, :], ps[:, (6, 4)[layer] + p % 2, 0:S], xTh[:, p, :].bitcast(F32),
                                  ALU.subtract).then_inc(oT_ready, 1)

            def group_out(g):
                for p in range(GH // 2):
                    head_out(0, g * GH // 2 + p)

            split_scores(0)
            for g in range(GROUPS):
                softplus_part(g)
                if g < 2:
                    units.until(2 * (4 + g) + 5)
                if g + 1 < GROUPS:
                    split_scores(g + 1)
                if g >= 2:
                    group_out(g - 2)
            group_out(GROUPS - 2)
            group_out(GROUPS - 1)
            units.until(first["gate"] + 2)
            add_projection(0, "sbo", 4)
            normalise(1)
            norm_transposed(1, G_FFN0)
            for c in range(6):
                nt = 4 if c < 5 else 2
                last = first["gate"] + 4 * c + (3 if c < 5 else 1)
                units.until(last + 4)
                dve.wait_ge(silu_ready, c + 1)
                if c:
                    dve.wait_ge(fT_ready, c)
                b = 4 * (c % 2)
                dve.tensor_tensor(hm[:, 0:nt, :], sg[:, 0:nt, :], ps[:, b:b + nt, S:2 * S], ALU.mult).then_inc(h_ready, 1)
                dve.wait_ge(fTh_ready, c + 1)
                dve.tensor_tensor(fTl[:, 4 * c:4 * c + nt, :], hm[:, 0:nt, :], fTh[:, 4 * c:4 * c + nt, :].bitcast(F32),
                                  ALU.subtract).then_inc(fT_ready, 1)
            units.until(first["down"] + 11 + 2)
            add_projection(1, "down", 11)
            normalise(2)
            norm_transposed(2, G_KV)
            units.until(first["down"] + 11 + 3)
            norm_transposed(3, G_MIX1)
            sq = xs[:].rearrange("p t d -> p (t d)")

            def low_reciprocal(a, b, n):
                dve.wait_ge(rms_ready, n)
                after(dve.reciprocal(rs[:, a:b], rt[:, a:b]))

            def low_lo(k_tiles, h, l, g, bank, n):
                dve.wait_ge(lowTh_ready, n)
                for k in range(k_tiles):
                    got = dve.scalar_tensor_tensor(out=l[:, k, :], in0=ps[:, bank + k // 2, (k % 2) * S:(k % 2 + 1) * S],
                                                   scalar=gains[:, g + k:g + k + 1], in1=h[:, k, :].bitcast(F32),
                                                   op0=ALU.mult, op1=ALU.subtract)
                got.then_inc(lowT_ready, 1)

            def heads_reciprocal(i):
                dve.wait_ge(rms_ready, 3 + i)
                after(dve.reciprocal(hi_[:, i, :], hr[:, i, :]))

            units.until(first["kva"] + 4)
            low_reciprocal(2, 6, 1)
            for t in range(T):
                dve.tensor_scalar(kva[:, t, 0:RKV], ps[:, t, 0:RKV], rs[:, 2 + t:3 + t], None, ALU.mult)
                dve.tensor_scalar(kva[:, t, RKV:RKV + ROPE], ps[:, t, RKV:RKV + ROPE], rs[:, 4 + t:5 + t], None,
                                  ALU.mult).then_inc(low_scaled, 1)
            units.until(first["kva"] + 5)
            low_lo(2, cTh, cTl, G_KVA, 0, 1)
            units.until(first["qa"] + 4)
            low_reciprocal(6, 8, 2)
            for t in range(T):
                dve.tensor_scalar(qa[:, t, :], ps[:, 2 + t, 0:RQ], rs[:, 6 + t:7 + t], None, ALU.mult).then_inc(low_scaled, 1)
            units.until(first["qa"] + 5)
            low_lo(3, aTh, aTl, G_QA, 2, 2)
            for q in range(2):
                b = 4 if q == 0 else 0
                dve.wait_ge(heads_squared, q + 1)
                dve.tensor_reduce(hs[:, q, :], sq[:, q * D:q * D + 16 * HD].rearrange("p (h d) -> p h d", d=HD), AXX,
                                  ALU.add).then_inc(sumsq_ready, 1)
                heads_reciprocal(q)
                heads = ps[:, b:b + 4, :].rearrange("p b (h d) -> p b h d", h=4)
                for n in range(2):
                    got = dve.tensor_tensor(
                        kf[:, :, KH * q + 4 * n:KH * q + 4 * n + 4, 0:HD], heads[:, 2 * n:2 * n + 2, :, 0:HD],
                        hi_[:, q, 8 * n:8 * n + 8].rearrange("p (t h) -> p t h", t=T).unsqueeze(3).to_broadcast([P, T, 4, HD]),
                        ALU.mult)
                got.then_inc(k_normed, 1)
                units.until(first["kvb"] + q + 4)
            for q in range(HEADS // QH):
                b = 4 + 2 * (q % 2)
                i = 2 + q
                dve.wait_ge(heads_squared, i + 1)
                squares = sq[:, (i % 2) * D:(i % 2) * D + T * QH * QK].rearrange("p (h d) -> p h d", d=QK)
                dve.tensor_reduce(hs[:, i, 0:8], squares[:, :, 0:HD], AXX, ALU.add)
                dve.tensor_reduce(hs[:, i, 8:16], squares[:, :, HD:QK], AXX, ALU.add).then_inc(sumsq_ready, 1)
                units.until(first["qb"] + min(q + 3, 4))
                heads_reciprocal(i)
                heads = ps[:, b:b + T, 0:QH * QK].rearrange("p t (h d) -> p t h d", h=QH)
                for part, (c0, c1) in ((1, (HD, QK)), (0, (0, HD))):
                    got = dve.tensor_tensor(
                        q2[:, :, QH * q:QH * q + QH, c0:c1], heads[:, :, :, c0:c1],
                        hi_[:, i, 8 * part:8 * part + 8].rearrange("p (t h) -> p t h", t=T).unsqueeze(3).to_broadcast(
                            [P, T, QH, c1 - c0]), ALU.mult)
                    got.then_inc(q_scaled, 1)
            for g in range(0, 8, 2):
                dve.wait_ge(kqT_raw, 8 + g + 1)
                dve.tensor_scalar(qT2[0:QK, 2 * g:2 * g + 2, :],
                                  ps[0:QK, Q_BANKS[g], :].rearrange("p (h s) -> p h s", h=2),
                                  gains[0:QK, G_QN:G_QN + 1], None, ALU.mult).then_inc(qT_even_out, 1)
            dve.wait_ge(mask_ready, 1)

            def max_part(h):
                dve.wait_ge(sc_ready, h + 1)
                for n, cols in enumerate((slice(0, P), slice(P, 384))):
                    got = dve.tensor_tensor_reduce(pm[:, h % 4, cols], ps[:, h % 4, cols], mask[:, cols],
                                                   -float(QK) ** -0.5, 3e38, ALU.add, ALU.min, nm[:, h, n:n + 1])
                got.then_inc(max_ready, 1)

            def share_part(h):
                dve.wait_ge(p_exp, 2 * h + 2)
                after(dve.reciprocal(rc[:, h, :], sm[:, h, :]))
                dve.tensor_scalar(pm[:, h % 4, 0:P], pm[:, h % 4, 0:P], rc[:, h, 0:1], None, ALU.mult).then_inc(p_ready, 1)
                dve.tensor_scalar(pm[:, h % 4, P:384], pm[:, h % 4, P:384], rc[:, h, 1:2], None,
                                  ALU.mult).then_inc(p_ready, 1)

            for i in range(HEADS + 6):
                if i < HEADS:
                    max_part(i)
                if 1 <= i < HEADS + 1:
                    share_part(i - 1)
                if i >= 7 and i % 2 == 1:
                    head_out(1, (i - 7) // 2)
                if i == HEADS - 1:
                    units.until(first["mlo"] + 1)
            units.until(NPRE)
            add_projection(2, "mlo", 4)
            normalise(4)
            norm_transposed(4, G_FFN1)
            def build_onehot(col):
                for t in range(T):
                    got = dve.tensor_scalar(onehot[:, t, :], iota[:], slot[:, t, col], None, ALU.is_equal)
                got.then_inc(onehot_ready, 1)

            def gather_lo(half, ready, bank=7):
                dve.wait_ge(xgh_ready, ready)
                dve.tensor_tensor(xgl[:, 4 * half:4 * half + 4, :], ps[:, bank, :].rearrange("p (k s) -> p k s", s=P),
                                  xgh[:, 4 * half:4 * half + 4, :].bitcast(F32), ALU.subtract).then_inc(aux_read, 1)

            dve.wait_ge(logits_ready, 1)
            dve.wait_ge(iota_ready, 1)
            after(dve.tensor_tensor(lg[:], ps[:, 1, 0:T * NE].rearrange("p (t e) -> p t e", t=T),
                                    br[:].unsqueeze(1).to_broadcast([P, T, NE]), ALU.add))
            for t in range(T):
                got = dve.max(mv[:, t, :], lg[:, t, :])
            after(got)
            for t in range(T):
                got = dve.max_index(mi[:, t, :], mv[:, t, :], lg[:, t, :])
            after(got)
            dve.tensor_tensor(gap[:], mv[:, :, 1], mv[:, :, 0], ALU.subtract).then_inc(gap_ready, 1)
            after(dve.tensor_copy(ix[:], mi[:]))
            after(dve.tensor_tensor(chosen[:], iota8[:].unsqueeze(1).unsqueeze(1).to_broadcast([P, T, 2, NE]),
                                    ix[:, :, 0:2].unsqueeze(3).to_broadcast([P, T, 2, NE]), ALU.is_equal))
            dve.tensor_tensor(msk[:], chosen[:, :, 0, :], chosen[:, :, 1, :], ALU.add).then_inc(msk_ready, 1)
            dve.wait_ge(msk_ready, 1)
            after(dve.tensor_scalar(far[:], msk[:], -FAR, FAR, ALU.mult, ALU.add))
            dve.wait_ge(pos_ready, 1)
            after(dve.tensor_tensor(slot[:, :, 0:NE], ps[:, 0, 0:T * NE].rearrange("p (t e) -> p t e", t=T), far[:], ALU.add))
            build_onehot(slice(0, 1))
            after(dve.tensor_scalar(cnt[:], ps[:, 0, 2 * NE:3 * NE], float(P), None, ALU.is_gt))
            for n in range(NPRE, NPRE + 2):
                subtract_unit(None, n, UNIT, 0)
            for half in range(2):
                gather_lo(half, half + 1, 7 - half)

            def further_items():
                after(dve.tensor_copy(rank[:, 1, 1:NE + 1], cnt[:]))
                for i, step in enumerate((1, 2, 4)):
                    src, dst = rank[:, 1 + i, :], rank[:, (2, 3, 0)[i], :]
                    dve.tensor_copy(dst[:, 1:1 + step], src[:, 1:1 + step])
                    after(dve.tensor_tensor(dst[:, 1 + step:], src[:, 1 + step:], src[:, 1:NE + 1 - step], ALU.add))

            def item_table():
                after(dve.tensor_tensor(sel[:], rank[:, 0, 0:NE].unsqueeze(1).to_broadcast([P, OVER, NE]),
                                        iota8[:, 0:OVER].unsqueeze(2).to_broadcast([P, OVER, NE]), ALU.is_equal))
                after(dve.tensor_tensor(sel[:], sel[:], cnt[:].unsqueeze(1).to_broadcast([P, OVER, NE]), ALU.mult))
                after(dve.tensor_tensor(pickede[:], sel[:], iota8[:].unsqueeze(1).to_broadcast([P, OVER, NE]), ALU.mult))
                dve.tensor_reduce(ef[:, 2:2 + OVER], pickede[:], AXX, ALU.add)
                dve.tensor_copy(ef[:, 1:2], rank[:, 0, NE:NE + 1])
                after(dve.tensor_scalar(ef[:, 0:1], rank[:, 0, NE:NE + 1], float(NE), None, ALU.add))
                dve.tensor_copy(tab[:, 0:2 + OVER], ef[:, 0:2 + OVER]).then_inc(route_ready, 1)

            def gates_of_items():
                dve.wait_ge(gexp_ready, 1)
                after(dve.tensor_scalar(gden[:], pex[:], 1.0, None, ALU.add))
                after(dve.reciprocal(gates[:, :, 0], gden[:]))
                after(dve.tensor_tensor(gates[:, :, 1], gates[:, :, 0], pex[:], ALU.mult))
                after(dve.tensor_tensor(gparts[:], chosen[:], gates[:].unsqueeze(3).to_broadcast([P, T, 2, NE]), ALU.mult))
                after(dve.tensor_tensor(gt[:, :, 1:NE + 1], gparts[:, :, 0, :], gparts[:, :, 1, :], ALU.add))

            def further_slots():
                selt = sel[:].unsqueeze(1).to_broadcast([P, T, OVER, NE])
                after(dve.tensor_tensor(picked[:], slot[:, :, 0:NE].unsqueeze(2).to_broadcast([P, T, OVER, NE]), selt, ALU.mult))
                after(dve.tensor_reduce(pslot[:], picked[:], AXX, ALU.add))
                after(dve.tensor_scalar(slot[:, :, NE:ITEMS], pslot[:], -float(P), None, ALU.add))
                after(dve.tensor_tensor(picked[:], gt[:, :, 1:NE + 1].unsqueeze(2).to_broadcast([P, T, OVER, NE]), selt, ALU.mult))
                after(dve.tensor_reduce(gt[:, :, NE + 1:ITEMS + 1], picked[:], AXX, ALU.add))

            for counts_from_one in (eh_ready, ehT_ready):
                dve.nop().then_inc(counts_from_one, 1)

            def add_back(n, fill, col):
                t, half = n // 2, n % 2
                dve.wait_ge(aux_filled, fill)
                xo = x[:, t, half * CH:(half + 1) * CH]
                dve.scalar_tensor_tensor(out=xo, in0=ps[:, 7, :], scalar=gt[:, t, col], in1=xo,
                                         op0=ALU.mult, op1=ALU.add).then_inc(aux_read, 1)

            def item(j, started=0, between=()):
                done = [started]

                def item_until(n):
                    while done[0] < n:
                        subtract_unit(None, NPRE + done[0], UNIT, j)
                        done[0] += 1

                def h_lo(c):
                    dve.wait_ge(ehTh_ready, j * NC + (c + 1))
                    dve.tensor_tensor(hTl[:, c % 2, :], ps[:, 6, :], hTh[:, c % 2, :].bitcast(F32),
                                      ALU.subtract).then_inc(ehT_ready, 1)

                for c in range(NC):
                    if c:
                        item_until(6 * c + 2)
                        h_lo(c - 1)
                    else:
                        item_until(2)
                        if not isinstance(j, int):
                            dve.wait_ge(ysbh_ready, j)
                            dve.tensor_tensor(ysbl[:], ps[:, 4:6, :].rearrange("p b n -> p (b n)"), ysbh[:].bitcast(F32),
                                              ALU.subtract).then_inc(ysb_ready, 1)
                        item_until(4)
                    if c < 2 and not isinstance(j, int):
                        add_back(2 * c, j * FILLS + (2 * c - 1), bass.ds(j, 1))
                    if c == 2:
                        dve.wait_ge(aux_filled, j * FILLS + 3)
                        dve.tensor_copy(ST[:], ps[:, 7, 0:S]).then_inc(aux_read, 1)
                        build_onehot(column(j, 1))
                    item_until(6 * c + 4 if c else 6)
                    dve.wait_ge(esilu_ready, j * NC + (c + 1))
                    dve.tensor_tensor(hb[:, c % 2, :], sl[:, c % 2, :], ps[:, 2 * (c % 2) + 1, :], ALU.mult).then_inc(eh_ready, 1)
                    if c < 2 and not isinstance(j, int):
                        add_back(2 * c + 1, j * FILLS + 2 * c, bass.ds(j, 1))
                    if c < len(between):
                        between[c]()
                gather_lo(0, j * 2 + 3)
                item_until(NI - 1)
                h_lo(NC - 1)
                item_until(NI)
                gather_lo(1, j * 2 + 4)

            item(0, 2, (gates_of_items, further_items, item_table, further_slots))
            dve.wait_ge(route_ready, 1)
            items = dve.value_load(tab[0:1, 0:1], min_val=NE, max_val=ITEMS)
            with dve.Fori(1, items) as j:
                item(j)
            for half in range(2):
                cols = slice(half * CH, (half + 1) * CH)
                dve.wait_ge(ysbh_ready, items + half)
                dve.tensor_tensor(ysbl[:, cols], ps[:, 4 + half, :], ysbh[:, cols].bitcast(F32), ALU.subtract).then_inc(ysb_ready, 1)
            for n in range(2 * T):
                half, t = divmod(n, T)
                xo = x[:, t, half * CH:(half + 1) * CH]
                dve.wait_ge(result_back, n + 1)
                dve.scalar_tensor_tensor(out=xo, in0=ps[:, n, :], scalar=gt[:, t, bass.ds(items, 1)], in1=xo,
                                         op0=ALU.mult, op1=ALU.add).then_inc(result_added, 1)

        @block.gpsimd
        def _(pool):
            for tile, value in ((ident, 0.0), (ones, 1.0), (before, 1.0), (ntri, -1.0), (nones, -1.0), (eps, EPS), (one, 1.0)):
                pool.memset(tile[:], value).then_inc(ones_set, 1)
            pool.wait_ge(ones_set, 7)
            pool.affine_select(out=ident[:], in_=ident[:], compare_op=ALU.not_equal, fill=1.0, base=0,
                               pattern=[[-1, P]], channel_multiplier=1)
            pool.affine_select(out=before[:], in_=before[:], compare_op=ALU.is_gt, fill=0.0, base=0,
                               pattern=[[1, P]], channel_multiplier=-1)
            pool.iota(iota8[:], pattern=[[1, NE]], base=0, channel_multiplier=0, allow_small_or_imprecise_dtypes=True)
            pool.affine_select(out=ntri[:], in_=ntri[:], compare_op=ALU.is_ge, fill=0.0, base=0,
                               pattern=[[-1, P]], channel_multiplier=1).then_inc(consts_ready, 1)

            steps = [0]

            def after(ins):
                steps[0] += 1
                ins.then_inc(pool_done, 1)
                pool.wait_ge(pool_done, steps[0])

            pool.wait_ge(consts_in, 16 * 3)
            half = ROPE // 2
            for m in range(2):
                for t in range(T):
                    pool.tensor_tensor(ropeg[:, m, t, 0, :], rope[:, t, 0, :], gpe[:, m, :], ALU.mult)
                    pool.tensor_tensor(ropeg[:, m, t, 1, 0:half], rope[:, t, 1, 0:half], gpe[:, m, half:ROPE], ALU.mult)
                    got = pool.tensor_tensor(ropeg[:, m, t, 1, half:ROPE], rope[:, t, 1, half:ROPE], gpe[:, m, 0:half], ALU.mult)
            got.then_inc(rope_ready, 1)

            def rotate(v, other, m):
                n = v.shape[2]

                def factor(which, a, b):
                    return ropeg[:, m, :, which, a:b].unsqueeze(2).to_broadcast([P, T, n, b - a])

                pool.tensor_tensor(other[:, :, :, 0:half], v[:, :, :, half:ROPE], factor(1, 0, half), ALU.mult)
                after(pool.tensor_tensor(other[:, :, :, half:ROPE], v[:, :, :, 0:half], factor(1, half, ROPE), ALU.mult))
                after(pool.tensor_tensor(v, v, factor(0, 0, ROPE), ALU.mult))
                return pool.tensor_tensor(v, v, other, ALU.add)

            def diagonal(tile, part, done):
                v = tile[:, part, :].rearrange("p (h n) -> p h n", h=GH if part == 2 else 2)[:, :, 0:P]
                pool.affine_select(out=v, in_=v, compare_op=ALU.is_gt, fill=0.0, base=0,
                                   pattern=[[0, v.shape[1]], [1, P]], channel_multiplier=-1).then_inc(done, 1)

            for g in range(GROUPS):
                for source, tile, done in ((sp_ready, spb, spm_ready), (att_exp, att, att_ready)):
                    for i, b in enumerate(PARTS):
                        pool.wait_ge(source, 3 * g + i + 1)
                        diagonal(tile[:, g % 2], b, done)
            pool.wait_ge(rope_ready, 1)
            pool.wait_ge(low_scaled, 2)
            kpe = kva[:, :, RKV:RKV + ROPE].unsqueeze(2)
            after(rotate(kpe, swapped[:, :, 0:1, :], 0))
            pool.tensor_copy(kf[:, :, :, HD:QK], kpe.to_broadcast([P, T, HEADS, ROPE])).then_inc(kpe_ready, 1)
            for q in range(HEADS // QH):
                pool.wait_ge(q_scaled, 2 * q + 1)
                if q:
                    pool.wait_ge(q_normed, q)
                rotate(q2[:, :, QH * q:QH * q + QH, HD:QK], swapped[:], 1).then_inc(q_normed, 1)
            pool.wait_ge(kqT_raw, 16)
            after(pool.memset(mask[:], 0.0))
            v = mask[:].rearrange("p (b n) -> p b n", b=3)[:, 0:3:2, :]
            pool.affine_select(out=v, in_=v, compare_op=ALU.is_ge, fill=NEG, base=0,
                               pattern=[[0, 2], [-1, P]], channel_multiplier=1).then_inc(mask_ready, 1)
            pool.wait_ge(x_added, 3 * T)
            pool.memset(slot[:, :, ITEMS:], -1.0)
            pool.memset(gt[:, :, 0:1], 0.0)
            pool.memset(rank[:], 0.0)
            pool.iota(iota[:], pattern=[[1, P]], base=0, channel_multiplier=0,
                      allow_small_or_imprecise_dtypes=True).then_inc(iota_ready, 1)
            pool.wait_ge(xT_raw, turned(4, 4))
            pool.wait_ge(gbc_in, 16)
            for t in range(T):
                pool.tensor_tensor(xs[:, t, :], xs[:, t, :], gbc[:], ALU.mult).then_inc(rows_gained, 1)
            for t in range(T):
                pool.wait_ge(rows_hi, t + 1)
                pool.tensor_tensor(xsl[:, t, :], xs[:, t, :], xsh[:, t, :].bitcast(F32), ALU.subtract).then_inc(rows_ready, 1)

        @block.tensor
        def _(pe):
            def three(out, a, b, start, stop):
                pe.matmul(out, a[0], b[0], start=start, stop=False, skip_group_check=True)
                pe.matmul(out, a[0], b[1], start=False, stop=False, skip_group_check=True)
                return pe.matmul(out, a[1], b[0], start=False, stop=stop, skip_group_check=True)

            def both(h, l, *at):
                return h[at], l[at]

            def keep_warm(bank, n):
                for _ in range(n):
                    pe.matmul(ps[:, bank, 0:P], ones[:], ones[:], start=True, stop=True, skip_group_check=True)

            def transpose_x(n):
                keep_warm(7, BEFORE_NORM[n])
                for t in range(T):
                    pe.wait_ge(xs_ready, T * (n - (n > 2)) + t + 1)
                    for k in range(KD):
                        o = (k % 2) * S + t * P
                        got = pe.transpose(ps[:, 4 + k // 2, o:o + P], xs[:, t, k * P:(k + 1) * P], ident[:])
                        if t == T - 1 and k % 2:
                            got.then_inc(xT_raw, 1)
                keep_warm(3, AFTER_TURN[n])

            def split(u):
                pe.wait_ge(lo_ready, u + 1)
                return halves(u)

            def projection(name, a_h, a_l, tiles, wait_rows):
                def product(k, kk, t, wh, wl):
                    for half in range(2):
                        got = three(ps[:, 2 * t + half, :], both(a_h, a_l, ALL, k, slice(t * P, t * P + P)),
                                    both(wh, wl, ALL, kk, slice(half * CH, half * CH + CH)), k == 0, k == tiles - 1)
                    return got

                for q in range(tiles // 2 - 1):
                    wh, wl = split(first[name] + q)
                    for kk in range(2):
                        wait_rows(2 * q + kk)
                        for t in range(T):
                            got = product(2 * q + kk, kk, t, wh, wl)
                    got.then_inc(units_used, 1)
                wh, wl = split(first[name] + tiles // 2 - 1)
                for t in range(T):
                    for kk in range(2):
                        if t == 0:
                            wait_rows(tiles - 2 + kk)
                        got = product(tiles - 2 + kk, kk, t, wh, wl)
                    got.then_inc(row0_ready if t == 0 else units_used, 1)

            pe.wait_ge(consts_ready, 1)
            transpose_x(0)
            for i in range(4):
                b = 4 * (i % 2)
                if i >= 2:
                    pe.wait_ge(qkv_out, i - 1)
                for q in range(2):
                    wh, wl = split(first["qkv"] + 2 * i + q)
                    pe.wait_ge(xT_ready, 2 * q + 2)
                    for m in range(4):
                        for kk in range(4):
                            k = 4 * q + kk
                            got = three(ps[:, b + m, 0:S], both(wh, wl, ALL, kk, slice(m * P, m * P + P)),
                                        both(xTh, xTl, ALL, k, slice(0, S)), k == 0, k == 7)
                    got.then_inc(units_used, 1)

            def v_chunk(n):
                pe.wait_ge(qkv_out, 4 + n)
                for q in range(2):
                    wh, wl = split(first["qkv"] + 2 * (4 + n) + q)
                    for m in range(T):
                        for kk in range(4):
                            k = 4 * q + kk
                            got = three(ps[:, 6 + m, :], both(xTh, xTl, ALL, k, slice(m * P, m * P + P)),
                                        both(wh, wl, ALL, kk, slice(0, CH)), k == 0, k == 7)
                    got.then_inc(units_used, 1)

            def z_part(g):
                if g < 2:
                    pe.wait_ge(qkv_out, 3 + g)
                else:
                    pe.wait_ge(att_exp, 3 * (g - 1))
                b = 3 * (g % 2)
                for parity in range(2):
                    r = slice(HD * parity, HD * parity + HD)
                    for j in range(2):
                        pair = GH // 2 * g + j
                        pe.matmul(ps[:, b + parity, j * S:(j + 1) * S], kT[r, pair, 0:P], qT[r, pair, :],
                                  start=j == 0, stop=False, skip_group_check=True)
                    if parity:
                        pe.wait_ge(z_ready, 2 * g + 1)
                    for j in range(2):
                        pair = GH // 2 * g + j
                        got = pe.matmul(ps[:, b + 2, (2 * parity + j) * P:(2 * parity + j + 1) * P], kT[r, pair, P:S],
                                        qT[r, pair, P:S], start=parity == 0 and j == 0, stop=False, skip_group_check=True)
                    got.then_inc(z_ready, 1)

            def sum_part(g):
                b = 3 * (g % 2)
                sp = spb[:, g % 2]
                pe.wait_ge(spm_ready, 3 * g + 1)
                pe.matmul(ps[:, b + 2, :], ntri[:], sp[:, 2, :], start=False, stop=True, skip_group_check=True).then_inc(expo_ready, 1)
                for i in range(2):
                    pe.matmul(ps[:, b + i, :].rearrange("p (h n) -> p h n", h=2)[:, :, P:S], nones[:],
                              sp[:, 2, i * S:(i + 1) * S].rearrange("p (h n) -> p h n", h=2),
                              start=False, stop=False, skip_group_check=True)
                    pe.wait_ge(spm_ready, 3 * g + 2 + i)
                    pe.matmul(ps[:, b + i, :], ntri[:], sp[:, i, :], start=False, stop=True,
                              skip_group_check=True).then_inc(expo_ready, 1)

            def v_part(layer, h, values, probs0, probs1):
                p, r, bank = h // 2, slice(HD * (h % 2), HD * (h % 2) + HD), (6, 4)[layer] + (h // 2) % 2
                if h % 2 == 0 and p >= 2:
                    pe.wait_ge(oT_ready, 8 * layer + p - 1)
                pe.matmul(ps[r, bank, 0:S], values(0, h), probs0, start=True, stop=False, skip_group_check=True)
                got = pe.matmul(ps[r, bank, P:S], values(1, h), probs1, start=False, stop=True, skip_group_check=True)
                if h % 2:
                    got.then_inc(oT_raw, 1)

            def values_part(g):
                for i in range(GH):
                    pe.wait_ge(att_ready, 3 * g + 2 + i % 2)
                    place = 2 * (i % 2) + i // 2
                    v_part(0, GH * g + i, lambda t, h: v1[:, t, h * HD:(h + 1) * HD],
                           att[:, g % 2, i % 2, (i // 2) * S:(i // 2 + 1) * S], att[:, g % 2, 2, place * P:(place + 1) * P])

            z_part(0)
            v_chunk(0)
            z_part(1)
            for g in range(GROUPS):
                sum_part(g)
                if g == 0:
                    v_chunk(1)
                else:
                    if g == 1:
                        pe.wait_ge(qkv_out, 6)
                    values_part(g - 1)
                if g + 2 < GROUPS:
                    z_part(g + 2)
            values_part(GROUPS - 1)
            projection("sbo", xTh, xTl, KD, lambda k: pe.wait_ge(oT_ready, k + 1))
            transpose_x(1)
            for c in range(6):
                b = 4 * (c % 2)
                if c >= 2:
                    pe.wait_ge(h_ready, c - 1)
                u0 = first["gate"] + 4 * c
                if c < 5:
                    for n in range(2):
                        for q in range(2):
                            wh, wl = split(u0 + 2 * n + q)
                            pe.wait_ge(xT_ready, 4 + 2 * q + 2)
                            for m in range(4):
                                for kk in range(4):
                                    k = 4 * q + kk
                                    got = three(ps[:, b + m, n * S:(n + 1) * S], both(wh, wl, ALL, kk, slice(m * P, m * P + P)),
                                                both(xTh, xTl, ALL, k, slice(0, S)), k == 0 and n == 0, k == 7)
                            got.then_inc(units_used, 1)
                else:
                    for q in range(2):
                        wh, wl = split(u0 + q)
                        for m in range(2):
                            for kk in range(4):
                                for n in range(2):
                                    k = 4 * q + kk
                                    got = three(ps[:, b + m, n * S:(n + 1) * S], both(wh, wl, ALL, kk, n, slice(m * P, m * P + P)),
                                                both(xTh, xTl, ALL, k, slice(0, S)), k == 0 and n == 0, k == 7)
                        got.then_inc(units_used, 1)
            pe.wait_ge(h_ready, 5)
            projection("down", fTh, fTl, FT, lambda k: pe.wait_ge(fT_ready, k // 4 + 1))
            transpose_x(2)

            def low(u, q, cols, a_h, a_l, bank, norm):
                wh, wl = split(u + q)
                pe.wait_ge(xT_ready, 4 * norm + 2 * q + 2)
                for t in range(T):
                    for kk in range(4):
                        k = 4 * q + kk
                        got = three(ps[:, bank + t, 0:cols], both(a_h, a_l, ALL, k, slice(t * P, t * P + P)),
                                    both(wh, wl, ALL, kk, slice(0, cols)), k == 0, k == 7)
                got.then_inc(units_used, 1)

            def low_transposed(src, tiles, scaled, bank):
                pe.wait_ge(low_scaled, scaled)
                for k in range(tiles):
                    for t in range(T):
                        o = (k % 2) * S + t * P
                        got = pe.transpose(ps[:, bank + k // 2, o:o + P], src[:, t, k * P:(k + 1) * P], ident[:])
                got.then_inc(lowT_raw, 1)

            def kv_heads(q, bank, between=None):
                wh, wl = split(first["kvb"] + q)
                for n in range(2):
                    for t in range(T):
                        for k in range(2):
                            got = three(ps[:, bank + 2 * n + t, :], both(cTh, cTl, ALL, k, slice(t * P, t * P + P)),
                                        both(wh, wl, ALL, k, slice(n * CH, n * CH + CH)), k == 0, k == 1)
                    if n == 0 and between:
                        between()
                got.then_inc(units_used, 1)

            def q_heads(q):
                wh, wl = split(first["qb"] + q)
                if q < 2:
                    pe.wait_ge(k_normed, 1)
                    pe.wait_ge(v_out, 1)
                else:
                    pe.wait_ge(q_scaled, 2 * (q - 1))
                for t in range(T):
                    for k in range(3):
                        got = three(ps[:, 4 + 2 * (q % 2) + t, 0:QH * QK], both(aTh, aTl, ALL, k, slice(t * P, t * P + P)),
                                    both(wh, wl, ALL, k, slice(0, QH * QK)), k == 0, k == 2)
                got.then_inc(units_used, 1)

            def turn_heads(src, g, bank):
                for n in range(2):
                    for t in range(T):
                        o = n * S + t * P
                        got = pe.transpose(ps[0:QK, bank, o:o + P], src[:, t, 2 * g + n, :], ident[:])
                got.then_inc(kqT_raw, 1)

            for q in range(2):
                low(first["kva"], q, RKV + ROPE, xTh, xTl, 0, 2)
            low(first["qa"], 0, RQ, x2h, x2l, 2, 3)
            low_transposed(kva, 2, 2, 0)
            low(first["qa"], 1, RQ, x2h, x2l, 2, 3)
            pe.wait_ge(lowT_ready, 1)
            kv_heads(0, 4, between=lambda: low_transposed(qa, 3, 4, 2))
            pe.wait_ge(lowT_ready, 2)
            kv_heads(1, 0)
            q_heads(0)
            q_heads(1)
            pe.wait_ge(kpe_ready, 1)
            pe.wait_ge(k_normed, 2)
            pe.wait_ge(v_out, 2)
            for g in range(4):
                turn_heads(kf, g, g)
            q_heads(2)
            q_heads(3)
            for g in range(4, 8):
                pe.wait_ge(kT_out, g - 3)
                turn_heads(kf, g, g - 4)
            for g in range(8):
                pe.wait_ge(q_normed, g // 2 + 1)
                pe.wait_ge(q_scaled, 2 * (g // 2 + 1))
                if g < 2:
                    pe.wait_ge(q_scaled, 6)
                elif g < 6:
                    pe.wait_ge(kT_out, g + 3)
                turn_heads(q2, g, Q_BANKS[g])

            for done in (qT_even_out, qT_odd_out):
                pe.wait_ge(done, 3)

            def score_part(h):
                if h >= 4:
                    pe.wait_ge(max_ready, h - 3)
                pe.matmul(ps[:, h % 4, 0:P], qT2[0:QK, h, 0:P], kT2[0:QK, h, 0:P], start=True, stop=True, skip_group_check=True)
                pe.matmul(ps[:, h % 4, P:384], qT2[0:QK, h, P:S], kT2[0:QK, h, :], start=True, stop=True,
                          skip_group_check=True).then_inc(sc_ready, 1)

            def turn_part(h):
                pe.wait_ge(p_ready, 2 * h + 2)
                if h == 0:
                    for done in (qT_even_out, qT_odd_out):
                        pe.wait_ge(done, 4)
                if h >= 2:
                    pe.wait_ge(pT_ready, h - 1)
                for b in range(3):
                    got = pe.transpose(ps[:, 6 + h % 2, b * P:(b + 1) * P], pm[:, h % 4, b * P:(b + 1) * P], ident[:])
                got.then_inc(pT_raw, 1)

            for i in range(HEADS + 4):
                if i < HEADS:
                    score_part(i)
                if 3 <= i < HEADS + 3:
                    turn_part(i - 3)
                if i >= 4:
                    h = i - 4
                    pe.wait_ge(pT_ready, h + 1)
                    v_part(1, h, lambda t, h: v2[:, t, h, :], pt[:, h % 4, 0:S], pt[:, h % 4, S:384])
            projection("mlo", xTh, xTl, KD, lambda k: pe.wait_ge(oT_ready, 8 + k + 1))
            transpose_x(4)
            pe.wait_ge(wr_ready, 2)
            for k in range(KD):
                pe.wait_ge(xT_ready, 16 + k // 2 + 1)
                got = three(ps[0:NE, 0, 0:S], both(wrh, wrl, ALL, k), both(xTh, xTl, ALL, k), k == 0, k == KD - 1)
            got.then_inc(logitsT_ready, 1)
            keep_warm(3, 2)
            pe.wait_ge(logitsT_out, 1)
            for t in range(T):
                got = pe.transpose(ps[:, 1, t * NE:(t + 1) * NE], lgT[0:NE, t * P:(t + 1) * P], ident[0:NE, 0:NE])
            got.then_inc(logits_ready, 1)
            keep_warm(3, 10)
            pe.wait_ge(msk_ready, 1)
            both_tiles = msk[:].rearrange("p t e -> p (t e)")
            pe.matmul(ps[:, 0, 0:2 * NE], before[:], both_tiles, start=True, stop=False, skip_group_check=True)
            pe.matmul(ps[:, 0, NE:3 * NE], ones[:], both_tiles, start=False, stop=False, skip_group_check=True)
            pe.matmul(ps[:, 0, 2 * NE:3 * NE], ones[:], msk[:, 0, :], start=False, stop=True,
                      skip_group_check=True).then_inc(pos_ready, 1)

            def gather(half, fill, onehots, bank=7):
                if fill is not None:
                    pe.wait_ge(aux_read, fill)
                pe.wait_ge(onehot_ready, onehots)
                for kk in range(4):
                    k = 4 * half + kk
                    for t in range(T):
                        for n, part in enumerate((xsh, xsl)):
                            got = pe.matmul(ps[:, bank, kk * P:(kk + 1) * P], part[:, t, k * P:(k + 1) * P], onehot[:, t, :],
                                            start=t == 0 and n == 0, stop=t == T - 1 and n == 1, skip_group_check=True)
                got.then_inc(aux_filled, 1)

            def put_back(bank, t, half):
                for n, part in enumerate((ysbh, ysbl)):
                    got = pe.matmul(ps[:, bank, :], ST[:, t * P:(t + 1) * P], part[:, half * CH:(half + 1) * CH],
                                    start=n == 0, stop=n == 1, skip_group_check=True)
                return got

            def back(n, fill, ys):
                t, half = n // 2, n % 2
                pe.wait_ge(aux_read, fill)
                pe.wait_ge(ysb_ready, ys)
                put_back(7, t, half).then_inc(aux_filled, 1)

            keep_warm(3, 3)
            pe.wait_ge(rows_ready, T)
            gather(0, None, 1)
            gather(1, None, 1, 6)

            def item(j):
                pe.wait_ge(aux_read, 2 if isinstance(j, int) else j * FILLS - 2)
                done = [0]

                def item_split(kind):
                    n = NPRE + done[0]
                    done[0] += 1
                    pe.wait_ge(lo_ready, j * NI + (n + 1))
                    return halves(n, kind)

                def hidden(c, n):
                    for q in range(2):
                        wh, wl = item_split("gate")
                        for kk in range(4):
                            k = 4 * q + kk
                            got = three(ps[:, 2 * (c % 2) + n, :], both(xgh, xgl, ALL, k), both(wh, wl, ALL, kk), k == 0, k == 7)
                        got.then_inc(units_used, 1)

                def turn(c):
                    pe.wait_ge(eh_ready, j * NC + (c + 2))
                    pe.wait_ge(ehT_ready, j * NC + (c + 1))
                    for q in range(2):
                        for k in range(2):
                            i = 2 * q + k
                            got = pe.transpose(ps[:, 6, i * P:(i + 1) * P], hb[:, c % 2, 2 * P * q + k:2 * P * (q + 1):2], ident[:])
                    got.then_inc(ehT_raw, 1)

                def down(c):
                    pe.wait_ge(ehT_ready, j * NC + (c + 2))
                    for q in range(2):
                        wh, wl = item_split("down")
                        for k in range(2):
                            i = 2 * q + k
                            for half in range(2):
                                got = three(ps[:, 4 + half, :], both(hTh, hTl, ALL, c % 2, slice(i * P, (i + 1) * P)),
                                            both(wh, wl, ALL, k, slice(half * CH, (half + 1) * CH)),
                                            c == 0 and i == 0, c == NC - 1 and i == 3)
                        got.then_inc(units_used, 1)

                for c in range(NC):
                    pe.wait_ge(eh_ready, j * NC + max(c, 1))
                    hidden(c, 0)
                    if c:
                        turn(c - 1)
                    if c < 2 and not isinstance(j, int):
                        back(2 * c, j * FILLS + (2 * c - 2), j)
                    if c == 2:
                        pe.wait_ge(aux_read, j * FILLS + 2)
                        for t in range(T):
                            got = pe.transpose(ps[:, 7, t * P:(t + 1) * P], onehot[:, t, :].bitcast(F32), ident[:])
                        got.then_inc(aux_filled, 1)
                    if c == NC - 1:
                        gather(0, j * FILLS + 3, j + 2)
                    hidden(c, 1)
                    if c < 2 and not isinstance(j, int):
                        back(2 * c + 1, j * FILLS + (2 * c - 1), j)
                    if c:
                        down(c - 1)
                turn(NC - 1)
                gather(1, j * FILLS + 4, j + 2)
                down(NC - 1)

            item(0)
            pe.wait_ge(route_ready, 1)
            items = pe.value_load(tab[0:1, 0:1], min_val=NE, max_val=ITEMS)
            with pe.Fori(1, items) as j:
                item(j)
            for n in range(2 * T):
                half, t = divmod(n, T)
                pe.wait_ge(ysb_ready, items + half)
                put_back(n, t, half).then_inc(result_back, 1)


def rope_table():
    import numpy as np

    freq = np.float32(10000.0) ** (-np.arange(0, ROPE, 2, dtype=np.float32) / np.float32(ROPE))
    ang = np.arange(S, dtype=np.float32)[:, None] * freq[None, :]
    cos, sin = np.cos(ang), np.sin(ang)
    return np.stack([np.concatenate([cos, cos], 1), np.concatenate([-sin, sin], 1)], 1).astype(np.float32)


def kernel(**inputs):
    import numpy as np
    import concourse.bacc as bacc
    from concourse.bass_utils import run_bass_kernel_spmd

    f = {k: np.ascontiguousarray(v) for k, v in inputs.items()}
    rest = np.ones((1, ROPE + 32), np.float32)
    gains = np.concatenate([
        f["g_mix"][0].reshape(KD, P), f["g_ffn"][0].reshape(KD, P), f["kv_g_src"].reshape(KD, P),
        f["g_mix"][1].reshape(KD, P), f["g_ffn"][1].reshape(KD, P), f["kv_g_a"].reshape(2, P),
        f["mla_g_q_a"].reshape(3, P), np.concatenate([f["kv_g_k_nope"].reshape(1, HD), rest], 1),
        np.concatenate([f["mla_g_q_nope"].reshape(1, HD), rest], 1)]).T
    gpe = np.broadcast_to(np.stack([f["kv_g_k_pe"], f["mla_g_q_pe"][0]])[None], (P, 2, ROPE))
    arrays = {
        "x": f["x"][0], "gains": gains, "gpe": gpe, "rope": rope_table(), "g_ffn1": f["g_ffn"][1],
        "w_router": f["moe_w_router"][0], "b_router": f["moe_b_router"][0],
        "w_qkv": f["sb_w_qkv"][0], "w_sbo": f["sb_w_o"][0], "w_gate": f["ffn_w_gate"][0], "w_up": f["ffn_w_up"][0],
        "w_down": f["ffn_w_down"][0], "w_kva": f["kv_w_a"], "w_kvb": f["kv_w_b"], "w_qa": f["mla_w_q_a"][0],
        "w_qb": f["mla_w_q_b"][0], "w_mlo": f["mla_w_o"][0],
        "e_gate": f["moe_w_gate"][0], "e_up": f["moe_w_up"][0], "e_down": f["moe_w_down"][0],
    }
    arrays = {k: np.ascontiguousarray(v) for k, v in arrays.items()}
    nc = bacc.Bacc("TRN2", target_bir_lowering=False, num_devices=1)
    d = {k: nc.dram_tensor(k, a.shape, F32, kind="ExternalInput").ap() for k, a in arrays.items()}
    out = nc.dram_tensor("out", (S, D), F32, kind="ExternalOutput").ap()
    build(nc, d["x"], d["gains"], d["gpe"], d["rope"], d["g_ffn1"], d["w_router"], d["b_router"],
          {k[2:]: d[k] for k in d if k.startswith("w_") and k != "w_router"}, d["e_gate"], d["e_up"], d["e_down"], out)
    r = run_bass_kernel_spmd(nc, [arrays], core_ids=[0])
    return r.results[0]["out"].reshape(1, S, D)
```
